# Optimizing a Trainium2 kernel written in Bass

```python
import jax, jax.numpy as jnp
from jax import lax
import numpy as np

D_MODEL = 1024
BATCH = 1
SEQ = 1024
DEPTH = 1

SSD_EXPAND = 2
SSD_D_INNER = SSD_EXPAND * D_MODEL
SSD_HEAD_DIM = 64
SSD_N_HEADS = SSD_D_INNER // SSD_HEAD_DIM
SSD_N_GROUPS = 4
SSD_HEADS_PER_GROUP = SSD_N_HEADS // SSD_N_GROUPS
SSD_D_STATE = 128
SSD_CONV_WIDTH = 4
SSD_CHUNK = 128
SSD_CONV_DIM = SSD_D_INNER + 2 * SSD_N_GROUPS * SSD_D_STATE

ATTN_HEAD_DIM = 64
ATTN_N_HEADS = D_MODEL // ATTN_HEAD_DIM
ATTN_N_KV_HEADS = 4
ATTN_REP = ATTN_N_HEADS // ATTN_N_KV_HEADS
ATTN_WINDOW = 128
ATTN_WIDTH = ATTN_N_HEADS * ATTN_HEAD_DIM
KV_WIDTH = ATTN_N_KV_HEADS * ATTN_HEAD_DIM
ROPE_THETA = 10000.0

FFN_D_FF = 2816
FFN_CONV_WIDTH = 3

NORM_EPS = 1e-6

IN_SIZES = (SSD_D_INNER, SSD_CONV_DIM, SSD_N_HEADS, ATTN_WIDTH, KV_WIDTH, KV_WIDTH, D_MODEL, D_MODEL)
IN_PROJ_DIM = sum(IN_SIZES)

kernel_name = "hybrid_ssd_swa_sink_gated_convffn"

def _split(t, sizes):
    idx = np.cumsum(np.array(sizes))[:-1].tolist()
    return jnp.split(t, idx, axis=-1)

def rms_norm(x, w):
    xf = x.astype(jnp.float32)
    y = xf * lax.rsqrt(jnp.mean(xf * xf, axis=-1, keepdims=True) + NORM_EPS)
    return (y * w.astype(jnp.float32)).astype(x.dtype)

def gated_group_rms_norm(y, z, w):
    b, s, d = y.shape
    g = (y.astype(jnp.float32) * jax.nn.silu(z.astype(jnp.float32))).reshape(b, s, SSD_N_GROUPS, d // SSD_N_GROUPS)
    g = g * lax.rsqrt(jnp.mean(g * g, axis=-1, keepdims=True) + NORM_EPS)
    return (g.reshape(b, s, d) * w.astype(jnp.float32)).astype(y.dtype)

def causal_dwconv(x, w, bias):
    k = w.shape[0]
    y = lax.conv_general_dilated(x, w[:, None, :].astype(x.dtype), window_strides=(1,), padding=((k - 1, 0),),
                                 dimension_numbers=('NWC', 'WIO', 'NWC'), feature_group_count=x.shape[-1])
    return y + bias.astype(x.dtype)

def rope_tables(positions):
    half = ATTN_HEAD_DIM // 2
    inv_freq = ROPE_THETA ** (-jnp.arange(half, dtype=jnp.float32) * 2.0 / ATTN_HEAD_DIM)
    ang = positions.astype(jnp.float32)[..., None] * inv_freq
    return jnp.cos(ang), jnp.sin(ang)

def apply_rope(t, cos, sin):
    b, s = t.shape[:2]
    half = t.shape[-1] // 2
    shp = (b, s) + (1,) * (t.ndim - 3) + (half,)
    c, sn = cos.reshape(shp), sin.reshape(shp)
    tf = t.astype(jnp.float32)
    t1, t2 = tf[..., :half], tf[..., half:]
    return jnp.concatenate([t1 * c - t2 * sn, t2 * c + t1 * sn], axis=-1).astype(t.dtype)

def ssd_chunked(xh, dt, a, bm, cm):
    b, s, g, j, p = xh.shape
    n = bm.shape[-1]
    c = s // SSD_CHUNK
    xf = xh.astype(jnp.float32)
    X = (xf * dt[..., None]).reshape(b, c, SSD_CHUNK, g, j, p)
    adt = (dt * a).reshape(b, c, SSD_CHUNK, g, j).transpose(0, 3, 4, 1, 2)
    a_cs = jnp.cumsum(adt, axis=-1)
    Bc = bm.astype(jnp.float32).reshape(b, c, SSD_CHUNK, g, n)
    Cc = cm.astype(jnp.float32).reshape(b, c, SSD_CHUNK, g, n)
    causal = jnp.tril(jnp.ones((SSD_CHUNK, SSD_CHUNK), dtype=bool))
    seg = a_cs[..., :, None] - a_cs[..., None, :]
    lmat = jnp.exp(jnp.where(causal, seg, -jnp.inf))
    cb = jnp.einsum('bclgn,bcsgn->bcgls', Cc, Bc)
    y_diag = jnp.einsum('bcgls,bgjcls,bcsgjp->bclgjp', cb, lmat, X)
    decay_states = jnp.exp(a_cs[..., -1:] - a_cs)
    states = jnp.einsum('bclgn,bgjcl,bclgjp->bcgjpn', Bc, decay_states, X)
    chunk_decay = jnp.exp(a_cs[..., -1])

    def step(h, inp):
        st, dc = inp
        return h * dc[..., None, None] + st, h

    h0 = jnp.zeros((b, g, j, p, n), jnp.float32)
    _, prev = lax.scan(step, h0, (jnp.moveaxis(states, 1, 0), jnp.moveaxis(chunk_decay, -1, 0)))
    prev = jnp.moveaxis(prev, 0, 1)
    y_off = jnp.einsum('bclgn,bcgjpn,bgjcl->bclgjp', Cc, prev, jnp.exp(a_cs))
    return (y_diag + y_off).reshape(b, s, g, j, p)

def sliding_window_sink_attention(q, k, v, sinks):
    b, s, g, r, d = q.shape
    w = ATTN_WINDOW
    nb = s // w
    qb = q.reshape(b, nb, w, g, r, d) * (d ** -0.5)
    kb = k.reshape(b, nb, w, g, d)
    vb = v.reshape(b, nb, w, g, d)
    kk = jnp.concatenate([jnp.concatenate([jnp.zeros_like(kb[:, :1]), kb[:, :-1]], axis=1), kb], axis=2)
    vv = jnp.concatenate([jnp.concatenate([jnp.zeros_like(vb[:, :1]), vb[:, :-1]], axis=1), vb], axis=2)
    scores = jnp.einsum('bnqgrd,bnkgd->bgrnqk', qb, kk, preferred_element_type=jnp.float32)
    qpos = jnp.arange(w)[:, None] + w
    kpos = jnp.arange(2 * w)[None, :]
    diff = qpos - kpos
    band = (diff >= 0) & (diff < w)
    valid = band[None] & ((jnp.arange(nb)[:, None, None] > 0) | (kpos[None] >= w))
    scores = jnp.where(valid, scores, -jnp.inf)
    sink = sinks.astype(jnp.float32).reshape(g, r)[None, :, :, None, None, None]
    m = jnp.maximum(jnp.max(scores, axis=-1, keepdims=True), sink)
    pexp = jnp.exp(scores - m)
    probs = pexp / (jnp.sum(pexp, axis=-1, keepdims=True) + jnp.exp(sink - m))
    out = jnp.einsum('bgrnqk,bnkgd->bnqgrd', probs.astype(v.dtype), vv)
    return out.reshape(b, s, g * r * d)

def hybrid_layer(x, cos, sin, norm_mix_pre_w, w_in, ssd_conv_w, ssd_conv_b, ssd_dt_bias, ssd_a_log, ssd_d,
                 ssd_norm_w, ssd_w_out, attn_sinks, attn_w_out, w_mix_out, norm_mix_post_w,
                 norm_ffn_pre_w, ffn_w_up, ffn_conv_w, ffn_conv_b, ffn_w_down, norm_ffn_post_w):
    b, s, _ = x.shape
    u = rms_norm(x, norm_mix_pre_w)
    proj = u @ w_in
    z, xbc, dt_raw, q, k, v, gate_ssd, gate_attn = _split(proj, IN_SIZES)

    xbc = jax.nn.silu(causal_dwconv(xbc, ssd_conv_w, ssd_conv_b))
    xs, bm, cm = _split(xbc, (SSD_D_INNER, SSD_N_GROUPS * SSD_D_STATE, SSD_N_GROUPS * SSD_D_STATE))
    xh = xs.reshape(b, s, SSD_N_GROUPS, SSD_HEADS_PER_GROUP, SSD_HEAD_DIM)
    bm = bm.reshape(b, s, SSD_N_GROUPS, SSD_D_STATE)
    cm = cm.reshape(b, s, SSD_N_GROUPS, SSD_D_STATE)
    dt = jax.nn.softplus(dt_raw.astype(jnp.float32) + ssd_dt_bias.astype(jnp.float32)).reshape(b, s, SSD_N_GROUPS, SSD_HEADS_PER_GROUP)
    a = -jnp.exp(ssd_a_log.astype(jnp.float32)).reshape(SSD_N_GROUPS, SSD_HEADS_PER_GROUP)
    y = ssd_chunked(xh, dt, a, bm, cm)
    y = y + ssd_d.astype(jnp.float32).reshape(SSD_N_GROUPS, SSD_HEADS_PER_GROUP)[..., None] * xh.astype(jnp.float32)
    y = gated_group_rms_norm(y.reshape(b, s, SSD_D_INNER).astype(x.dtype), z, ssd_norm_w)
    y_ssd = y @ ssd_w_out

    q = apply_rope(q.reshape(b, s, ATTN_N_KV_HEADS, ATTN_REP, ATTN_HEAD_DIM), cos, sin)
    k = apply_rope(k.reshape(b, s, ATTN_N_KV_HEADS, ATTN_HEAD_DIM), cos, sin)
    v = v.reshape(b, s, ATTN_N_KV_HEADS, ATTN_HEAD_DIM)
    y_attn = sliding_window_sink_attention(q, k, v, attn_sinks) @ attn_w_out

    merged = jax.nn.sigmoid(gate_ssd) * y_ssd + jax.nn.sigmoid(gate_attn) * y_attn
    x = x + rms_norm(merged @ w_mix_out, norm_mix_post_w)

    h = rms_norm(x, norm_ffn_pre_w)
    up = causal_dwconv(h @ ffn_w_up, ffn_conv_w, ffn_conv_b)
    gate, val = _split(up, (FFN_D_FF, FFN_D_FF))
    ff = (jax.nn.gelu(gate, approximate=True) * val) @ ffn_w_down
    return x + rms_norm(ff, norm_ffn_post_w)

def setup_inputs(seed: int = 0) -> dict:
    key = jax.random.key(seed)
    ks = jax.random.split(key, 24)
    L = DEPTH
    f32 = jnp.float32

    def nrm(k, shape, scale):
        return jax.random.normal(k, shape, f32) * scale

    def gain(k, d):
        return 1.0 + 0.02 * jax.random.normal(k, (L, d), f32)

    x = jax.random.normal(ks[0], (BATCH, SEQ, D_MODEL), f32)
    start = jax.random.randint(ks[1], (BATCH,), 0, 4096, dtype=jnp.int32)
    positions = (start[:, None] + jnp.arange(SEQ, dtype=jnp.int32)[None, :]).astype(jnp.int32)
    u = jax.random.uniform(ks[2], (L, SSD_N_HEADS), f32)
    dt0 = jnp.exp(u * (np.log(0.1) - np.log(0.001)) + np.log(0.001)).astype(f32)
    ssd_dt_bias = dt0 + jnp.log(-jnp.expm1(-dt0))
    ssd_a_log = jnp.log(jax.random.uniform(ks[3], (L, SSD_N_HEADS), f32, minval=1.0, maxval=16.0))
    return {
        "x": x,
        "positions": positions,
        "norm_mix_pre_w": gain(ks[4], D_MODEL),
        "w_in": nrm(ks[5], (L, D_MODEL, IN_PROJ_DIM), D_MODEL ** -0.5),
        "ssd_conv_w": nrm(ks[6], (L, SSD_CONV_WIDTH, SSD_CONV_DIM), SSD_CONV_WIDTH ** -0.5),
        "ssd_conv_b": nrm(ks[7], (L, SSD_CONV_DIM), 0.02),
        "ssd_dt_bias": ssd_dt_bias,
        "ssd_a_log": ssd_a_log,
        "ssd_d": 1.0 + 0.1 * jax.random.normal(ks[8], (L, SSD_N_HEADS), f32),
        "ssd_norm_w": gain(ks[9], SSD_D_INNER),
        "ssd_w_out": nrm(ks[10], (L, SSD_D_INNER, D_MODEL), SSD_D_INNER ** -0.5),
        "attn_sinks": nrm(ks[11], (L, ATTN_N_HEADS), 1.0),
        "attn_w_out": nrm(ks[12], (L, ATTN_WIDTH, D_MODEL), ATTN_WIDTH ** -0.5),
        "w_mix_out": nrm(ks[13], (L, D_MODEL, D_MODEL), D_MODEL ** -0.5),
        "norm_mix_post_w": gain(ks[14], D_MODEL),
        "norm_ffn_pre_w": gain(ks[15], D_MODEL),
        "ffn_w_up": nrm(ks[16], (L, D_MODEL, 2 * FFN_D_FF), D_MODEL ** -0.5),
        "ffn_conv_w": nrm(ks[17], (L, FFN_CONV_WIDTH, 2 * FFN_D_FF), FFN_CONV_WIDTH ** -0.5),
        "ffn_conv_b": nrm(ks[18], (L, 2 * FFN_D_FF), 0.02),
        "ffn_w_down": nrm(ks[19], (L, FFN_D_FF, D_MODEL), FFN_D_FF ** -0.5),
        "norm_ffn_post_w": gain(ks[20], D_MODEL),
    }

def reference(x, positions, norm_mix_pre_w, w_in, ssd_conv_w, ssd_conv_b, ssd_dt_bias, ssd_a_log, ssd_d,
              ssd_norm_w, ssd_w_out, attn_sinks, attn_w_out, w_mix_out, norm_mix_post_w,
              norm_ffn_pre_w, ffn_w_up, ffn_conv_w, ffn_conv_b, ffn_w_down, norm_ffn_post_w):
    cos, sin = rope_tables(positions)
    for i in range(DEPTH):
        x = hybrid_layer(x, cos, sin, norm_mix_pre_w[i], w_in[i], ssd_conv_w[i], ssd_conv_b[i], ssd_dt_bias[i],
                         ssd_a_log[i], ssd_d[i], ssd_norm_w[i], ssd_w_out[i], attn_sinks[i], attn_w_out[i],
                         w_mix_out[i], norm_mix_post_w[i], norm_ffn_pre_w[i], ffn_w_up[i], ffn_conv_w[i],
                         ffn_conv_b[i], ffn_w_down[i], norm_ffn_post_w[i])
    return x


_drawn_inputs = setup_inputs


def setup_inputs(seed=0):
    import zlib

    import numpy as np

    out = dict(_drawn_inputs(seed))
    spreads = {}
    factors = {'ssd_norm_w': 3.475,
     'attn_sinks': 5.642,
     'norm_mix_post_w': 3.499,
     'norm_ffn_pre_w': 3.431,
     'ffn_conv_b': 3.442,
     'norm_ffn_post_w': 5.119}
    for name, (base, spread) in spreads.items():
        noise = np.random.default_rng([zlib.crc32(name.encode()), seed]).standard_normal(out[name].shape)
        drawn = base * np.exp(spread * noise) if base else spread * noise
        out[name] = __import__('jax').numpy.asarray(drawn.astype(out[name].dtype))
    for name, factor in factors.items():
        out[name] = (out[name] * factor).astype(out[name].dtype)
    return out
```

```python
from contextlib import ExitStack

import concourse.bass as bass
from concourse import mybir

P = 128
SEQ = 1024
D = 1024
KT = D // P
NT = SEQ // P
HALF = 512
INNER = 2048
NH = 32
NG = 4
HPG = NH // NG
HD = 64
GW = HPG * HD
CONV_DIM = INNER + 2 * NG * P
XT = CONV_DIM // P
AH = 16
REP = AH // NG
ROWS = NH + D + 2 * NG * HD
RC = 4
RW = ROWS // RC
Q0 = NH
K0 = Q0 + D
V0 = K0 + NG * HD
FF = 2816
FT = FF // P
EPS = 1e-6
NEG = -1.0e30
MAGIC = 1.5 * 2.0 ** 23
FAR = 4096.0

F32 = mybir.dt.float32
F32R = mybir.dt.float32r
I32 = mybir.dt.int32
ALU = mybir.AluOpType
ACT = mybir.ActivationFunctionType
AX = mybir.AxisListType.X


def turn_parts(count):
    digits = 314159265358979323846264338327950288419716939937510582097494459230781640628620899
    rest = 2 * digits * 2 ** 400 // 10 ** (len(str(digits)) - 1)
    parts = []
    for _ in range(count):
        shift = rest.bit_length() - 7
        top = rest >> shift
        parts.append(float(top) * 2.0 ** (shift - 400))
        rest -= top << shift
    return parts


TURN = turn_parts(9)


def hybrid_block_kernel(nc, A, out):
    def scratch(name, shape):
        return nc.dram_tensor(name, shape, F32, kind="Internal").ap()

    rows_s = scratch("rows_s", (NT, P, ROWS))
    acs_s = scratch("acs_s", (NT * NH, P))
    feat_s = scratch("feat_s", (2 * NG, P, SEQ))
    tok_s = scratch("tok_s", (NT, P, CONV_DIM))
    gate_s = scratch("gate_s", (2 * KT, P, SEQ))
    o_s = scratch("o_s", (KT, P, SEQ))
    y_s = scratch("y_s", (2 * KT, P, SEQ))
    merged_s = scratch("merged_s", (KT, P, SEQ))
    x2_s = scratch("x2_s", (NT, P, D))
    ff_s = scratch("ff_s", (FT, P, SEQ))

    with ExitStack() as whole:
        def hold(ctx, name, shape, dt=F32):
            return ctx.enter_context(nc.sbuf_tensor(name, shape, dt))

        ident = hold(whole, "ident", [P, P])
        consts_done = whole.enter_context(nc.semaphore("consts_done"))

        with ExitStack() as early:
            utri = hold(early, "utri", [P, P])
            band = hold(early, "band", [P, 3, P])
            ones = hold(early, "ones", [P, P])
            u_hi = hold(early, "u_hi", [P, KT, SEQ], F32R)
            u_lo = hold(early, "u_lo", [P, KT, SEQ], F32R)
            dt_v = hold(early, "dt_v", [P, NT, NH])
            acs = hold(early, "acs", [P, NT, NH])
            ea = hold(early, "ea", [P, NT, NH])
            decay = hold(early, "decay", [P, NT, NH])
            cdecay = hold(early, "cdecay", [P, NT, NH])
            cos_t = hold(early, "cos_t", [P, NT, HD // 2])
            sin_t = hold(early, "sin_t", [P, NT, HD // 2])
            projection_rows(nc, A, rows_s, ident, utri, band, ones, consts_done, u_hi, u_lo)
            tables(nc, A, rows_s, acs_s, ident, utri, ones, dt_v, acs, ea, decay, cdecay, cos_t, sin_t)
            conv_features(nc, A, feat_s, tok_s, ident, u_hi, u_lo)
            mixers(nc, A, rows_s, acs_s, feat_s, tok_s, gate_s, o_s, y_s, ident, utri, band, u_hi, u_lo,
                   dt_v, acs, ea, decay, cdecay, cos_t, sin_t)
        with ExitStack() as late:
            part = hold(late, "part", [P, KT, SEQ])
            merge(nc, A, gate_s, o_s, merged_s, part, False)
            merge(nc, A, gate_s, y_s, merged_s, part, True)
        with ExitStack() as late:
            h_hi = hold(late, "h_hi", [P, KT, SEQ], F32R)
            h_lo = hold(late, "h_lo", [P, KT, SEQ], F32R)
            mix_rows(nc, A, merged_s, x2_s, h_hi, h_lo, ident)
            ffn_up(nc, A, ff_s, h_hi, h_lo)
        ffn_down(nc, A, ff_s, x2_s, out, ident)


class Stage:

    def __init__(self, nc, tag):
        self.nc, self.tag, self.ctx, self.used = nc, tag, ExitStack(), []

    def __enter__(self):
        self.ctx.__enter__()
        return self

    def __exit__(self, *a):
        self.ctx.__exit__(*a)
        self.nc.clear_and_free_semaphores(self.used)
        self.nc.all_engine_barrier()

    def sb(self, name, shape, dt=F32):
        return self.ctx.enter_context(self.nc.sbuf_tensor(f"{self.tag}_{name}", shape, dt))

    def ps(self, name, shape):
        return self.ctx.enter_context(self.nc.psum_tensor(f"{self.tag}_{name}", shape, F32))

    def sem(self, name):
        self.used.append(self.nc.alloc_semaphore(name=f"{self.tag}_{name}"))
        return self.used[-1]

    def sems(self, name, n):
        return [self.sem(f"{name}{i}") for i in range(n)]

    def block(self):
        return self.ctx.enter_context(self.nc.Block())


class Chain:

    def __init__(self, eng, sem, base=0):
        self.eng, self.sem, self.n, self.base = eng, sem, 0, base

    def did(self, ins):
        ins.then_inc(self.sem, 1)
        self.n += 1
        return self.n

    def wait(self, n=None):
        self.eng.wait_ge(self.sem, self.base + (self.n if n is None else n))


def matmul3(pe, dst, s_hi, s_lo, m_hi, m_lo, first, last):
    pe.matmul(dst, s_hi, m_hi, start=first, stop=False)
    pe.matmul(dst, s_hi, m_lo, start=False, stop=False)
    return pe.matmul(dst, s_lo, m_hi, start=False, stop=last)


def bcast(ap, n):
    return ap.unsqueeze(2).to_broadcast([ap.shape[0], ap.shape[1], n])


def projection_rows(nc, A, rows_s, ident, utri, band, ones, consts_done, u_hi, u_lo):
    with Stage(nc, "pr") as s:
        x_t = s.sb("x_t", [P, 2, D])
        sq = s.sb("sq", [P, D])
        w_row = s.sb("w_row", [P, D])
        stat = s.sb("stat", [P, NT, 6])
        w_raw = s.sb("w_raw", [P, 2, KT // 2, RW])
        w_hi = s.sb("w_hi", [P, RC, KT, RW], F32R)
        w_lo = s.sb("w_lo", [P, RC, KT, RW], F32R)
        o_t = s.sb("o_t", [P, RC, RW])
        ps_t = s.ps("ps_t", [P, KT, P])
        ps_o = s.ps("ps_o", [P, RC, HALF])
        x_in = s.sems("x_in", 2)
        row_in, sq_done, v_ready, r0_ready, xn_ready = (s.sem(n) for n in "row_in sq_done v_ready r0_ready xn_ready".split())
        act_own, dve_own = s.sem("act_own"), s.sem("dve_own")
        w_in = s.sems("w_in", 2)
        w_hi_done, w_lo_done, t_done, u_hi_done, u_lo_done = (s.sem(n) for n in "w_hi_done w_lo_done t_done u_hi_done u_lo_done".split())
        rows_done, rows_out = s.sem("rows_done"), s.sem("rows_out")
        stored = s.sems("stored", RC)
        block = s.block()
        x_tiles = A["x"].rearrange("(t p) d -> t p d", p=P)

        @block.sync
        def _(sp):
            for t in range(2):
                sp.dma_start(x_t[:, t], x_tiles[t]).then_inc(x_in[t], 16)
            sp.dma_start(w_row[:], A["mix_pre_row"].partition_broadcast(P)).then_inc(row_in, 16)
            for h in range(2 * RC):
                if h >= 2:
                    sp.wait_ge(w_lo_done, h - 1)
                sp.dma_start(w_raw[:, h % 2], A["w_rows"][h // 2, :, (h % 2) * 4:(h % 2) * 4 + 4]).then_inc(w_in[h % 2], 16)
            for t in range(2, NT):
                sp.wait_ge(t_done, t - 1)
                sp.dma_start(x_t[:, t % 2], x_tiles[t]).then_inc(x_in[t % 2], 16)

        @block.gpsimd
        def _(pool):
            pool.memset(ident[:], 0.0).then_inc(consts_done, 1)
            pool.memset(utri[:], 1.0).then_inc(consts_done, 1)
            pool.memset(band[:], 0.0).then_inc(consts_done, 1)
            pool.memset(ones[:], 1.0).then_inc(consts_done, 1)
            pool.wait_ge(consts_done, 4)
            pool.affine_select(out=ident[:], in_=ident[:], compare_op=ALU.not_equal, fill=1.0, base=0,
                               pattern=[[-1, P]], channel_multiplier=1).then_inc(consts_done, 1)
            pool.affine_select(out=utri[:], in_=utri[:], compare_op=ALU.is_ge, fill=0.0, base=0,
                               pattern=[[1, P]], channel_multiplier=-1).then_inc(consts_done, 1)
            for b, (sign, base) in enumerate([(1, -1), (-1, 0), (1, -1)]):
                pool.affine_select(out=band[:, b], in_=band[:, b], compare_op=ALU.is_ge, fill=NEG, base=base,
                                   pattern=[[sign, P]], channel_multiplier=-sign).then_inc(consts_done, 1)
            for t in range(NT):
                for c in range(RC):
                    pool.wait_ge(rows_out, t * RC + c + 1)
                    pool.dma_start(rows_s[t, :, c * RW:(c + 1) * RW], o_t[:, c]).then_inc(stored[c], 16)
            for c in range(RC):
                pool.wait_ge(stored[c], 16 * NT)

        @block.scalar
        def _(act):
            own = Chain(act, act_own)

            def square(t):
                act.wait_ge(x_in[t % 2], 16 * (t // 2 + 1))
                if t:
                    act.wait_ge(sq_done, t)
                act.activation(sq[:], x_t[:, t % 2], ACT.Square, accum_out=stat[:, t, 0:1]).then_inc(sq_done, 1)

            def root(t):
                act.wait_ge(v_ready, t + 1)
                own.did(act.activation(stat[:, t, 2:3], stat[:, t, 1:2], ACT.Ln))
                own.wait()
                act.activation(stat[:, t, 3:4], stat[:, t, 2:3], ACT.Exp, scale=-0.5).then_inc(r0_ready, 1)

            def split_w(h):
                act.wait_ge(w_in[h % 2], 16 * (h // 2 + 1))
                c, k = h // 2, (h % 2) * 4
                act.activation(w_hi[:, c, k:k + 4], w_raw[:, h % 2], ACT.Copy).then_inc(w_hi_done, 1)

            def split_u(t):
                act.wait_ge(t_done, t + 1)
                act.activation(u_hi[:, :, t * P:(t + 1) * P], ps_t[:], ACT.Copy).then_inc(u_hi_done, 1)

            square(0)
            split_w(0)
            root(0)
            split_w(1)
            square(1)
            split_u(0)
            split_w(2)
            root(1)
            for h in range(3, 8):
                split_w(h)
            split_u(1)
            for t in range(2, NT):
                square(t)
                root(t)
                split_u(t)

        @block.vector
        def _(dve):
            own = Chain(dve, dve_own)

            def norm(t):
                dve.wait_ge(sq_done, t + 1)
                dve.tensor_scalar(stat[:, t, 1:2], stat[:, t, 0:1], 1.0 / D, EPS, ALU.mult, ALU.add).then_inc(v_ready, 1)
                dve.wait_ge(r0_ready, t + 1)
                newton(dve, own, stat[:, t, 3:4], stat[:, t, 1:2], stat[:, t, 4:5], stat[:, t, 5:6])
                if t == 0:
                    dve.wait_ge(row_in, 16)
                dve.scalar_tensor_tensor(x_t[:, t % 2], x_t[:, t % 2], stat[:, t, 5:6], w_row[:], ALU.mult,
                                         ALU.mult).then_inc(xn_ready, 1)

            def split_w(h):
                dve.wait_ge(w_hi_done, h + 1)
                c, k = h // 2, (h % 2) * 4
                dve.tensor_tensor(w_lo[:, c, k:k + 4], w_raw[:, h % 2], w_hi[:, c, k:k + 4].bitcast(F32),
                                  ALU.subtract).then_inc(w_lo_done, 1)

            def split_u(t):
                dve.wait_ge(u_hi_done, t + 1)
                dve.tensor_tensor(u_lo[:, :, t * P:(t + 1) * P], ps_t[:], u_hi[:, :, t * P:(t + 1) * P].bitcast(F32),
                                  ALU.subtract).then_inc(u_lo_done, 1)

            def rows(t):
                for c in range(RC):
                    dve.wait_ge(rows_done, t * RC + c + 1)
                    if t:
                        dve.wait_ge(stored[c], 16 * t)
                    dve.tensor_copy(o_t[:, c], ps_o[:, c, 0:RW]).then_inc(rows_out, 1)

            norm(0)
            split_w(0)
            split_u(0)
            split_w(1)
            split_w(2)
            norm(1)
            for h in range(3, 8):
                split_w(h)
            split_u(1)
            for t in range(NT):
                if t + 2 < NT:
                    norm(t + 2)
                rows(t)
                if t + 2 < NT:
                    split_u(t + 2)

        @block.tensor
        def _(pe):
            pe.wait_ge(consts_done, 5)

            def turn(t):
                pe.wait_ge(xn_ready, t + 1)
                if t:
                    pe.wait_ge(u_lo_done, t)
                for k in range(KT):
                    last = pe.transpose(ps_t[:, k], x_t[:, t % 2, k * P:(k + 1) * P], ident[:])
                last.then_inc(t_done, 1)

            turn(0)
            for t in range(NT):
                if t == 0:
                    turn(1)
                elif t + 1 < NT:
                    turn(t + 1)
                pe.wait_ge(u_lo_done, t + 1)
                for c in range(RC):
                    if t:
                        pe.wait_ge(rows_out, (t - 1) * RC + c + 1)
                    for k in range(KT):
                        if t == 0 and k % 4 == 0:
                            pe.wait_ge(w_lo_done, 2 * c + k // 4 + 1)
                        last = matmul3(pe, ps_o[:, c, 0:RW], u_hi[:, k, t * P:(t + 1) * P], u_lo[:, k, t * P:(t + 1) * P],
                                       w_hi[:, c, k], w_lo[:, c, k], k == 0, k == KT - 1)
                    last.then_inc(rows_done, 1)


def newton(dve, own, r0, v, tmp, r):
    own.did(dve.tensor_scalar(tmp, r0, r0, v, ALU.mult, ALU.mult))
    own.wait()
    own.did(dve.tensor_scalar(tmp, tmp, -0.5, 1.5, ALU.mult, ALU.add))
    own.wait()
    own.did(dve.tensor_tensor(r, r0, tmp, ALU.mult))
    own.wait()


def tables(nc, A, rows_s, acs_s, ident, utri, ones, dt_v, acs, ea, decay, cdecay, cos_t, sin_t):
    W = NT * NH
    with Stage(nc, "tb") as s:
        raw = s.sb("raw", [P, NT, NH])
        bias = s.sb("bias", [P, NH])
        alog = s.sb("alog", [P, NH])
        a_neg = s.sb("a_neg", [P, NH])
        freq = s.sb("freq", [P, HD // 2])
        pos = s.sb("pos", [P, NT], I32)
        posf = s.sb("posf", [P, NT])
        adt = s.sb("adt", [P, NT, NH])
        t1 = s.sb("t1", [P, NT, NH])
        t2 = s.sb("t2", [P, NT, NH])
        t3 = s.sb("t3", [P, NT, NH])
        mx = s.sb("mx", [P, NT, NH])
        ang = s.sb("ang", [P, NT, HD // 2])
        k_t = s.sb("k_t", [P, NT, HD // 2])
        m_t = s.sb("m_t", [P, NT, HD // 2])
        half_pi = s.sb("half_pi", [P, 1])
        tot = s.sb("tot", [P, NT, NH])
        acs_f = s.sb("acs_f", [P, 2, P])
        ps_a = s.ps("ps_a", [P, W])
        ps_b = s.ps("ps_b", [P, W])
        ps_c = s.ps("ps_c", [P, 2, P])
        ins_in, raw_in = s.sem("ins_in"), s.sem("raw_in")
        u_need, u_ready, a_ready, adt_ready, sums_done = (s.sem(n) for n in "u_need u_ready a_ready adt_ready sums_done".split())
        dve_own, act_own, ang_ready, acs_ready, turned, flat = (s.sem(n) for n in "dve_own act_own ang_ready acs_ready turned flat".split())
        diff_ready, stored = s.sem("diff_ready"), s.sem("stored")
        block = s.block()

        @block.sync
        def _(sp):
            sp.dma_start(raw[:], rows_s.rearrange("t p n -> p t n")[:, :, 0:NH]).then_inc(raw_in, 16)
            sp.dma_start(bias[:], A["dt_bias_row"].partition_broadcast(P)).then_inc(ins_in, 16)
            sp.dma_start(alog[:], A["a_log_row"].partition_broadcast(P)).then_inc(ins_in, 16)
            sp.dma_start(freq[:], A["freq_row"].partition_broadcast(P)).then_inc(ins_in, 16)
            sp.dma_start(pos[:], A["pos"]).then_inc(ins_in, 16)
            sp.wait_ge(flat, 1)
            sp.dma_start(acs_s.rearrange("(a r) l -> r a l", r=P), acs_f[:]).then_inc(stored, 16)
            sp.wait_ge(stored, 16)

        @block.vector
        def _(dve):
            own = Chain(dve, dve_own)

            def do(ins):
                own.did(ins)
                own.wait()

            dve.wait_ge(raw_in, 16)
            dve.wait_ge(ins_in, 64)
            do(dve.tensor_tensor(t1[:], raw[:], bias[:].unsqueeze(1).to_broadcast([P, NT, NH]), ALU.add))
            do(dve.tensor_scalar(mx[:], t1[:], 0.0, None, ALU.max))
            dve.scalar_tensor_tensor(t2[:], mx[:], -2.0, t1[:], ALU.mult, ALU.add).then_inc(u_need, 1)
            dve.wait_ge(u_ready, 1)
            do(dve.tensor_scalar(t1[:], t3[:], 2.0, None, ALU.add))
            do(dve.reciprocal(t1[:], t1[:]))
            do(dve.tensor_tensor(t3[:], t3[:], t1[:], ALU.mult))
            do(dve.tensor_tensor(t1[:], t3[:], t3[:], ALU.mult))
            do(dve.tensor_scalar(t2[:], t1[:], 1.0 / 19, 1.0 / 17, ALU.mult, ALU.add))
            for n in (15, 13, 11, 9, 7, 5, 3, 1):
                do(dve.tensor_tensor(t2[:], t2[:], t1[:], ALU.mult))
                do(dve.tensor_scalar(t2[:], t2[:], 1.0 / n, None, ALU.add))
            do(dve.tensor_tensor(t2[:], t2[:], t3[:], ALU.mult))
            do(dve.scalar_tensor_tensor(dt_v[:], t2[:], 2.0, mx[:], ALU.mult, ALU.add))
            dve.wait_ge(a_ready, 1)
            dve.scalar_tensor_tensor(adt[:], dt_v[:], -1.0, a_neg[:].unsqueeze(1).to_broadcast([P, NT, NH]),
                                     ALU.mult, ALU.mult).then_inc(adt_ready, 1)
            do(dve.memset(half_pi[:], 1.5707963267948966))
            do(dve.tensor_copy(posf[:], pos[:]))
            do(dve.tensor_tensor(ang[:], posf[:].unsqueeze(2).to_broadcast([P, NT, HD // 2]),
                                 freq[:].unsqueeze(1).to_broadcast([P, NT, HD // 2]), ALU.mult))
            turn = sum(TURN)
            for scale in (FAR, 1.0):
                do(dve.tensor_scalar(k_t[:], ang[:], 1.0 / (turn * scale), MAGIC, ALU.mult, ALU.add))
                do(dve.tensor_scalar(k_t[:], k_t[:], MAGIC, None, ALU.subtract))
                for part in TURN:
                    do(dve.scalar_tensor_tensor(ang[:], k_t[:], -part * scale, ang[:], ALU.mult, ALU.add))
            do(dve.tensor_scalar(ang[:], ang[:], 3.1415925, -3.1415925, ALU.min, ALU.max))
            dve.tensor_scalar(m_t[:], ang[:], -1.0, None, ALU.mult).then_inc(dve_own, 1)
            own.n += 1
            own.wait()
            dve.tensor_tensor(m_t[:], m_t[:], ang[:], ALU.max).then_inc(ang_ready, 1)
            dve.wait_ge(sums_done, 1)
            dve.tensor_copy(acs[:].rearrange("p t h -> p (t h)"), ps_a[:]).then_inc(acs_ready, 1)
            do(dve.tensor_copy(tot[:].rearrange("p t h -> p (t h)"), ps_b[:]))
            dve.tensor_tensor(decay[:], tot[:], acs[:], ALU.subtract).then_inc(diff_ready, 1)
            dve.wait_ge(turned, 1)
            dve.tensor_copy(acs_f[:], ps_c[:]).then_inc(flat, 1)

        @block.scalar
        def _(act):
            act.wait_ge(ins_in, 64)
            act.activation(a_neg[:], alog[:], ACT.Exp).then_inc(a_ready, 1)
            act.wait_ge(u_need, 1)
            act.activation(t3[:], t2[:], ACT.Exp).then_inc(u_ready, 1)
            act.wait_ge(diff_ready, 1)
            act.activation(decay[:], decay[:], ACT.Exp)
            act.activation(ea[:], acs[:], ACT.Exp)
            act.activation(cdecay[:], tot[:], ACT.Exp).then_inc(act_own, 1)
            act.wait_ge(ang_ready, 1)
            act.activation(sin_t[:], ang[:], ACT.Sin)
            act.activation(cos_t[:], m_t[:], ACT.Sin, scale=-1.0, bias=half_pi[:]).then_inc(act_own, 1)
            act.wait_ge(act_own, 2)

        @block.tensor
        def _(pe):
            pe.wait_ge(adt_ready, 1)
            flat_adt = adt[:].rearrange("p t h -> p (t h)")
            pe.matmul(ps_a[:], utri[:], flat_adt, start=True, stop=True)
            pe.matmul(ps_b[:], ones[:], flat_adt, start=True, stop=True).then_inc(sums_done, 1)
            pe.wait_ge(acs_ready, 1)
            flat_acs = acs[:].rearrange("p t h -> p (t h)")
            for i in range(2):
                last = pe.transpose(ps_c[:, i], flat_acs[:, i * P:(i + 1) * P], ident[:])
            last.then_inc(turned, 1)


def conv_features(nc, A, feat_s, tok_s, ident, u_hi, u_lo):
    TAPS = 4
    with Stage(nc, "cf") as s:
        cw = s.sb("cw", [P, XT, TAPS + 1])
        w_raw = s.sb("w_raw", [P, 2, KT, P])
        w_hi = s.sb("w_hi", [P, 2, KT, P], F32R)
        w_lo = s.sb("w_lo", [P, 2, KT, P], F32R)
        xc = s.sb("xc", [P, 2, SEQ])
        xt = s.sb("xt", [P, 2, NT, P])
        ps = s.ps("ps", [P, 2, SEQ])
        ps_t = s.ps("ps_t", [P, NT, P])
        cw_in = s.sem("cw_in")
        w_in, f_stored, t_stored = s.sems("w_in", 2), s.sems("f_stored", 2), s.sems("t_stored", 2)
        hi_done, lo_done, product_done, tap_done, dve_own, conv_done, silu_done, turned, t_out = (
            s.sem(n) for n in "hi_done lo_done product_done tap_done dve_own conv_done silu_done turned t_out".split())
        block = s.block()
        n_pairs = XT // 2
        feature_pairs = (INNER // P) // 2

        @block.sync
        def _(sp):
            sp.dma_start(cw[:], A["ssd_conv"]).then_inc(cw_in, 16)
            for j in range(2):
                sp.dma_start(w_raw[:, j], A["w_xbc"][j]).then_inc(w_in[j], 16)
            with sp.Fori(0, n_pairs - 1) as i:
                for j in range(2):
                    sp.wait_ge(lo_done, 2 * i + j + 1)
                    sp.dma_start(w_raw[:, j], A["w_xbc"][2 * i + (j + 2)]).then_inc(w_in[j], 16)

        @block.gpsimd
        def _(pool):
            def store(i, j, features):
                f = 2 * i + j
                if features:
                    pool.wait_ge(silu_done, f + 1)
                    pool.dma_start(feat_s[f - INNER // P], xc[:, j]).then_inc(f_stored[j], 16)
                pool.wait_ge(t_out, f + 1)
                pool.dma_start(tok_s[:, :, bass.ds(f * P, P)].rearrange("t p n -> p t n"), xt[:, j]).then_inc(t_stored[j], 16)

            with pool.Fori(0, feature_pairs) as i:
                for j in range(2):
                    store(i, j, False)
            with pool.Fori(feature_pairs, n_pairs) as i:
                for j in range(2):
                    store(i, j, True)
            for j in range(2):
                pool.wait_ge(t_stored[j], 16 * n_pairs)
                pool.wait_ge(f_stored[j], 16 * (n_pairs - feature_pairs))

        @block.scalar
        def _(act):
            def split(i, j):
                f = 2 * i + j
                act.wait_ge(w_in[j], 16 * (i + 1))
                act.activation(w_hi[:, j], w_raw[:, j], ACT.Copy).then_inc(hi_done, 1)

            def tile(i, j, first, features, last):
                f = 2 * i + j
                act.wait_ge(product_done, f + 1)
                if not first:
                    act.wait_ge(turned, f - 1)
                    if features:
                        act.wait_ge(f_stored[j], 16 * (i - feature_pairs))
                act.activation(xc[:, j], ps[:, j], ACT.Identity, scale=cw[:, bass.ds(f, 1), TAPS - 1],
                               bias=cw[:, bass.ds(f, 1), TAPS]).then_inc(tap_done, 1)
                if not last:
                    split(i + 1, j)
                act.wait_ge(conv_done, f + 1)
                act.activation(xc[:, j], xc[:, j], ACT.Silu).then_inc(silu_done, 1)

            for j in range(2):
                split(0, j)
            act.wait_ge(cw_in, 16)
            for j in range(2):
                tile(0, j, True, False, False)
            with act.Fori(1, feature_pairs) as i:
                for j in range(2):
                    tile(i, j, False, False, False)
            with act.Fori(feature_pairs, n_pairs - 1) as i:
                for j in range(2):
                    tile(i, j, False, True, False)
            for j in range(2):
                tile(n_pairs - 1, j, False, True, True)

        @block.vector
        def _(dve):
            def split(i, j):
                f = 2 * i + j
                dve.wait_ge(hi_done, f + 1)
                dve.tensor_tensor(w_lo[:, j], w_raw[:, j], w_hi[:, j].bitcast(F32), ALU.subtract).then_inc(lo_done, 1)

            def conv(i, j, last):
                f = 2 * i + j
                dve.wait_ge(tap_done, f + 1)
                for n in range(1, TAPS):
                    if n > 1:
                        dve.wait_ge(dve_own, f * (TAPS - 2) + n - 1)
                    ins = dve.scalar_tensor_tensor(xc[:, j, n:SEQ], ps[:, j, 0:SEQ - n], cw[:, bass.ds(f, 1), TAPS - 1 - n],
                                                   xc[:, j, n:SEQ], ALU.mult, ALU.add)
                    ins.then_inc(dve_own if n < TAPS - 1 else conv_done, 1)
                if not last:
                    split(i + 1, j)

            def by_tokens(i, j, first):
                f = 2 * i + j
                dve.wait_ge(turned, f + 1)
                if not first:
                    dve.wait_ge(t_stored[j], 16 * i)
                dve.tensor_copy(xt[:, j], ps_t[:]).then_inc(t_out, 1)

            for j in range(2):
                split(0, j)
            dve.wait_ge(cw_in, 16)
            conv(0, 0, False)
            conv(0, 1, False)
            by_tokens(0, 0, True)
            with dve.Fori(1, n_pairs - 1) as i:
                conv(i, 0, False)
                by_tokens(i - 1, 1, False)
                conv(i, 1, False)
                by_tokens(i, 0, False)
            conv(n_pairs - 1, 0, True)
            by_tokens(n_pairs - 2, 1, False)
            conv(n_pairs - 1, 1, True)
            by_tokens(n_pairs - 1, 0, False)
            by_tokens(n_pairs - 1, 1, False)

        @block.tensor
        def _(pe):
            def half(i, j, h):
                for k in range(KT):
                    last = matmul3(pe, ps[:, j, h * HALF:(h + 1) * HALF], w_hi[:, j, k], w_lo[:, j, k],
                                   u_hi[:, k, h * HALF:(h + 1) * HALF], u_lo[:, k, h * HALF:(h + 1) * HALF], k == 0, k == KT - 1)
                return last

            def turn(f, j):
                pe.wait_ge(silu_done, f + 1)
                pe.wait_ge(t_out, f)
                for t in range(NT):
                    last = pe.transpose(ps_t[:, t], xc[:, j, t * P:(t + 1) * P], ident[:])
                last.then_inc(turned, 1)

            def tile(i, j, first):
                f = 2 * i + j
                pe.wait_ge(lo_done, f + 1)
                if not first:
                    pe.wait_ge(conv_done, f - 1)
                half(i, j, 0)
                if not (first and j == 0):
                    turn(f - 1, 1 - j)
                half(i, j, 1).then_inc(product_done, 1)

            for j in range(2):
                tile(0, j, True)
            with pe.Fori(1, n_pairs) as i:
                for j in range(2):
                    tile(i, j, False)
            turn(XT - 1, 1)


def mixers(nc, A, rows_s, acs_s, feat_s, tok_s, gate_s, o_s, y_s, ident, utri, band, u_hi, u_lo,
           dt_v, acs, ea, decay, cdecay, cos_t, sin_t):
    R2 = HD // 2
    with Stage(nc, "mx") as s:
        z_raw = s.sb("z_raw", [P, 2, 2, GW])
        z_hi = s.sb("z_hi", [P, KT, GW], F32R)
        z_lo = s.sb("z_lo", [P, KT, GW], F32R)
        g_raw = s.sb("g_raw", [P, 2, KT, P])
        g_hi = s.sb("g_hi", [P, 2, KT, P], F32R)
        g_lo = s.sb("g_lo", [P, 2, KT, P], F32R)
        g_out = s.sb("g_out", [P, 2, HALF])
        x_in = s.sb("x_in", [P, 2, GW])
        b_tok = s.sb("b_tok", [P, 2, P])
        bc_f = s.sb("bc_f", [P, 2, 2, P])
        a_row = s.sb("a_row", [P, 2, HPG, P])
        dt_g, acs_g, decay_g = (s.sb(n, [P, NT, HPG]) for n in ("dt_g", "acs_g", "decay_g"))
        d_g = s.sb("d_g", [P, HPG])
        seg = s.sb("seg", [P, HPG, P])
        cbm = s.sb("cbm", [P, P])
        xdt = s.sb("xdt", [P, GW])
        xdec = s.sb("xdec", [P, GW])
        xd = s.sb("xd", [P, GW])
        state = s.sb("state", [P, GW])
        kept = s.sb("kept", [P, GW])
        y1 = s.sb("y1", [P, GW])
        silu = s.sb("silu", [P, GW])
        yn = s.sb("yn", [P, GW])
        y_t = s.sb("y_t", [P, 2, 4, P])
        stat = s.sb("stat", [P, 6])
        norm_row = s.sb("norm_row", [P, GW])
        d_row = s.sb("d_row", [P, NH])
        qk = s.sb("qk", [P, 2, REP + 2, HD])
        v_in = s.sb("v_in", [P, 4, HD])
        m1 = s.sb("m1", [P, REP + 2, R2])
        m2 = s.sb("m2", [P, REP + 2, R2])
        qr = s.sb("qr", [P, REP + 2, HD])
        q_t = s.sb("q_t", [P, 2, P])
        k_t = s.sb("k_t", [P, 2, P])
        sc = s.sb("sc", [P, REP, 2 * P])
        mx = s.sb("mx", [P, 2, REP])
        negm = s.sb("negm", [P, REP])
        sums = s.sb("sums", [P, REP])
        sink_e = s.sb("sink_e", [P, REP])
        rden = s.sb("rden", [P, REP])
        sinks = s.sb("sinks", [P, AH])
        p_t = s.sb("p_t", [P, REP, 2, P])
        o_tok = s.sb("o_tok", [P, REP * HD])
        o_t = s.sb("o_t", [P, 2, 2, P])
        ps_z = s.ps("ps_z", [P, HALF])
        ps_g = s.ps("ps_g", [P, HALF])
        ps_a = s.ps("ps_a", [P, HALF])
        ps_s = s.ps("ps_s", [P, 2, 2, 2 * P])
        ps_d = s.ps("ps_d", [P, HALF])
        ps_e = s.ps("ps_e", [P, HALF])
        ps_f = s.ps("ps_f", [P, HALF])

        rows_in, norm_in, step_in, z_in, g_in = s.sem("rows_in"), s.sem("norm_in"), s.sems("step_in", 2), s.sems("z_in", 2), s.sems("g_in", 2)
        z_hi_done, z_lo_done, g_hi_done, g_lo_done = (s.sem(n) for n in "z_hi_done z_lo_done g_hi_done g_lo_done".split())
        z_done, z_exp_done, z_used, gate_done, gate_out = (s.sem(n) for n in "z_done z_exp_done z_used gate_done gate_out".split())
        g_stored, y_stored, o_stored = s.sems("g_stored", 2), s.sems("y_stored", 2), s.sems("o_stored", 2)
        seg_ready, seg_min, decays_done, mix_ready, cb_done, cbm_ready = (
            s.sem(n) for n in "seg_ready seg_min decays_done mix_ready cb_done cbm_ready".split())
        xdt_ready, xdec_ready, xd_ready, off_done, state_done, state_ready, diag_done, y2_ready, y1_ready = (
            s.sem(n) for n in "xdt_ready xdec_ready xd_ready off_done state_done state_ready diag_done y2_ready y1_ready".split())
        gated, sq_done, v_ready, r0_ready, yn_ready, y_turned, y_out = (
            s.sem(n) for n in "gated sq_done v_ready r0_ready yn_ready y_turned y_out".split())
        rotated, qk_turned, q_ready, scored, masked, max_ready, exp_done, sink_done, p_turned, p_ready, pv_done, o_ready, o_turned, o_out = (
            s.sem(n) for n in "rotated qk_turned q_ready scored masked max_ready exp_done sink_done p_turned p_ready pv_done o_ready o_turned o_out".split())
        dve_own, pool_own, act_own = s.sem("dve_own"), s.sem("pool_own"), s.sem("act_own")
        block = s.block()
        LOADS = 8

        @block.sync
        def _(sp):
            def load_step(g, c):
                j = c % 2
                for dst, src in (
                    (qk[:, j, 0:REP].rearrange("p a d -> p (a d)"), rows_s[c, :, bass.ds(Q0 + g * (REP * HD), REP * HD)]),
                    (qk[:, j, REP], rows_s[c, :, bass.ds(K0 + g * HD, HD)]),
                    (qk[:, j, REP + 1], rows_s[c, :, bass.ds(K0 + g * HD, HD)]),
                    (v_in[:, c % 4], rows_s[c, :, bass.ds(V0 + g * HD, HD)]),
                    (a_row[:, j].rearrange("p h l -> p (h l)"),
                     acs_s[bass.ds(c * NH + g * HPG, HPG), :].rearrange("h l -> (h l)").partition_broadcast(P)),
                    (x_in[:, j], tok_s[c, :, bass.ds(g * GW, GW)]),
                    (b_tok[:, j], tok_s[c, :, bass.ds(INNER + g * P, P)]),
                    (bc_f[:, j], feat_s.rearrange("(b g) p n -> g p b n", b=2)[g, :, :, c * P:(c + 1) * P]),
                ):
                    sp.dma_start(dst, src).then_inc(step_in[j], 16)

            def load_z(g, q):
                sp.dma_start(z_raw[:, q % 2], A["w_z"][g, :, 2 * q:2 * q + 2]).then_inc(z_in[q % 2], 16)

            def group(g, last):
                for q in range(2, 4):
                    sp.wait_ge(z_lo_done, KT * g + 2 * q - 2)
                    load_z(g, q)
                sp.wait_ge(yn_ready, NT * g)
                sp.dma_start(norm_row[:], A["ssd_norm_row"][bass.ds(g * GW, GW)].partition_broadcast(P)).then_inc(norm_in, 16)
                for c in range(NT):
                    if c % 2 == 0 and not (last and c >= 4):
                        u = 4 * g + c // 2
                        sp.wait_ge(g_lo_done, u + 1)
                        sp.dma_start(g_raw[:, u_slot(c)], A["w_gate"][u + 2]).then_inc(g_in[u_slot(c)], 16)
                    if c == 1 and not last:
                        for q in range(2):
                            sp.wait_ge(z_lo_done, KT * g + KT)
                            load_z(g + 1, q)
                    if not (last and c >= NT - 2):
                        for sem in (diag_done, pv_done, xd_ready, rotated):
                            sp.wait_ge(sem, NT * g + c + 1)
                        if c < NT - 2:
                            load_step(g, c + 2)
                        else:
                            load_step(g + 1, c + 2 - NT)

            def u_slot(c):
                return (c // 2) % 2

            load_step(0, 0)
            for j in range(2):
                sp.dma_start(g_raw[:, j], A["w_gate"][j]).then_inc(g_in[j], 16)
            for q in range(2):
                load_z(0, q)
            for dst, src in ((d_row, "d_row"), (sinks, "sink_row")):
                sp.dma_start(dst[:], A[src].partition_broadcast(P)).then_inc(rows_in, 16)
            load_step(0, 1)
            with sp.Fori(0, NG - 1) as g:
                group(g, False)
            group(NG - 1, True)

        @block.gpsimd
        def _(pool):
            def group(g):
                own = Chain(pool, pool_own, g * OWN)
                heads = bass.ds(g * HPG, HPG)

                def do(ins):
                    own.did(ins)
                    own.wait()

                def rotate(c):
                    pool.wait_ge(step_in[c % 2], 16 * LOADS * (4 * g + c // 2 + 1))
                    pool.wait_ge(qk_turned, NT * g + c)
                    t1, t2 = qk[:, c % 2, :, 0:R2], qk[:, c % 2, :, R2:HD]
                    cs, sn = (t[:, c].unsqueeze(1).to_broadcast([P, REP + 2, R2]) for t in (cos_t, sin_t))
                    own.did(pool.tensor_tensor(m1[:], t1, cs, ALU.mult))
                    do(pool.tensor_tensor(m2[:], t2, sn, ALU.mult))
                    do(pool.tensor_tensor(qr[:, :, 0:R2], m1[:], m2[:], ALU.subtract))
                    own.did(pool.tensor_tensor(m1[:], t2, cs, ALU.mult))
                    do(pool.tensor_tensor(m2[:], t1, sn, ALU.mult))
                    pool.tensor_tensor(qr[:, :, R2:HD], m1[:], m2[:], ALU.add).then_inc(rotated, 1)

                pool.wait_ge(mix_ready, NT * g)
                pool.wait_ge(rows_in, 32)
                for mine, whole in ((dt_g, dt_v), (acs_g, acs), (decay_g, decay)):
                    pool.tensor_copy(mine[:], whole[:, :, heads])
                do(pool.tensor_copy(d_g[:], d_row[:, heads]))
                rotate(0)
                for c in range(NT):
                    j, n = c % 2, NT * g + c
                    pool.wait_ge(step_in[j], 16 * LOADS * (4 * g + c // 2 + 1))
                    pool.wait_ge(diag_done, n)
                    pool.tensor_tensor(seg[:], a_row[:, j], bcast(acs_g[:, c], P), ALU.subtract).then_inc(seg_ready, 1)
                    x_h = x_in[:, j].rearrange("p (h d) -> p h d", d=HD)
                    pool.tensor_tensor(xdt[:].rearrange("p (h d) -> p h d", d=HD), x_h, bcast(dt_g[:, c], HD),
                                       ALU.mult).then_inc(xdt_ready, 1)
                    if c < NT - 1:
                        pool.wait_ge(xdt_ready, n + 1)
                        pool.wait_ge(state_done, (NT - 1) * g + c)
                        pool.tensor_tensor(xdec[:].rearrange("p (h d) -> p h d", d=HD),
                                           xdt[:].rearrange("p (h d) -> p h d", d=HD), bcast(decay_g[:, c], HD),
                                           ALU.mult).then_inc(xdec_ready, 1)
                    pool.wait_ge(gated, n)
                    pool.tensor_tensor(xd[:].rearrange("p (h d) -> p h d", d=HD), x_h, bcast(d_g[:], HD),
                                       ALU.mult).then_inc(xd_ready, 1)
                    pool.wait_ge(decays_done, n + 1)
                    pool.wait_ge(cbm_ready, n + 1)
                    pool.tensor_tensor(seg[:], seg[:], cbm[:].unsqueeze(1).to_broadcast([P, HPG, P]),
                                       ALU.mult).then_inc(mix_ready, 1)
                    if c + 1 < NT:
                        rotate(c + 1)
                return own.n

            OWN = 1 + 5 * NT
            with pool.Fori(0, NG) as g:
                assert group(g) == OWN

        @block.scalar
        def _(act):
            def outputs(g, c):
                n, j, before = NT * g + c, c % 2, 16 * (4 * g + c // 2)
                act.wait_ge(y_turned, n + 1)
                act.wait_ge(y_stored[j], before)
                act.activation(y_t[:, j], ps_e[:].rearrange("p (a n) -> p a n", a=4), ACT.Copy).then_inc(y_out, 1)
                act.wait_ge(o_turned, n + 1)
                act.wait_ge(o_stored[j], before)
                act.activation(o_t[:, j], ps_f[:, 0:2 * P].rearrange("p (a n) -> p a n", a=2), ACT.Copy).then_inc(o_out, 1)
                act.wait_ge(y_out, n + 1)
                act.dma_start(y_s[bass.ds(4 * g, 4), :, c * P:(c + 1) * P].rearrange("a p n -> p a n"),
                              y_t[:, j]).then_inc(y_stored[j], 16)
                act.wait_ge(o_out, n + 1)
                act.dma_start(o_s[bass.ds(2 * g, 2), :, c * P:(c + 1) * P].rearrange("a p n -> p a n"),
                              o_t[:, j]).then_inc(o_stored[j], 16)

            def group(g):
                act.wait_ge(z_done, NT * g)
                for k in range(KT):
                    q = k // 2
                    if k % 2 == 0:
                        act.wait_ge(z_in[q % 2], 16 * (2 * g + q // 2 + 1))
                    act.activation(z_hi[:, k], z_raw[:, q % 2, k % 2], ACT.Copy).then_inc(z_hi_done, 1)
                for c in range(NT):
                    j, n = c % 2, NT * g + c
                    w = (c // 2) % 2
                    act.wait_ge(qk_turned, n + 1)
                    act.wait_ge(scored, n)
                    act.activation(q_t[:], ps_a[:, 0:2 * P].rearrange("p (a n) -> p a n", a=2), ACT.Copy)
                    act.activation(k_t[:, j], ps_a[:, 2 * P:3 * P], ACT.Copy).then_inc(q_ready, 1)
                    act.wait_ge(seg_min, n + 1)
                    act.activation(seg[:], seg[:], ACT.Exp).then_inc(decays_done, 1)
                    if c % 2 == 0:
                        act.wait_ge(g_in[w], 16 * (2 * g + c // 4 + 1))
                        act.wait_ge(gate_done, n)
                        act.activation(g_hi[:, w], g_raw[:, w], ACT.Copy).then_inc(g_hi_done, 1)
                    act.wait_ge(z_done, n + 1)
                    act.wait_ge(sq_done, n)
                    act.activation(silu[:], ps_z[:], ACT.Exp, scale=-1.0).then_inc(z_exp_done, 1)
                    act.wait_ge(max_ready, n + 1)
                    keys = P if c == 0 else 2 * P
                    for r in range(REP):
                        ins = act.activation(sc[:, r, 0:keys], sc[:, r, 0:keys], ACT.Exp, bias=negm[:, r:r + 1],
                                             accum_out=sums[:, r:r + 1])
                    ins.then_inc(exp_done, 1)
                    act.activation(sink_e[:], mx[:, 1], ACT.Exp).then_inc(sink_done, 1)
                    if c:
                        outputs(g, c - 1)
                    act.wait_ge(p_turned, n + 1)
                    act.wait_ge(pv_done, n)
                    b = keys // P
                    act.activation(p_t[:, :, 0:b], ps_s[:].rearrange("p a b (k n) -> p (a b) k n", n=P)[:, :, 0:b],
                                   ACT.Copy).then_inc(p_ready, 1)
                    act.wait_ge(gated, n + 1)
                    act.activation(silu[:], y1[:], ACT.Square, accum_out=stat[:, 0:1]).then_inc(sq_done, 1)
                    act.wait_ge(v_ready, n + 1)
                    act.activation(stat[:, 2:3], stat[:, 1:2], ACT.Ln).then_inc(act_own, 1)
                    act.wait_ge(act_own, n + 1)
                    act.activation(stat[:, 3:4], stat[:, 2:3], ACT.Exp, scale=-0.5).then_inc(r0_ready, 1)
                    act.wait_ge(gate_done, n + 1)
                    act.wait_ge(g_stored[j], 16 * (4 * g + c // 2))
                    act.activation(g_out[:, j], ps_g[:], ACT.Copy).then_inc(gate_out, 1)
                    act.wait_ge(gate_out, n + 1)
                    act.dma_start(gate_s[4 * g + c // 2, :, j * HALF:(j + 1) * HALF], g_out[:, j]).then_inc(g_stored[j], 16)
                outputs(g, NT - 1)

            act.preload_act_table_set("natural_log_exp_and_others")
            with act.Fori(0, NG) as g:
                group(g)
            for sems in (g_stored, y_stored, o_stored):
                for j in range(2):
                    act.wait_ge(sems[j], 16 * NG * NT // 2)

        @block.vector
        def _(dve):
            def group(g):
                own = Chain(dve, dve_own, g * OWN)
                heads = bass.ds(g * HPG, HPG)

                def do(ins):
                    own.did(ins)
                    own.wait()

                for k in range(KT):
                    dve.wait_ge(z_hi_done, KT * g + k + 1)
                    dve.tensor_tensor(z_lo[:, k], z_raw[:, (k // 2) % 2, k % 2], z_hi[:, k].bitcast(F32), ALU.subtract).then_inc(z_lo_done, 1)
                for c in range(NT):
                    j, n = c % 2, NT * g + c
                    w = (c // 2) % 2
                    dve.wait_ge(seg_ready, n + 1)
                    dve.tensor_scalar(seg[:], seg[:], 0.0, None, ALU.min).then_inc(seg_min, 1)
                    dve.wait_ge(cb_done, n + 1)
                    dve.wait_ge(mix_ready, n)
                    dve.tensor_tensor(cbm[:], ps_d[:, 0:P], utri[:], ALU.mult).then_inc(cbm_ready, 1)
                    if c % 2 == 0:
                        dve.wait_ge(g_hi_done, 4 * g + c // 2 + 1)
                        dve.tensor_tensor(g_lo[:, w], g_raw[:, w], g_hi[:, w].bitcast(F32), ALU.subtract).then_inc(g_lo_done, 1)
                    keys, first = (P, 1) if c == 0 else (2 * P, 0 if j else 1)
                    mask = band[:, first:first + keys // P].rearrange("p b k -> p (b k)").unsqueeze(1)
                    dve.wait_ge(scored, n + 1)
                    dve.wait_ge(p_turned, n)
                    for a in range(2):
                        ins = dve.scalar_tensor_tensor(sc[:, 2 * a:2 * a + 2, 0:keys], ps_s[:, a, :, 0:keys], HD ** -0.5,
                                                       mask.to_broadcast([P, 2, keys]), ALU.mult, ALU.add)
                    ins.then_inc(masked, 1)
                    dve.wait_ge(masked, n + 1)
                    do(dve.tensor_reduce(mx[:, 0], sc[:, :, 0:keys], AX, ALU.max))
                    if c == 0:
                        dve.wait_ge(rows_in, 32)
                    sink = sinks[:, bass.ds(g * REP, REP)]
                    dve.wait_ge(sink_done, n)
                    do(dve.tensor_tensor(mx[:, 0], mx[:, 0], sink, ALU.max))
                    own.did(dve.tensor_scalar(negm[:], mx[:, 0], -1.0, None, ALU.mult))
                    dve.tensor_tensor(mx[:, 1], sink, mx[:, 0], ALU.subtract).then_inc(max_ready, 1)
                    dve.wait_ge(z_exp_done, n + 1)
                    do(dve.tensor_scalar(silu[:], silu[:], 1.0, None, ALU.add))
                    do(dve.reciprocal(silu[:], silu[:]))
                    dve.tensor_tensor(silu[:], ps_z[:], silu[:], ALU.mult).then_inc(z_used, 1)
                    heads_of = lambda t: t.rearrange("p (h d) -> p h d", d=HD)
                    if c:
                        dve.wait_ge(off_done, (NT - 1) * g + c)
                        own.did(dve.tensor_tensor(heads_of(y1[:]), heads_of(ps_e[:]), bcast(ea[:, c, heads], HD), ALU.mult))
                    if c == 0:
                        dve.wait_ge(state_done, (NT - 1) * g + 1)
                        dve.tensor_copy(state[:], ps_f[:]).then_inc(state_ready, 1)
                    elif c < NT - 1:
                        do(dve.tensor_tensor(heads_of(kept[:]), heads_of(state[:]), bcast(cdecay[:, c, heads], HD), ALU.mult))
                        dve.wait_ge(state_done, (NT - 1) * g + c + 1)
                        dve.tensor_tensor(state[:], kept[:], ps_f[:], ALU.add).then_inc(state_ready, 1)
                    dve.wait_ge(diag_done, n + 1)
                    dve.wait_ge(xd_ready, n + 1)
                    dve.tensor_tensor(xd[:], ps_d[:], xd[:], ALU.add).then_inc(y2_ready, 1)
                    dve.wait_ge(y2_ready, n + 1)
                    dve.wait_ge(z_used, n + 1)
                    if c:
                        do(dve.tensor_tensor(xd[:], xd[:], y1[:], ALU.add))
                    dve.tensor_tensor(y1[:], xd[:], silu[:], ALU.mult).then_inc(gated, 1)
                    dve.wait_ge(sink_done, n + 1)
                    do(dve.tensor_tensor(rden[:], sums[:], sink_e[:], ALU.add))
                    do(dve.reciprocal(rden[:], rden[:]))
                    dve.wait_ge(sq_done, n + 1)
                    dve.tensor_scalar(stat[:, 1:2], stat[:, 0:1], 1.0 / GW, EPS, ALU.mult, ALU.add).then_inc(v_ready, 1)
                    dve.wait_ge(r0_ready, n + 1)
                    newton(dve, own, stat[:, 3:4], stat[:, 1:2], stat[:, 4:5], stat[:, 5:6])
                    dve.wait_ge(y_turned, n)
                    if c == 0:
                        dve.wait_ge(norm_in, 16 * (g + 1))
                    dve.scalar_tensor_tensor(yn[:], y1[:], stat[:, 5:6], norm_row[:], ALU.mult,
                                             ALU.mult).then_inc(yn_ready, 1)
                    dve.wait_ge(pv_done, n + 1)
                    dve.wait_ge(o_turned, n)
                    dve.tensor_tensor(o_tok[:].rearrange("p (a b d) -> p b a d", a=2, b=2),
                                      ps_a[:, 0:REP * HD].rearrange("p (b a d) -> p b a d", a=2, b=2),
                                      rden[:].rearrange("p (b a) -> p b a", a=2).unsqueeze(3).to_broadcast([P, 2, 2, HD]),
                                      ALU.mult).then_inc(o_ready, 1)
                return own.n

            OWN = 10 * NT + 2 * (NT - 1) + (NT - 2)
            with dve.Fori(0, NG) as g:
                n = group(g)
                assert n == OWN, n

        @block.tensor
        def _(pe):
            def gate(g, c, ks):
                j, w = c % 2, (c // 2) % 2
                if ks[0] == 0:
                    pe.wait_ge(g_lo_done, 4 * g + c // 2 + 1)
                    pe.wait_ge(gate_out, NT * g + c)
                for k in ks:
                    last = matmul3(pe, ps_g[:], g_hi[:, w, k], g_lo[:, w, k], u_hi[:, k, j * HALF:(j + 1) * HALF],
                                   u_lo[:, k, j * HALF:(j + 1) * HALF], k == 0, k == KT - 1)
                if ks[-1] == KT - 1:
                    last.then_inc(gate_done, 1)

            def z(g, c):
                pe.wait_ge(z_used, NT * g + c)
                for k in range(KT):
                    if c == 0:
                        pe.wait_ge(z_lo_done, KT * g + k + 1)
                    last = matmul3(pe, ps_z[:], u_hi[:, k, c * P:(c + 1) * P], u_lo[:, k, c * P:(c + 1) * P],
                                   z_hi[:, k], z_lo[:, k], k == 0, k == KT - 1)
                last.then_inc(z_done, 1)

            def turn_outputs(g, c):
                n = NT * g + c
                pe.wait_ge(yn_ready, n + 1)
                pe.wait_ge(y_out, n)
                for a in range(4):
                    last = pe.transpose(ps_e[:, a * P:(a + 1) * P], yn[:, a * P:(a + 1) * P], ident[:])
                last.then_inc(y_turned, 1)
                pe.wait_ge(o_ready, n + 1)
                if c < NT - 1:
                    pe.wait_ge(state_ready, (NT - 1) * g + c + 1)
                else:
                    pe.wait_ge(o_out, n)
                for a in range(2):
                    last = pe.transpose(ps_f[:, a * P:(a + 1) * P], o_tok[:, a * P:(a + 1) * P], ident[:])
                last.then_inc(o_turned, 1)

            def group(g):
                for c in range(NT):
                    j, n = c % 2, NT * g + c
                    pe.wait_ge(step_in[j], 16 * LOADS * (4 * g + c // 2 + 1))
                    pe.wait_ge(rotated, n + 1)
                    pe.wait_ge(o_ready, n)
                    for a in range(3):
                        two = qr[:, 2 * a:2 * a + 2].rearrange("p a d -> p (a d)")
                        last = pe.transpose(ps_a[:, a * P:(a + 1) * P], two, ident[:])
                    last.then_inc(qk_turned, 1)
                    pe.wait_ge(y2_ready, n)
                    pe.matmul(ps_d[:, 0:P], bc_f[:, j, 0], bc_f[:, j, 1], start=True, stop=True).then_inc(cb_done, 1)
                    z(g, c)
                    pe.wait_ge(q_ready, n + 1)
                    pe.wait_ge(p_ready, n)
                    keys = P if c == 0 else 2 * P
                    for r in range(REP):
                        lo = (r % 2) * HD
                        last = pe.matmul(ps_s[:, r % 2, r // 2, 0:keys], q_t[lo:lo + HD, r // 2],
                                         k_t[lo:lo + HD].rearrange("p b n -> p (b n)")[:, 0:keys], start=True, stop=True)
                    last.then_inc(scored, 1)
                    if c:
                        turn_outputs(g, c - 1)
                    gate(g, c, range(0, 4))
                    if c:
                        pe.wait_ge(state_ready, (NT - 1) * g + c)
                        pe.wait_ge(y_out, n)
                        pe.matmul(ps_e[:], bc_f[:, j, 1], state[:], start=True, stop=True).then_inc(off_done, 1)
                    if c < NT - 1:
                        pe.wait_ge(xdec_ready, (NT - 1) * g + c + 1)
                        pe.wait_ge(o_out, n)
                        pe.matmul(ps_f[:], b_tok[:, j], xdec[:], start=True, stop=True).then_inc(state_done, 1)
                    pe.wait_ge(mix_ready, n + 1)
                    pe.wait_ge(xdt_ready, n + 1)
                    for h in range(HPG):
                        last = pe.matmul(ps_d[:, h * HD:(h + 1) * HD], seg[:, h], xdt[:, h * HD:(h + 1) * HD], start=True, stop=True)
                    last.then_inc(diag_done, 1)
                    pe.wait_ge(exp_done, n + 1)
                    for r in range(REP):
                        for b in range(keys // P):
                            last = pe.transpose(ps_s[:, r // 2, r % 2, b * P:(b + 1) * P], sc[:, r, b * P:(b + 1) * P], ident[:])
                    last.then_inc(p_turned, 1)
                    gate(g, c, range(4, KT))
                    pe.wait_ge(p_ready, n + 1)
                    for r in range(REP):
                        for b in range(keys // P):
                            block_of = c if b == j else c - 1
                            last = pe.matmul(ps_a[:, r * HD:(r + 1) * HD], p_t[:, r, b], v_in[:, block_of % 4],
                                             start=(b == 0), stop=(b == keys // P - 1))
                    last.then_inc(pv_done, 1)
                turn_outputs(g, NT - 1)

            with pe.Fori(0, NG) as g:
                group(g)


def merge(nc, A, gate_s, src_s, merged_s, part, ssd):
    NB = 2 if ssd else 1
    NK = NB * KT
    w_name, gate_0 = ("w_ssd_out", 0) if ssd else ("w_attn_out", KT)
    with Stage(nc, "ms" if ssd else "ma") as s:
        w_raw = s.sb("w_raw", [P, 2, KT, P])
        w_hi = s.sb("w_hi", [P, 2, KT, P], F32R)
        w_lo = s.sb("w_lo", [P, 2, KT, P], F32R)
        src = s.sb("src", [P, 2, SEQ])
        s_hi = s.sb("s_hi", [P, NK, SEQ], F32R)
        s_lo = s.sb("s_lo", [P, NK, SEQ], F32R)
        sig = s.sb("sig", [P, 2, SEQ])
        ps = s.ps("ps", [P, 2, SEQ])
        w_in, s_in, sig_in, stored = s.sems("w_in", 2), s.sems("s_in", 2), s.sems("sig_in", 2), s.sems("stored", 2)
        w_hi_done, w_lo_done, s_hi_done, s_lo_done, sig_done, product_done, scaled, out_done, block_used = (
            s.sem(n) for n in "w_hi_done w_lo_done s_hi_done s_lo_done sig_done product_done scaled out_done block_used".split())
        block = s.block()
        BLOCKS = KT * NB

        @block.sync
        def _(sp):
            for q in range(2):
                sp.dma_start(w_raw[:, q], A[w_name][q]).then_inc(w_in[q], 16)
            for k in range(NK):
                if k >= 2:
                    sp.wait_ge(s_lo_done, k - 1)
                sp.dma_start(src[:, k % 2], src_s[k]).then_inc(s_in[k % 2], 16)
            for j in range(2):
                sp.dma_start(sig[:, j], gate_s[gate_0 + j]).then_inc(sig_in[j], 16)

            def pair(i, last):
                for j in range(2):
                    f = 2 * i + j
                    for b in range(NB):
                        q = f * NB + b
                        if not (last and j * NB + b >= 2 * NB - 2):
                            sp.wait_ge(w_lo_done, q + 1)
                            w = (j * NB + b) % 2
                            sp.dma_start(w_raw[:, w], A[w_name][q + 2]).then_inc(w_in[w], 16)
                    if ssd:
                        sp.wait_ge(out_done, f + 1)
                        sp.dma_start(merged_s[f], sig[:, j]).then_inc(stored[j], 16)
                    if not last:
                        if ssd:
                            sp.wait_ge(stored[j], 16 * (i + 1))
                        else:
                            sp.wait_ge(out_done, f + 1)
                        sp.dma_start(sig[:, j], gate_s[f + (2 + gate_0)]).then_inc(sig_in[j], 16)

            with sp.Fori(0, KT // 2 - 1) as i:
                pair(i, False)
            pair(KT // 2 - 1, True)
            if ssd:
                for j in range(2):
                    sp.wait_ge(stored[j], 16 * KT // 2)

        @block.scalar
        def _(act):
            def split_w(q, w, use):
                act.wait_ge(w_in[w], 16 * (use + 1))
                act.activation(w_hi[:, w], w_raw[:, w], ACT.Copy).then_inc(w_hi_done, 1)

            def pair(i, last):
                for j in range(2):
                    f = 2 * i + j
                    act.wait_ge(sig_in[j], 16 * (i + 1))
                    act.activation(sig[:, j], sig[:, j], ACT.Sigmoid).then_inc(sig_done, 1)
                    for b in range(NB):
                        p = j * NB + b
                        if not (last and p >= 2 * NB - 2):
                            act.wait_ge(block_used, 2 * NB * i + p + 1)
                            split_w(None, p % 2, NB * i + (p + 2) // 2)

            for w in range(2):
                split_w(w, w, 0)
            for k in range(NK):
                act.wait_ge(s_in[k % 2], 16 * (k // 2 + 1))
                act.activation(s_hi[:, k], src[:, k % 2], ACT.Copy).then_inc(s_hi_done, 1)
            with act.Fori(0, KT // 2 - 1) as i:
                pair(i, False)
            pair(KT // 2 - 1, True)

        @block.vector
        def _(dve):
            def split_w(q, w):
                dve.wait_ge(w_hi_done, q + 1)
                dve.tensor_tensor(w_lo[:, w], w_raw[:, w], w_hi[:, w].bitcast(F32), ALU.subtract).then_inc(w_lo_done, 1)

            def pair(i, last):
                for j in range(2):
                    f = 2 * i + j
                    for b in range(NB):
                        p = j * NB + b
                        if not (last and p >= 2 * NB - 2):
                            split_w(2 * NB * i + p + 2, p % 2)
                    dve.wait_ge(product_done, f + 1)
                    dve.wait_ge(sig_done, f + 1)
                    mine = part[:, bass.ds(f, 1)].rearrange("p a n -> p (a n)")
                    if ssd:
                        dve.tensor_tensor(sig[:, j], sig[:, j], ps[:, j], ALU.mult).then_inc(scaled, 1)
                        dve.wait_ge(scaled, f + 1)
                        dve.tensor_tensor(sig[:, j], sig[:, j], mine, ALU.add).then_inc(out_done, 1)
                    else:
                        dve.tensor_tensor(mine, sig[:, j], ps[:, j], ALU.mult).then_inc(out_done, 1)

            for w in range(2):
                split_w(w, w)
            for k in range(NK):
                dve.wait_ge(s_hi_done, k + 1)
                dve.tensor_tensor(s_lo[:, k], src[:, k % 2], s_hi[:, k].bitcast(F32), ALU.subtract).then_inc(s_lo_done, 1)
            with dve.Fori(0, KT // 2 - 1) as i:
                pair(i, False)
            pair(KT // 2 - 1, True)

        @block.tensor
        def _(pe):
            def pair(i, first):
                for j in range(2):
                    f = 2 * i + j
                    if not first:
                        pe.wait_ge(out_done, f - 1)
                    for b in range(NB):
                        p = j * NB + b
                        pe.wait_ge(w_lo_done, 2 * NB * i + p + 1)
                        for h in range(2):
                            for k in range(KT):
                                kk = b * KT + k
                                if first and h == 0 and j == 0:
                                    pe.wait_ge(s_lo_done, kk + 1)
                                last = matmul3(pe, ps[:, j, h * HALF:(h + 1) * HALF], w_hi[:, p % 2, k], w_lo[:, p % 2, k],
                                               s_hi[:, kk, h * HALF:(h + 1) * HALF], s_lo[:, kk, h * HALF:(h + 1) * HALF],
                                               kk == 0, kk == NK - 1)
                        last.then_inc(block_used, 1)
                    pe.wait_ge(block_used, 2 * NB * i + (j + 1) * NB)
                    pe.sem_inc(product_done, 1)

            pair(0, True)
            with pe.Fori(1, KT // 2) as i:
                pair(i, False)


def mix_rows(nc, A, merged_s, x2_s, h_hi, h_lo, ident):
    with Stage(nc, "mr") as s:
        src = s.sb("src", [P, 2, SEQ])
        w_raw = s.sb("w_raw", [P, 2, D])
        w_hi = s.sb("w_hi", [P, KT, D], F32R)
        w_lo = s.sb("w_lo", [P, KT, D], F32R)
        post = s.sb("post", [P, D])
        pre = s.sb("pre", [P, D])
        x_t = s.sb("x_t", [P, 2, D])
        y_t = s.sb("y_t", [P, 2, D])
        stat = s.sb("stat", [P, 2, NT, 6])
        ps = s.ps("ps", [P, 2, D])
        ps_t = s.ps("ps_t", [P, KT, P])
        rows_in, s_in, w_in, x_in, stored = s.sem("rows_in"), s.sems("s_in", 2), s.sems("w_in", 2), s.sems("x_in", 2), s.sems("stored", 2)
        s_hi_done, s_lo_done, w_hi_done, w_lo_done, product_done, sq_done, v_ready, r0_ready, y_ready, x2_ready, h_ready, turned, h_hi_done, h_lo_done, act_own, dve_own = (
            s.sem(n) for n in ("s_hi_done s_lo_done w_hi_done w_lo_done product_done sq_done v_ready r0_ready y_ready "
                               "x2_ready h_ready turned h_hi_done h_lo_done act_own dve_own").split())
        block = s.block()
        x_tiles = A["x"].rearrange("(t p) d -> t p d", p=P)

        @block.sync
        def _(sp):
            for k in range(KT):
                if k >= 2:
                    sp.wait_ge(s_lo_done, k - 1)
                    sp.wait_ge(w_lo_done, k - 1)
                sp.dma_start(src[:, k % 2], merged_s[k]).then_inc(s_in[k % 2], 16)
                sp.dma_start(w_raw[:, k % 2], A["w_mix"][:, k]).then_inc(w_in[k % 2], 16)
            sp.dma_start(post[:], A["mix_post_row"].partition_broadcast(P)).then_inc(rows_in, 16)
            sp.dma_start(pre[:], A["ffn_pre_row"].partition_broadcast(P)).then_inc(rows_in, 16)
            for t in range(NT):
                if t >= 2:
                    sp.wait_ge(stored[t % 2], 16 * (t // 2))
                    sp.wait_ge(h_ready, t - 1)
                sp.dma_start(x_t[:, t % 2], x_tiles[t]).then_inc(x_in[t % 2], 16)

        @block.gpsimd
        def _(pool):
            for t in range(NT):
                pool.wait_ge(x2_ready, t + 1)
                pool.dma_start(x2_s[t], x_t[:, t % 2]).then_inc(stored[t % 2], 16)
            for j in range(2):
                pool.wait_ge(stored[j], 16 * NT // 2)

        @block.scalar
        def _(act):
            def rstd(t, n, src_ap, junk):
                act.activation(junk, src_ap, ACT.Square, accum_out=stat[:, n, t, 0:1]).then_inc(sq_done, 1)
                act.wait_ge(v_ready, 2 * t + n + 1)
                act.activation(stat[:, n, t, 2:3], stat[:, n, t, 1:2], ACT.Ln).then_inc(act_own, 1)
                act.wait_ge(act_own, 2 * t + n + 1)
                act.activation(stat[:, n, t, 3:4], stat[:, n, t, 2:3], ACT.Exp, scale=-0.5).then_inc(r0_ready, 1)

            act.preload_act_table_set("natural_log_exp_and_others")
            for k in range(KT):
                act.wait_ge(s_in[k % 2], 16 * (k // 2 + 1))
                act.activation(h_hi[:, k], src[:, k % 2], ACT.Copy).then_inc(s_hi_done, 1)
                act.wait_ge(w_in[k % 2], 16 * (k // 2 + 1))
                act.activation(w_hi[:, k], w_raw[:, k % 2], ACT.Copy).then_inc(w_hi_done, 1)
            for t in range(NT):
                j = t % 2
                act.wait_ge(product_done, t + 1)
                if t >= 2:
                    act.wait_ge(turned, t - 1)
                rstd(t, 0, ps[:, j], y_t[:, j])
                act.wait_ge(x2_ready, t + 1)
                rstd(t, 1, x_t[:, j], y_t[:, j])
                act.wait_ge(turned, t + 1)
                act.activation(h_hi[:, :, t * P:(t + 1) * P], ps_t[:], ACT.Copy).then_inc(h_hi_done, 1)

        @block.vector
        def _(dve):
            own = Chain(dve, dve_own)

            def rstd(t, n):
                dve.wait_ge(sq_done, 2 * t + n + 1)
                dve.tensor_scalar(stat[:, n, t, 1:2], stat[:, n, t, 0:1], 1.0 / D, EPS, ALU.mult, ALU.add).then_inc(v_ready, 1)
                dve.wait_ge(r0_ready, 2 * t + n + 1)
                newton(dve, own, stat[:, n, t, 3:4], stat[:, n, t, 1:2], stat[:, n, t, 4:5], stat[:, n, t, 5:6])

            for k in range(KT):
                dve.wait_ge(s_hi_done, k + 1)
                dve.tensor_tensor(h_lo[:, k], src[:, k % 2], h_hi[:, k].bitcast(F32), ALU.subtract).then_inc(s_lo_done, 1)
                dve.wait_ge(w_hi_done, k + 1)
                dve.tensor_tensor(w_lo[:, k], w_raw[:, k % 2], w_hi[:, k].bitcast(F32), ALU.subtract).then_inc(w_lo_done, 1)
            dve.wait_ge(rows_in, 32)
            for t in range(NT):
                j = t % 2
                rstd(t, 0)
                dve.scalar_tensor_tensor(y_t[:, j], ps[:, j], stat[:, 0, t, 5:6], post[:], ALU.mult, ALU.mult).then_inc(y_ready, 1)
                dve.wait_ge(y_ready, t + 1)
                dve.wait_ge(x_in[j], 16 * (t // 2 + 1))
                dve.tensor_tensor(x_t[:, j], x_t[:, j], y_t[:, j], ALU.add).then_inc(x2_ready, 1)
                rstd(t, 1)
                dve.scalar_tensor_tensor(y_t[:, j], x_t[:, j], stat[:, 1, t, 5:6], pre[:], ALU.mult, ALU.mult).then_inc(h_ready, 1)
                dve.wait_ge(h_hi_done, t + 1)
                dve.tensor_tensor(h_lo[:, :, t * P:(t + 1) * P], ps_t[:], h_hi[:, :, t * P:(t + 1) * P].bitcast(F32),
                                  ALU.subtract).then_inc(h_lo_done, 1)

        @block.tensor
        def _(pe):
            def turn(t):
                pe.wait_ge(h_ready, t + 1)
                if t:
                    pe.wait_ge(h_lo_done, t)
                for k in range(KT):
                    last = pe.transpose(ps_t[:, k], y_t[:, t % 2, k * P:(k + 1) * P], ident[:])
                last.then_inc(turned, 1)

            for t in range(NT):
                if t >= 2:
                    pe.wait_ge(y_ready, t - 1)
                for k in range(KT):
                    if t == 0:
                        pe.wait_ge(s_lo_done, k + 1)
                        pe.wait_ge(w_lo_done, k + 1)
                    for h in range(2):
                        last = matmul3(pe, ps[:, t % 2, h * HALF:(h + 1) * HALF], h_hi[:, k, t * P:(t + 1) * P],
                                       h_lo[:, k, t * P:(t + 1) * P], w_hi[:, k, h * HALF:(h + 1) * HALF],
                                       w_lo[:, k, h * HALF:(h + 1) * HALF], k == 0, k == KT - 1)
                last.then_inc(product_done, 1)
                if t:
                    turn(t - 1)
            turn(NT - 1)


def ffn_up(nc, A, ff_s, h_hi, h_lo):
    TAPS = 3
    with Stage(nc, "fu") as s:
        cw = s.sb("cw", [P, FT, 2, TAPS + 1])
        w_raw = s.sb("w_raw", [P, 2, KT, P])
        w_hi = s.sb("w_hi", [P, 2, KT, P], F32R)
        w_lo = s.sb("w_lo", [P, 2, KT, P], F32R)
        xc = s.sb("xc", [P, 2, SEQ])
        ff = s.sb("ff", [P, SEQ])
        ps = s.ps("ps", [P, 2, SEQ])
        cw_in, w_in, stored = s.sem("cw_in"), s.sems("w_in", 2), s.sem("stored")
        hi_done, lo_done, product_done, tap_done, dve_own, conv_done, gelu_done, ff_done = (
            s.sem(n) for n in "hi_done lo_done product_done tap_done dve_own conv_done gelu_done ff_done".split())
        block = s.block()

        @block.sync
        def _(sp):
            sp.dma_start(cw[:], A["ffn_conv"]).then_inc(cw_in, 16)
            for j in range(2):
                sp.dma_start(w_raw[:, j], A["w_up"][j]).then_inc(w_in[j], 16)
            with sp.Fori(0, FT - 1) as i:
                for j in range(2):
                    sp.wait_ge(lo_done, 2 * i + j + 1)
                    sp.dma_start(w_raw[:, j], A["w_up"][2 * i + (j + 2)]).then_inc(w_in[j], 16)

        @block.gpsimd
        def _(pool):
            with pool.Fori(0, FT) as i:
                pool.wait_ge(ff_done, i + 1)
                pool.dma_start(ff_s[i], ff[:]).then_inc(stored, 16)
            pool.wait_ge(stored, 16 * FT)

        @block.scalar
        def _(act):
            def split(i, j):
                act.wait_ge(w_in[j], 16 * (i + 1))
                act.activation(w_hi[:, j], w_raw[:, j], ACT.Copy).then_inc(hi_done, 1)

            def pair(i, last):
                for j in range(2):
                    act.wait_ge(product_done, 2 * i + j + 1)
                    if j == 0:
                        act.wait_ge(ff_done, i)
                    act.activation(xc[:, j], ps[:, j], ACT.Identity, scale=cw[:, bass.ds(i, 1), j, TAPS - 1],
                                   bias=cw[:, bass.ds(i, 1), j, TAPS]).then_inc(tap_done, 1)
                    if not last:
                        split(i + 1, j)
                    if j == 0:
                        act.wait_ge(conv_done, 2 * i + 1)
                        act.activation(xc[:, 0], xc[:, 0], ACT.Gelu_apprx_tanh).then_inc(gelu_done, 1)

            for j in range(2):
                split(0, j)
            act.wait_ge(cw_in, 16)
            with act.Fori(0, FT - 1) as i:
                pair(i, False)
            pair(FT - 1, True)

        @block.vector
        def _(dve):
            def split(i, j):
                dve.wait_ge(hi_done, 2 * i + j + 1)
                dve.tensor_tensor(w_lo[:, j], w_raw[:, j], w_hi[:, j].bitcast(F32), ALU.subtract).then_inc(lo_done, 1)

            def pair(i, last):
                for j in range(2):
                    f = 2 * i + j
                    dve.wait_ge(tap_done, f + 1)
                    dve.scalar_tensor_tensor(xc[:, j, 1:SEQ], ps[:, j, 0:SEQ - 1], cw[:, bass.ds(i, 1), j, 1],
                                             xc[:, j, 1:SEQ], ALU.mult, ALU.add).then_inc(dve_own, 1)
                    dve.wait_ge(dve_own, f + 1)
                    dve.scalar_tensor_tensor(xc[:, j, 2:SEQ], ps[:, j, 0:SEQ - 2], cw[:, bass.ds(i, 1), j, 0],
                                             xc[:, j, 2:SEQ], ALU.mult, ALU.add).then_inc(conv_done, 1)
                    if not last:
                        split(i + 1, j)
                dve.wait_ge(gelu_done, i + 1)
                dve.wait_ge(conv_done, 2 * i + 2)
                dve.wait_ge(stored, 16 * i)
                dve.tensor_tensor(ff[:], xc[:, 0], xc[:, 1], ALU.mult).then_inc(ff_done, 1)

            for j in range(2):
                split(0, j)
            dve.wait_ge(cw_in, 16)
            with dve.Fori(0, FT - 1) as i:
                pair(i, False)
            pair(FT - 1, True)

        @block.tensor
        def _(pe):
            def pair(i, first):
                for j in range(2):
                    f = 2 * i + j
                    pe.wait_ge(lo_done, f + 1)
                    if not first:
                        pe.wait_ge(conv_done, f - 1)
                    for h in range(2):
                        for k in range(KT):
                            last = matmul3(pe, ps[:, j, h * HALF:(h + 1) * HALF], w_hi[:, j, k], w_lo[:, j, k],
                                           h_hi[:, k, h * HALF:(h + 1) * HALF], h_lo[:, k, h * HALF:(h + 1) * HALF],
                                           k == 0, k == KT - 1)
                    last.then_inc(product_done, 1)

            pair(0, True)
            with pe.Fori(1, FT) as i:
                pair(i, False)


def ffn_down(nc, A, ff_s, x2_s, out, ident):
    BLK = ((0, 8), (8, 8), (16, 6))
    TH = NT // 2
    with Stage(nc, "fd") as s:
        w_raw = s.sb("w_raw", [P, 2, KT, P])
        w_hi = s.sb("w_hi", [P, 2, KT, P], F32R)
        w_lo = s.sb("w_lo", [P, 2, KT, P], F32R)
        src = s.sb("src", [P, 2, HALF])
        s_hi = s.sb("s_hi", [P, FT, HALF], F32R)
        s_lo = s.sb("s_lo", [P, FT, HALF], F32R)
        d_f = s.sb("d_f", [P, 2, HALF])
        d_tok = s.sb("d_tok", [P, TH, D])
        x2 = s.sb("x2", [P, 2, D])
        sq = s.sb("sq", [P, D])
        post = s.sb("post", [P, D])
        stat = s.sb("stat", [P, NT, 6])
        ps = s.ps("ps", [P, 2, HALF])
        ps_t = s.ps("ps_t", [P, 2, TH, P])
        row_in, w_in, s_in, x2_in, stored = s.sem("row_in"), s.sems("w_in", 2), s.sems("s_in", 2), s.sems("x2_in", 2), s.sems("stored", 2)
        w_hi_done, w_lo_done, block_used, s_hi_done, s_lo_done, product_done, f_out, turned, t_out = (
            s.sem(n) for n in "w_hi_done w_lo_done block_used s_hi_done s_lo_done product_done f_out turned t_out".split())
        sq_done, v_ready, r0_ready, scaled, out_ready, act_own, dve_own = (
            s.sem(n) for n in "sq_done v_ready r0_ready scaled out_ready act_own dve_own".split())
        block = s.block()
        NBK = len(BLK)
        PB = 2 * NBK
        PAIRS = KT // 2
        out_tiles = out.rearrange("(t p) d -> t p d", p=P)

        def block_src(f, b):
            k0, n = BLK[b]
            return A["w_down"][f, :, k0:k0 + n]

        def ahead(b, j):
            p = j * NBK + b + 2
            return p // NBK - j, p % NBK

        @block.sync
        def _(sp):
            sp.dma_start(post[:], A["ffn_post_row"].partition_broadcast(P)).then_inc(row_in, 16)

            def pair(base, i, last):
                for j in range(2):
                    for b in range(NBK):
                        p = j * NBK + b
                        if last and p >= PB - 2:
                            continue
                        sp.wait_ge(w_lo_done, PB * (base + i) + p + 1)
                        df, bb = ahead(b, j)
                        sp.dma_start(w_raw[:, p % 2, 0:BLK[bb][1]], block_src(2 * i + j + df, bb)).then_inc(w_in[p % 2], 16)

            for h in range(2):
                if h:
                    sp.wait_ge(w_lo_done, PB * PAIRS)
                for b in range(2):
                    sp.dma_start(w_raw[:, b], block_src(0, b)).then_inc(w_in[b], 16)
                for k in range(FT):
                    if h * FT + k >= 2:
                        sp.wait_ge(s_lo_done, h * FT + k - 1)
                    sp.dma_start(src[:, k % 2], ff_s[k, :, h * HALF:(h + 1) * HALF]).then_inc(s_in[k % 2], 16)
                with sp.Fori(0, PAIRS - 1) as i:
                    pair(h * PAIRS, i, False)
                pair(h * PAIRS, PAIRS - 1, True)

        @block.gpsimd
        def _(pool):
            for t in range(2):
                pool.dma_start(x2[:, t], x2_s[t]).then_inc(x2_in[t], 16)
            for t in range(NT):
                pool.wait_ge(out_ready, t + 1)
                pool.dma_start(out_tiles[t], x2[:, t % 2]).then_inc(stored[t % 2], 16)
                if t < NT - 2:
                    pool.wait_ge(stored[t % 2], 16 * (t // 2 + 1))
                    pool.dma_start(x2[:, t % 2], x2_s[t + 2]).then_inc(x2_in[t % 2], 16)
            for j in range(2):
                pool.wait_ge(stored[j], 16 * NT // 2)

        @block.scalar
        def _(act):
            def split_w(use, p, n):
                act.wait_ge(w_in[p % 2], 16 * (use + 1))
                act.activation(w_hi[:, p % 2, 0:n], w_raw[:, p % 2, 0:n], ACT.Copy).then_inc(w_hi_done, 1)

            def pair(base, i, last):
                for j in range(2):
                    f = 2 * (base + i) + j
                    for b in range(NBK):
                        p = j * NBK + b
                        if not (last and p >= PB - 2):
                            act.wait_ge(block_used, PB * (base + i) + p + 1)
                            split_w(NBK * (base + i) + (p + 2) // 2, p, BLK[ahead(b, j)[1]][1])
                    act.wait_ge(product_done, f + 1)
                    act.wait_ge(turned, f if j else f)
                    act.activation(d_f[:, j], ps[:, j], ACT.Copy).then_inc(f_out, 1)

            def norm(h):
                for t in range(TH):
                    n = h * TH + t
                    act.wait_ge(t_out, KT * (h + 1))
                    if n:
                        act.wait_ge(sq_done, n)
                    act.activation(sq[:], d_tok[:, t], ACT.Square, accum_out=stat[:, n, 0:1]).then_inc(sq_done, 1)
                    act.wait_ge(v_ready, n + 1)
                    act.activation(stat[:, n, 2:3], stat[:, n, 1:2], ACT.Ln).then_inc(act_own, 1)
                    act.wait_ge(act_own, n + 1)
                    act.activation(stat[:, n, 3:4], stat[:, n, 2:3], ACT.Exp, scale=-0.5).then_inc(r0_ready, 1)

            act.preload_act_table_set("natural_log_exp_and_others")
            for h in range(2):
                if h:
                    act.wait_ge(block_used, PB * PAIRS)
                for b in range(2):
                    split_w(h * NBK * PAIRS, b, BLK[b][1])
                for k in range(FT):
                    n = h * FT + k
                    act.wait_ge(s_in[k % 2], 16 * (n // 2 + 1))
                    act.activation(s_hi[:, k], src[:, k % 2], ACT.Copy).then_inc(s_hi_done, 1)
                if h:
                    norm(0)
                with act.Fori(0, PAIRS - 1) as i:
                    pair(h * PAIRS, i, False)
                pair(h * PAIRS, PAIRS - 1, True)
            norm(1)

        @block.vector
        def _(dve):
            own = Chain(dve, dve_own)

            def split_w(q, p, n):
                dve.wait_ge(w_hi_done, q + 1)
                dve.tensor_tensor(w_lo[:, p % 2, 0:n], w_raw[:, p % 2, 0:n], w_hi[:, p % 2, 0:n].bitcast(F32),
                                  ALU.subtract).then_inc(w_lo_done, 1)

            def pair(base, i, last):
                for j in range(2):
                    for b in range(NBK):
                        p = j * NBK + b
                        if not (last and p >= PB - 2):
                            split_w(PB * (base + i) + p + 2, p, BLK[ahead(b, j)[1]][1])
                    dve.wait_ge(turned, 2 * (base + i) + j + 1)
                    dve.tensor_copy(d_tok[:, :, bass.ds((2 * i + j) * P, P)], ps_t[:, j]).then_inc(t_out, 1)

            def norm(h):
                for t in range(TH):
                    n = h * TH + t
                    dve.wait_ge(sq_done, n + 1)
                    dve.tensor_scalar(stat[:, n, 1:2], stat[:, n, 0:1], 1.0 / D, EPS, ALU.mult, ALU.add).then_inc(v_ready, 1)
                    dve.wait_ge(r0_ready, n + 1)
                    newton(dve, own, stat[:, n, 3:4], stat[:, n, 1:2], stat[:, n, 4:5], stat[:, n, 5:6])
                    dve.scalar_tensor_tensor(d_tok[:, t], d_tok[:, t], stat[:, n, 5:6], post[:], ALU.mult, ALU.mult).then_inc(scaled, 1)
                    dve.wait_ge(scaled, n + 1)
                    dve.wait_ge(x2_in[n % 2], 16 * (n // 2 + 1))
                    dve.tensor_tensor(x2[:, n % 2], x2[:, n % 2], d_tok[:, t], ALU.add).then_inc(out_ready, 1)

            dve.wait_ge(row_in, 16)
            for h in range(2):
                for b in range(2):
                    split_w(h * PB * PAIRS + b, b, BLK[b][1])
                for k in range(FT):
                    dve.wait_ge(s_hi_done, h * FT + k + 1)
                    dve.tensor_tensor(s_lo[:, k], src[:, k % 2], s_hi[:, k].bitcast(F32), ALU.subtract).then_inc(s_lo_done, 1)
                if h:
                    norm(0)
                with dve.Fori(0, PAIRS - 1) as i:
                    pair(h * PAIRS, i, False)
                pair(h * PAIRS, PAIRS - 1, True)
            norm(1)

        @block.tensor
        def _(pe):
            def turn(f, j):
                pe.wait_ge(f_out, f + 1)
                for t in range(TH):
                    last = pe.transpose(ps_t[:, j, t], d_f[:, j, t * P:(t + 1) * P], ident[:])
                last.then_inc(turned, 1)

            def pair(h, i, first):
                base = h * PAIRS
                for j in range(2):
                    f = 2 * (base + i) + j
                    if not (first and h == 0):
                        pe.wait_ge(f_out, f - 1)
                        pe.wait_ge(t_out, f - 1)
                    for b, (k0, n) in enumerate(BLK):
                        p = j * NBK + b
                        pe.wait_ge(w_lo_done, PB * (base + i) + p + 1)
                        for k in range(n):
                            if first and j == 0:
                                pe.wait_ge(s_lo_done, h * FT + k0 + k + 1)
                            last = matmul3(pe, ps[:, j], w_hi[:, p % 2, k], w_lo[:, p % 2, k], s_hi[:, k0 + k],
                                           s_lo[:, k0 + k], k0 + k == 0, k0 + k == FT - 1)
                        last.then_inc(block_used, 1)
                        if b == 0 and not (first and j == 0):
                            turn(f - 1, 1 - j)
                    pe.wait_ge(block_used, PB * (base + i) + (j + 1) * NBK)
                    pe.sem_inc(product_done, 1)

            for h in range(2):
                pair(h, 0, True)
                with pe.Fori(1, PAIRS) as i:
                    pair(h, i, False)
                turn(2 * PAIRS * (h + 1) - 1, 1)


def lay_out(x, positions, norm_mix_pre_w, w_in, ssd_conv_w, ssd_conv_b, ssd_dt_bias, ssd_a_log, ssd_d,
            ssd_norm_w, ssd_w_out, attn_sinks, attn_w_out, w_mix_out, norm_mix_post_w,
            norm_ffn_pre_w, ffn_w_up, ffn_conv_w, ffn_conv_b, ffn_w_down, norm_ffn_post_w):
    import numpy as np

    def tiles(w, width):
        k, n = w.shape
        return np.ascontiguousarray(w.reshape(k // P, P, n // width, width).transpose(2, 1, 0, 3))

    def columns(*rows):
        return np.ascontiguousarray(np.stack([r.reshape(-1, P).T for r in rows], axis=2))

    w = w_in[0]
    xbc_0, rows_0, gate_0 = INNER, INNER + CONV_DIM, INNER + CONV_DIM + ROWS
    w_ssd = ssd_w_out[0]
    w_up = ffn_w_up[0].reshape(D, 2, FT, P).transpose(0, 2, 1, 3).reshape(D, 2 * FF)
    conv = [r.reshape(2, FT, P) for r in (*ffn_conv_w[0], ffn_conv_b[0])]
    head_order = [(h % 2) * 2 + h // 2 for h in range(REP)]
    freq = (10000.0 ** (-np.arange(HD // 2, dtype=np.float32) * 2.0 / HD)).astype(np.float32)
    return {
        "x": x[0],
        "pos": np.ascontiguousarray(positions[0].reshape(NT, P).T),
        "mix_pre_row": norm_mix_pre_w[0],
        "w_rows": tiles(w[:, rows_0:gate_0], RW),
        "w_xbc": tiles(w[:, xbc_0:rows_0], P),
        "w_z": tiles(w[:, 0:INNER], GW),
        "w_gate": tiles(w[:, gate_0:], P),
        "ssd_conv": columns(*ssd_conv_w[0], ssd_conv_b[0]),
        "dt_bias_row": ssd_dt_bias[0],
        "a_log_row": ssd_a_log[0],
        "d_row": ssd_d[0],
        "freq_row": freq,
        "ssd_norm_row": ssd_norm_w[0],
        "w_ssd_out": np.ascontiguousarray(w_ssd.reshape(2, KT, P, KT, P).transpose(3, 0, 2, 1, 4)).reshape(2 * KT, P, KT, P),
        "sink_row": np.ascontiguousarray(attn_sinks[0].reshape(NG, REP)[:, head_order]).reshape(-1),
        "w_attn_out": tiles(attn_w_out[0], P),
        "w_mix": np.ascontiguousarray(w_mix_out[0].reshape(KT, P, D).transpose(1, 0, 2)),
        "mix_post_row": norm_mix_post_w[0],
        "ffn_pre_row": norm_ffn_pre_w[0],
        "w_up": tiles(w_up, P),
        "ffn_conv": np.ascontiguousarray(np.stack(conv, axis=3).transpose(2, 1, 0, 3)),
        "w_down": tiles(ffn_w_down[0], P),
        "ffn_post_row": norm_ffn_post_w[0],
    }


def kernel(**inputs):
    import numpy as np
    import concourse.bacc as bacc
    from concourse.bass_utils import run_bass_kernel_spmd

    arrays = lay_out(**{k: np.asarray(v) for k, v in inputs.items()})
    arrays = {f"in_{k}": np.ascontiguousarray(v) for k, v in arrays.items()}
    nc = bacc.Bacc("TRN2", target_bir_lowering=False, num_devices=1)
    aps = {k[3:]: nc.dram_tensor(k, v.shape, mybir.dt.from_np(v.dtype), kind="ExternalInput").ap()
           for k, v in arrays.items()}
    out = nc.dram_tensor("out", (SEQ, D), F32, kind="ExternalOutput").ap()
    hybrid_block_kernel(nc, aps, out)
    got = run_bass_kernel_spmd(nc, [arrays], core_ids=[0])
    return got.results[0]["out"].reshape(1, SEQ, D)
```

```python
from contextlib import ExitStack

import concourse.bass as bass
from concourse import mybir

P = 128
SEQ = 1024
D = 1024
KT = D // P
NT = SEQ // P
HALF = 512
INNER = 2048
NH = 32
NG = 4
HPG = NH // NG
HD = 64
GW = HPG * HD
CONV_DIM = INNER + 2 * NG * P
XT = CONV_DIM // P
AH = 16
REP = AH // NG
ROWS = NH + D + 2 * NG * HD
RC = 4
RW = ROWS // RC
Q0 = NH
K0 = Q0 + D
V0 = K0 + NG * HD
FF = 2816
FT = FF // P
EPS = 1e-6
NEG = -1.0e30
MAGIC = 1.5 * 2.0 ** 23
FAR = 4096.0

F32 = mybir.dt.float32
F32R = mybir.dt.float32r
I32 = mybir.dt.int32
ALU = mybir.AluOpType
ACT = mybir.ActivationFunctionType
AX = mybir.AxisListType.X


def turn_parts(count):
    digits = 314159265358979323846264338327950288419716939937510582097494459230781640628620899
    rest = 2 * digits * 2 ** 400 // 10 ** (len(str(digits)) - 1)
    parts = []
    for _ in range(count):
        shift = rest.bit_length() - 7
        top = rest >> shift
        parts.append(float(top) * 2.0 ** (shift - 400))
        rest -= top << shift
    return parts


TURN = turn_parts(9)


def hybrid_block_kernel(nc, A, out):
    def scratch(name, shape):
        return nc.dram_tensor(name, shape, F32, kind="Internal").ap()

    rows_s = scratch("rows_s", (NT, P, ROWS))
    acs_s = scratch("acs_s", (NT * NH, P))
    feat_s = scratch("feat_s", (2 * NG, P, SEQ))
    tok_s = scratch("tok_s", (NT, P, CONV_DIM))
    gate_s = scratch("gate_s", (2 * KT, P, SEQ))
    o_s = scratch("o_s", (KT, P, SEQ))
    y_s = scratch("y_s", (2 * KT, P, SEQ))
    merged_s = scratch("merged_s", (KT, P, SEQ))
    x2_s = scratch("x2_s", (NT, P, D))

    with ExitStack() as whole:
        def hold(ctx, name, shape, dt=F32):
            return ctx.enter_context(nc.sbuf_tensor(name, shape, dt))

        ident = hold(whole, "ident", [P, P])
        consts_done = whole.enter_context(nc.semaphore("consts_done"))

        with ExitStack() as early:
            utri = hold(early, "utri", [P, P])
            band = hold(early, "band", [P, 3, P])
            ones = hold(early, "ones", [P, P])
            u_hi = hold(early, "u_hi", [P, KT, SEQ], F32R)
            u_lo = hold(early, "u_lo", [P, KT, SEQ], F32R)
            dt_v = hold(early, "dt_v", [P, NT, NH])
            acs = hold(early, "acs", [P, NT, NH])
            ea = hold(early, "ea", [P, NT, NH])
            decay = hold(early, "decay", [P, NT, NH])
            cdecay = hold(early, "cdecay", [P, NT, NH])
            cos_t = hold(early, "cos_t", [P, NT, HD // 2])
            sin_t = hold(early, "sin_t", [P, NT, HD // 2])
            projection_rows(nc, A, rows_s, ident, utri, band, ones, consts_done, u_hi, u_lo)
            tables(nc, A, rows_s, acs_s, ident, utri, ones, dt_v, acs, ea, decay, cdecay, cos_t, sin_t)
            conv_features(nc, A, feat_s, tok_s, ident, u_hi, u_lo)
            mixers(nc, A, rows_s, acs_s, feat_s, tok_s, gate_s, o_s, y_s, ident, utri, band, u_hi, u_lo,
                   dt_v, acs, ea, decay, cdecay, cos_t, sin_t)
        with ExitStack() as late:
            part = hold(late, "part", [P, KT, SEQ])
            merge(nc, A, gate_s, o_s, merged_s, part, False)
            merge(nc, A, gate_s, y_s, merged_s, part, True)
        with ExitStack() as late:
            h_hi = hold(late, "h_hi", [P, KT, SEQ], F32R)
            h_lo = hold(late, "h_lo", [P, KT, SEQ], F32R)
            mix_rows(nc, A, merged_s, x2_s, h_hi, h_lo, ident)
            ff = whole.enter_context(nc.sbuf_tensor("ff", [P, FT, SEQ], F32, side="right"))
            ffn_up(nc, A, ff, h_hi, h_lo)
        ffn_down(nc, A, ff, x2_s, out, ident)


class Stage:

    def __init__(self, nc, tag):
        self.nc, self.tag, self.ctx, self.used = nc, tag, ExitStack(), []

    def __enter__(self):
        self.ctx.__enter__()
        return self

    def __exit__(self, *a):
        self.ctx.__exit__(*a)
        self.nc.clear_and_free_semaphores(self.used)
        self.nc.all_engine_barrier()

    def sb(self, name, shape, dt=F32):
        return self.ctx.enter_context(self.nc.sbuf_tensor(f"{self.tag}_{name}", shape, dt))

    def ps(self, name, shape):
        return self.ctx.enter_context(self.nc.psum_tensor(f"{self.tag}_{name}", shape, F32))

    def sem(self, name):
        self.used.append(self.nc.alloc_semaphore(name=f"{self.tag}_{name}"))
        return self.used[-1]

    def sems(self, name, n):
        return [self.sem(f"{name}{i}") for i in range(n)]

    def block(self):
        return self.ctx.enter_context(self.nc.Block())


class Chain:

    def __init__(self, eng, sem, base=0):
        self.eng, self.sem, self.n, self.base = eng, sem, 0, base

    def did(self, ins):
        ins.then_inc(self.sem, 1)
        self.n += 1
        return self.n

    def wait(self, n=None):
        self.eng.wait_ge(self.sem, self.base + (self.n if n is None else n))


def matmul3(pe, dst, s_hi, s_lo, m_hi, m_lo, first, last):
    pe.matmul(dst, s_hi, m_hi, start=first, stop=False)
    pe.matmul(dst, s_hi, m_lo, start=False, stop=False)
    return pe.matmul(dst, s_lo, m_hi, start=False, stop=last)


def bcast(ap, n):
    return ap.unsqueeze(2).to_broadcast([ap.shape[0], ap.shape[1], n])


def projection_rows(nc, A, rows_s, ident, utri, band, ones, consts_done, u_hi, u_lo):
    with Stage(nc, "pr") as s:
        x_t = s.sb("x_t", [P, 2, D])
        sq = s.sb("sq", [P, D])
        w_row = s.sb("w_row", [P, D])
        stat = s.sb("stat", [P, NT, 6])
        w_raw = s.sb("w_raw", [P, 2, KT // 2, RW])
        w_hi = s.sb("w_hi", [P, RC, KT, RW], F32R)
        w_lo = s.sb("w_lo", [P, RC, KT, RW], F32R)
        o_t = s.sb("o_t", [P, RC, RW])
        ps_t = s.ps("ps_t", [P, KT, P])
        ps_o = s.ps("ps_o", [P, RC, HALF])
        x_in = s.sems("x_in", 2)
        row_in, sq_done, v_ready, r0_ready, xn_ready = (s.sem(n) for n in "row_in sq_done v_ready r0_ready xn_ready".split())
        act_own, dve_own = s.sem("act_own"), s.sem("dve_own")
        w_in = s.sems("w_in", 2)
        w_hi_done, w_lo_done, t_done, u_hi_done, u_lo_done = (s.sem(n) for n in "w_hi_done w_lo_done t_done u_hi_done u_lo_done".split())
        rows_done, rows_out = s.sem("rows_done"), s.sem("rows_out")
        stored = s.sems("stored", RC)
        block = s.block()
        x_tiles = A["x"].rearrange("(t p) d -> t p d", p=P)

        @block.sync
        def _(sp):
            for t in range(2):
                sp.dma_start(x_t[:, t], x_tiles[t]).then_inc(x_in[t], 16)
            sp.dma_start(w_row[:], A["mix_pre_row"].partition_broadcast(P)).then_inc(row_in, 16)
            for h in range(2 * RC):
                if h >= 2:
                    sp.wait_ge(w_lo_done, h - 1)
                sp.dma_start(w_raw[:, h % 2], A["w_rows"][h // 2, :, (h % 2) * 4:(h % 2) * 4 + 4]).then_inc(w_in[h % 2], 16)
            for t in range(2, NT):
                sp.wait_ge(t_done, t - 1)
                sp.dma_start(x_t[:, t % 2], x_tiles[t]).then_inc(x_in[t % 2], 16)

        @block.gpsimd
        def _(pool):
            pool.memset(ident[:], 0.0).then_inc(consts_done, 1)
            pool.memset(utri[:], 1.0).then_inc(consts_done, 1)
            pool.memset(band[:], 0.0).then_inc(consts_done, 1)
            pool.memset(ones[:], 1.0).then_inc(consts_done, 1)
            pool.wait_ge(consts_done, 4)
            pool.affine_select(out=ident[:], in_=ident[:], compare_op=ALU.not_equal, fill=1.0, base=0,
                               pattern=[[-1, P]], channel_multiplier=1).then_inc(consts_done, 1)
            pool.affine_select(out=utri[:], in_=utri[:], compare_op=ALU.is_ge, fill=0.0, base=0,
                               pattern=[[1, P]], channel_multiplier=-1).then_inc(consts_done, 1)
            for b, (sign, base) in enumerate([(1, -1), (-1, 0), (1, -1)]):
                pool.affine_select(out=band[:, b], in_=band[:, b], compare_op=ALU.is_ge, fill=NEG, base=base,
                                   pattern=[[sign, P]], channel_multiplier=-sign).then_inc(consts_done, 1)
            for t in range(NT):
                for c in range(RC):
                    pool.wait_ge(rows_out, t * RC + c + 1)
                    pool.dma_start(rows_s[t, :, c * RW:(c + 1) * RW], o_t[:, c]).then_inc(stored[c], 16)
            for c in range(RC):
                pool.wait_ge(stored[c], 16 * NT)

        @block.scalar
        def _(act):
            own = Chain(act, act_own)

            def square(t):
                act.wait_ge(x_in[t % 2], 16 * (t // 2 + 1))
                if t:
                    act.wait_ge(sq_done, t)
                act.activation(sq[:], x_t[:, t % 2], ACT.Square, accum_out=stat[:, t, 0:1]).then_inc(sq_done, 1)

            def root(t):
                act.wait_ge(v_ready, t + 1)
                own.did(act.activation(stat[:, t, 2:3], stat[:, t, 1:2], ACT.Ln))
                own.wait()
                act.activation(stat[:, t, 3:4], stat[:, t, 2:3], ACT.Exp, scale=-0.5).then_inc(r0_ready, 1)

            def split_w(h):
                act.wait_ge(w_in[h % 2], 16 * (h // 2 + 1))
                c, k = h // 2, (h % 2) * 4
                act.activation(w_hi[:, c, k:k + 4], w_raw[:, h % 2], ACT.Copy).then_inc(w_hi_done, 1)

            def split_u(t):
                act.wait_ge(t_done, t + 1)
                act.activation(u_hi[:, :, t * P:(t + 1) * P], ps_t[:], ACT.Copy).then_inc(u_hi_done, 1)

            square(0)
            split_w(0)
            root(0)
            split_w(1)
            square(1)
            split_u(0)
            split_w(2)
            root(1)
            for h in range(3, 8):
                split_w(h)
            split_u(1)
            for t in range(2, NT):
                square(t)
                root(t)
                split_u(t)

        @block.vector
        def _(dve):
            own = Chain(dve, dve_own)

            def norm(t):
                dve.wait_ge(sq_done, t + 1)
                dve.tensor_scalar(stat[:, t, 1:2], stat[:, t, 0:1], 1.0 / D, EPS, ALU.mult, ALU.add).then_inc(v_ready, 1)
                dve.wait_ge(r0_ready, t + 1)
                newton(dve, own, stat[:, t, 3:4], stat[:, t, 1:2], stat[:, t, 4:5], stat[:, t, 5:6])
                if t == 0:
                    dve.wait_ge(row_in, 16)
                dve.scalar_tensor_tensor(x_t[:, t % 2], x_t[:, t % 2], stat[:, t, 5:6], w_row[:], ALU.mult,
                                         ALU.mult).then_inc(xn_ready, 1)

            def split_w(h):
                dve.wait_ge(w_hi_done, h + 1)
                c, k = h // 2, (h % 2) * 4
                dve.tensor_tensor(w_lo[:, c, k:k + 4], w_raw[:, h % 2], w_hi[:, c, k:k + 4].bitcast(F32),
                                  ALU.subtract).then_inc(w_lo_done, 1)

            def split_u(t):
                dve.wait_ge(u_hi_done, t + 1)
                dve.tensor_tensor(u_lo[:, :, t * P:(t + 1) * P], ps_t[:], u_hi[:, :, t * P:(t + 1) * P].bitcast(F32),
                                  ALU.subtract).then_inc(u_lo_done, 1)

            def rows(t):
                for c in range(RC):
                    dve.wait_ge(rows_done, t * RC + c + 1)
                    if t:
                        dve.wait_ge(stored[c], 16 * t)
                    dve.tensor_copy(o_t[:, c], ps_o[:, c, 0:RW]).then_inc(rows_out, 1)

            norm(0)
            split_w(0)
            split_u(0)
            split_w(1)
            split_w(2)
            norm(1)
            for h in range(3, 8):
                split_w(h)
            split_u(1)
            for t in range(NT):
                if t + 2 < NT:
                    norm(t + 2)
                rows(t)
                if t + 2 < NT:
                    split_u(t + 2)

        @block.tensor
        def _(pe):
            pe.wait_ge(consts_done, 5)

            def turn(t):
                pe.wait_ge(xn_ready, t + 1)
                if t:
                    pe.wait_ge(u_lo_done, t)
                for k in range(KT):
                    last = pe.transpose(ps_t[:, k], x_t[:, t % 2, k * P:(k + 1) * P], ident[:])
                last.then_inc(t_done, 1)

            turn(0)
            for t in range(NT):
                if t == 0:
                    turn(1)
                elif t + 1 < NT:
                    turn(t + 1)
                pe.wait_ge(u_lo_done, t + 1)
                for c in range(RC):
                    if t:
                        pe.wait_ge(rows_out, (t - 1) * RC + c + 1)
                    for k in range(KT):
                        if t == 0 and k % 4 == 0:
                            pe.wait_ge(w_lo_done, 2 * c + k // 4 + 1)
                        last = matmul3(pe, ps_o[:, c, 0:RW], u_hi[:, k, t * P:(t + 1) * P], u_lo[:, k, t * P:(t + 1) * P],
                                       w_hi[:, c, k], w_lo[:, c, k], k == 0, k == KT - 1)
                    last.then_inc(rows_done, 1)


def newton(dve, own, r0, v, tmp, r):
    own.did(dve.tensor_scalar(tmp, r0, r0, v, ALU.mult, ALU.mult))
    own.wait()
    own.did(dve.tensor_scalar(tmp, tmp, -0.5, 1.5, ALU.mult, ALU.add))
    own.wait()
    own.did(dve.tensor_tensor(r, r0, tmp, ALU.mult))
    own.wait()


def tables(nc, A, rows_s, acs_s, ident, utri, ones, dt_v, acs, ea, decay, cdecay, cos_t, sin_t):
    W = NT * NH
    with Stage(nc, "tb") as s:
        raw = s.sb("raw", [P, NT, NH])
        bias = s.sb("bias", [P, NH])
        alog = s.sb("alog", [P, NH])
        a_neg = s.sb("a_neg", [P, NH])
        freq = s.sb("freq", [P, HD // 2])
        pos = s.sb("pos", [P, NT], I32)
        posf = s.sb("posf", [P, NT])
        adt = s.sb("adt", [P, NT, NH])
        t1 = s.sb("t1", [P, NT, NH])
        t2 = s.sb("t2", [P, NT, NH])
        t3 = s.sb("t3", [P, NT, NH])
        mx = s.sb("mx", [P, NT, NH])
        ang = s.sb("ang", [P, NT, HD // 2])
        k_t = s.sb("k_t", [P, NT, HD // 2])
        m_t = s.sb("m_t", [P, NT, HD // 2])
        half_pi = s.sb("half_pi", [P, 1])
        tot = s.sb("tot", [P, NT, NH])
        acs_f = s.sb("acs_f", [P, 2, P])
        ps_a = s.ps("ps_a", [P, W])
        ps_b = s.ps("ps_b", [P, W])
        ps_c = s.ps("ps_c", [P, 2, P])
        ins_in, raw_in = s.sem("ins_in"), s.sem("raw_in")
        u_need, u_ready, a_ready, adt_ready, sums_done = (s.sem(n) for n in "u_need u_ready a_ready adt_ready sums_done".split())
        dve_own, act_own, ang_ready, acs_ready, turned, flat = (s.sem(n) for n in "dve_own act_own ang_ready acs_ready turned flat".split())
        diff_ready, stored = s.sem("diff_ready"), s.sem("stored")
        block = s.block()

        @block.sync
        def _(sp):
            sp.dma_start(raw[:], rows_s.rearrange("t p n -> p t n")[:, :, 0:NH]).then_inc(raw_in, 16)
            sp.dma_start(bias[:], A["dt_bias_row"].partition_broadcast(P)).then_inc(ins_in, 16)
            sp.dma_start(alog[:], A["a_log_row"].partition_broadcast(P)).then_inc(ins_in, 16)
            sp.dma_start(freq[:], A["freq_row"].partition_broadcast(P)).then_inc(ins_in, 16)
            sp.dma_start(pos[:], A["pos"]).then_inc(ins_in, 16)
            sp.wait_ge(flat, 1)
            sp.dma_start(acs_s.rearrange("(a r) l -> r a l", r=P), acs_f[:]).then_inc(stored, 16)
            sp.wait_ge(stored, 16)

        @block.vector
        def _(dve):
            own = Chain(dve, dve_own)

            def do(ins):
                own.did(ins)
                own.wait()

            dve.wait_ge(raw_in, 16)
            dve.wait_ge(ins_in, 64)
            do(dve.tensor_tensor(t1[:], raw[:], bias[:].unsqueeze(1).to_broadcast([P, NT, NH]), ALU.add))
            do(dve.tensor_scalar(mx[:], t1[:], 0.0, None, ALU.max))
            dve.scalar_tensor_tensor(t2[:], mx[:], -2.0, t1[:], ALU.mult, ALU.add).then_inc(u_need, 1)
            dve.wait_ge(u_ready, 1)
            do(dve.tensor_scalar(t1[:], t3[:], 2.0, None, ALU.add))
            do(dve.reciprocal(t1[:], t1[:]))
            do(dve.tensor_tensor(t3[:], t3[:], t1[:], ALU.mult))
            do(dve.tensor_tensor(t1[:], t3[:], t3[:], ALU.mult))
            do(dve.tensor_scalar(t2[:], t1[:], 1.0 / 19, 1.0 / 17, ALU.mult, ALU.add))
            for n in (15, 13, 11, 9, 7, 5, 3, 1):
                do(dve.tensor_tensor(t2[:], t2[:], t1[:], ALU.mult))
                do(dve.tensor_scalar(t2[:], t2[:], 1.0 / n, None, ALU.add))
            do(dve.tensor_tensor(t2[:], t2[:], t3[:], ALU.mult))
            do(dve.scalar_tensor_tensor(dt_v[:], t2[:], 2.0, mx[:], ALU.mult, ALU.add))
            dve.wait_ge(a_ready, 1)
            dve.scalar_tensor_tensor(adt[:], dt_v[:], -1.0, a_neg[:].unsqueeze(1).to_broadcast([P, NT, NH]),
                                     ALU.mult, ALU.mult).then_inc(adt_ready, 1)
            do(dve.memset(half_pi[:], 1.5707963267948966))
            do(dve.tensor_copy(posf[:], pos[:]))
            do(dve.tensor_tensor(ang[:], posf[:].unsqueeze(2).to_broadcast([P, NT, HD // 2]),
                                 freq[:].unsqueeze(1).to_broadcast([P, NT, HD // 2]), ALU.mult))
            turn = sum(TURN)
            for scale in (FAR, 1.0):
                do(dve.tensor_scalar(k_t[:], ang[:], 1.0 / (turn * scale), MAGIC, ALU.mult, ALU.add))
                do(dve.tensor_scalar(k_t[:], k_t[:], MAGIC, None, ALU.subtract))
                for part in TURN:
                    do(dve.scalar_tensor_tensor(ang[:], k_t[:], -part * scale, ang[:], ALU.mult, ALU.add))
            do(dve.tensor_scalar(ang[:], ang[:], 3.1415925, -3.1415925, ALU.min, ALU.max))
            dve.tensor_scalar(m_t[:], ang[:], -1.0, None, ALU.mult).then_inc(dve_own, 1)
            own.n += 1
            own.wait()
            dve.tensor_tensor(m_t[:], m_t[:], ang[:], ALU.max).then_inc(ang_ready, 1)
            dve.wait_ge(sums_done, 1)
            dve.tensor_copy(acs[:].rearrange("p t h -> p (t h)"), ps_a[:]).then_inc(acs_ready, 1)
            do(dve.tensor_copy(tot[:].rearrange("p t h -> p (t h)"), ps_b[:]))
            dve.tensor_tensor(decay[:], tot[:], acs[:], ALU.subtract).then_inc(diff_ready, 1)
            dve.wait_ge(turned, 1)
            dve.tensor_copy(acs_f[:], ps_c[:]).then_inc(flat, 1)

        @block.scalar
        def _(act):
            act.wait_ge(ins_in, 64)
            act.activation(a_neg[:], alog[:], ACT.Exp).then_inc(a_ready, 1)
            act.wait_ge(u_need, 1)
            act.activation(t3[:], t2[:], ACT.Exp).then_inc(u_ready, 1)
            act.wait_ge(diff_ready, 1)
            act.activation(decay[:], decay[:], ACT.Exp)
            act.activation(ea[:], acs[:], ACT.Exp)
            act.activation(cdecay[:], tot[:], ACT.Exp).then_inc(act_own, 1)
            act.wait_ge(ang_ready, 1)
            act.activation(sin_t[:], ang[:], ACT.Sin)
            act.activation(cos_t[:], m_t[:], ACT.Sin, scale=-1.0, bias=half_pi[:]).then_inc(act_own, 1)
            act.wait_ge(act_own, 2)

        @block.tensor
        def _(pe):
            pe.wait_ge(adt_ready, 1)
            flat_adt = adt[:].rearrange("p t h -> p (t h)")
            pe.matmul(ps_a[:], utri[:], flat_adt, start=True, stop=True)
            pe.matmul(ps_b[:], ones[:], flat_adt, start=True, stop=True).then_inc(sums_done, 1)
            pe.wait_ge(acs_ready, 1)
            flat_acs = acs[:].rearrange("p t h -> p (t h)")
            for i in range(2):
                last = pe.transpose(ps_c[:, i], flat_acs[:, i * P:(i + 1) * P], ident[:])
            last.then_inc(turned, 1)


def conv_features(nc, A, feat_s, tok_s, ident, u_hi, u_lo):
    TAPS = 4
    with Stage(nc, "cf") as s:
        cw = s.sb("cw", [P, XT, TAPS + 1])
        w_raw = s.sb("w_raw", [P, 2, KT, P])
        w_hi = s.sb("w_hi", [P, 2, KT, P], F32R)
        w_lo = s.sb("w_lo", [P, 2, KT, P], F32R)
        xc = s.sb("xc", [P, 2, SEQ])
        xt = s.sb("xt", [P, 2, NT, P])
        ps = s.ps("ps", [P, 2, SEQ])
        ps_t = s.ps("ps_t", [P, NT, P])
        cw_in = s.sem("cw_in")
        w_in, f_stored, t_stored = s.sems("w_in", 2), s.sems("f_stored", 2), s.sems("t_stored", 2)
        hi_done, lo_done, product_done, tap_done, dve_own, conv_done, silu_done, turned, t_out = (
            s.sem(n) for n in "hi_done lo_done product_done tap_done dve_own conv_done silu_done turned t_out".split())
        block = s.block()
        n_pairs = XT // 2
        feature_pairs = (INNER // P) // 2

        @block.sync
        def _(sp):
            sp.dma_start(cw[:], A["ssd_conv"]).then_inc(cw_in, 16)
            for j in range(2):
                sp.dma_start(w_raw[:, j], A["w_xbc"][j]).then_inc(w_in[j], 16)
            with sp.Fori(0, n_pairs - 1) as i:
                for j in range(2):
                    sp.wait_ge(lo_done, 2 * i + j + 1)
                    sp.dma_start(w_raw[:, j], A["w_xbc"][2 * i + (j + 2)]).then_inc(w_in[j], 16)

        @block.gpsimd
        def _(pool):
            def store(i, j, features):
                f = 2 * i + j
                if features:
                    pool.wait_ge(silu_done, f + 1)
                    pool.dma_start(feat_s[f - INNER // P], xc[:, j]).then_inc(f_stored[j], 16)
                pool.wait_ge(t_out, f + 1)
                pool.dma_start(tok_s[:, :, bass.ds(f * P, P)].rearrange("t p n -> p t n"), xt[:, j]).then_inc(t_stored[j], 16)

            with pool.Fori(0, feature_pairs) as i:
                for j in range(2):
                    store(i, j, False)
            with pool.Fori(feature_pairs, n_pairs) as i:
                for j in range(2):
                    store(i, j, True)
            for j in range(2):
                pool.wait_ge(t_stored[j], 16 * n_pairs)
                pool.wait_ge(f_stored[j], 16 * (n_pairs - feature_pairs))

        @block.scalar
        def _(act):
            def split(i, j):
                f = 2 * i + j
                act.wait_ge(w_in[j], 16 * (i + 1))
                act.activation(w_hi[:, j], w_raw[:, j], ACT.Copy).then_inc(hi_done, 1)

            def tile(i, j, first, features, last):
                f = 2 * i + j
                act.wait_ge(product_done, f + 1)
                if not first:
                    act.wait_ge(turned, f - 1)
                    if features:
                        act.wait_ge(f_stored[j], 16 * (i - feature_pairs))
                act.activation(xc[:, j], ps[:, j], ACT.Identity, scale=cw[:, bass.ds(f, 1), TAPS - 1],
                               bias=cw[:, bass.ds(f, 1), TAPS]).then_inc(tap_done, 1)
                if not last:
                    split(i + 1, j)
                act.wait_ge(conv_done, f + 1)
                act.activation(xc[:, j], xc[:, j], ACT.Silu).then_inc(silu_done, 1)

            for j in range(2):
                split(0, j)
            act.wait_ge(cw_in, 16)
            for j in range(2):
                tile(0, j, True, False, False)
            with act.Fori(1, feature_pairs) as i:
                for j in range(2):
                    tile(i, j, False, False, False)
            for j in range(2):
                tile(feature_pairs, j, False, False, False)
            with act.Fori(feature_pairs + 1, n_pairs - 1) as i:
                for j in range(2):
                    tile(i, j, False, True, False)
            for j in range(2):
                tile(n_pairs - 1, j, False, True, True)

        @block.vector
        def _(dve):
            def split(i, j):
                f = 2 * i + j
                dve.wait_ge(hi_done, f + 1)
                dve.tensor_tensor(w_lo[:, j], w_raw[:, j], w_hi[:, j].bitcast(F32), ALU.subtract).then_inc(lo_done, 1)

            def conv(i, j, last):
                f = 2 * i + j
                dve.wait_ge(tap_done, f + 1)
                for n in range(1, TAPS):
                    if n > 1:
                        dve.wait_ge(dve_own, f * (TAPS - 2) + n - 1)
                    ins = dve.scalar_tensor_tensor(xc[:, j, n:SEQ], ps[:, j, 0:SEQ - n], cw[:, bass.ds(f, 1), TAPS - 1 - n],
                                                   xc[:, j, n:SEQ], ALU.mult, ALU.add)
                    ins.then_inc(dve_own if n < TAPS - 1 else conv_done, 1)
                if not last:
                    split(i + 1, j)

            def by_tokens(i, j, first):
                f = 2 * i + j
                dve.wait_ge(turned, f + 1)
                if not first:
                    dve.wait_ge(t_stored[j], 16 * i)
                dve.tensor_copy(xt[:, j], ps_t[:]).then_inc(t_out, 1)

            for j in range(2):
                split(0, j)
            dve.wait_ge(cw_in, 16)
            conv(0, 0, False)
            conv(0, 1, False)
            by_tokens(0, 0, True)
            conv(1, 0, False)
            by_tokens(0, 1, True)
            conv(1, 1, False)
            by_tokens(1, 0, False)
            with dve.Fori(2, n_pairs - 1) as i:
                conv(i, 0, False)
                by_tokens(i - 1, 1, False)
                conv(i, 1, False)
                by_tokens(i, 0, False)
            conv(n_pairs - 1, 0, True)
            by_tokens(n_pairs - 2, 1, False)
            conv(n_pairs - 1, 1, True)
            by_tokens(n_pairs - 1, 0, False)
            by_tokens(n_pairs - 1, 1, False)

        @block.tensor
        def _(pe):
            def half(i, j, h):
                for k in range(KT):
                    last = matmul3(pe, ps[:, j, h * HALF:(h + 1) * HALF], w_hi[:, j, k], w_lo[:, j, k],
                                   u_hi[:, k, h * HALF:(h + 1) * HALF], u_lo[:, k, h * HALF:(h + 1) * HALF], k == 0, k == KT - 1)
                return last

            def turn(f, j, first):
                pe.wait_ge(silu_done, f + 1)
                if not first:
                    pe.wait_ge(t_out, f)
                for t in range(NT):
                    last = pe.transpose(ps_t[:, t], xc[:, j, t * P:(t + 1) * P], ident[:])
                last.then_inc(turned, 1)

            def tile(i, j, first):
                f = 2 * i + j
                pe.wait_ge(lo_done, f + 1)
                if not first:
                    pe.wait_ge(conv_done, f - 1)
                half(i, j, 0)
                half(i, j, 1).then_inc(product_done, 1)
                if not (first and j == 0):
                    turn(f - 1, 1 - j, first and j == 1)

            for j in range(2):
                tile(0, j, True)
            with pe.Fori(1, n_pairs) as i:
                for j in range(2):
                    tile(i, j, False)
            turn(XT - 1, 1, False)


def mixers(nc, A, rows_s, acs_s, feat_s, tok_s, gate_s, o_s, y_s, ident, utri, band, u_hi, u_lo,
           dt_v, acs, ea, decay, cdecay, cos_t, sin_t):
    R2 = HD // 2
    with Stage(nc, "mx") as s:
        z_raw = s.sb("z_raw", [P, 2, 2, GW])
        z_hi = s.sb("z_hi", [P, KT, GW], F32R)
        z_lo = s.sb("z_lo", [P, KT, GW], F32R)
        g_raw = s.sb("g_raw", [P, 2, KT, P])
        g_hi = s.sb("g_hi", [P, 2, KT, P], F32R)
        g_lo = s.sb("g_lo", [P, 2, KT, P], F32R)
        g_out = s.sb("g_out", [P, 2, HALF])
        x_in = s.sb("x_in", [P, 2, GW])
        b_tok = s.sb("b_tok", [P, 2, P])
        bc_f = s.sb("bc_f", [P, 2, 2, P])
        a_row = s.sb("a_row", [P, 2, HPG, P])
        dt_g, acs_g, decay_g = (s.sb(n, [P, NT, HPG]) for n in ("dt_g", "acs_g", "decay_g"))
        d_g = s.sb("d_g", [P, HPG])
        seg = s.sb("seg", [P, HPG, P])
        cbm = s.sb("cbm", [P, P])
        xdt = s.sb("xdt", [P, GW])
        xdec = s.sb("xdec", [P, GW])
        xd = s.sb("xd", [P, GW])
        state = s.sb("state", [P, GW])
        kept = s.sb("kept", [P, GW])
        y1 = s.sb("y1", [P, GW])
        silu = s.sb("silu", [P, GW])
        yn = s.sb("yn", [P, GW])
        y_t = s.sb("y_t", [P, 2, 4, P])
        stat = s.sb("stat", [P, 6])
        norm_row = s.sb("norm_row", [P, GW])
        d_row = s.sb("d_row", [P, NH])
        qk = s.sb("qk", [P, 2, REP + 2, HD])
        v_in = s.sb("v_in", [P, 4, HD])
        m1 = s.sb("m1", [P, REP + 2, R2])
        m2 = s.sb("m2", [P, REP + 2, R2])
        qr = s.sb("qr", [P, REP + 2, HD])
        q_t = s.sb("q_t", [P, 2, P])
        k_t = s.sb("k_t", [P, 2, P])
        sc = s.sb("sc", [P, REP, 2 * P])
        mx = s.sb("mx", [P, 2, REP])
        negm = s.sb("negm", [P, REP])
        sums = s.sb("sums", [P, REP])
        sink_e = s.sb("sink_e", [P, REP])
        rden = s.sb("rden", [P, REP])
        sinks = s.sb("sinks", [P, AH])
        p_t = s.sb("p_t", [P, REP, 2, P])
        o_tok = s.sb("o_tok", [P, REP * HD])
        o_t = s.sb("o_t", [P, 2, 2, P])
        ps_z = s.ps("ps_z", [P, HALF])
        ps_g = s.ps("ps_g", [P, HALF])
        ps_a = s.ps("ps_a", [P, HALF])
        ps_s = s.ps("ps_s", [P, 2, 2, 2 * P])
        ps_d = s.ps("ps_d", [P, HALF])
        ps_e = s.ps("ps_e", [P, HALF])
        ps_f = s.ps("ps_f", [P, HALF])

        rows_in, norm_in, step_in, z_in, g_in = s.sem("rows_in"), s.sem("norm_in"), s.sems("step_in", 2), s.sems("z_in", 2), s.sems("g_in", 2)
        z_hi_done, z_lo_done, g_hi_done, g_lo_done = (s.sem(n) for n in "z_hi_done z_lo_done g_hi_done g_lo_done".split())
        z_done, z_exp_done, z_used, gate_done, gate_out = (s.sem(n) for n in "z_done z_exp_done z_used gate_done gate_out".split())
        g_stored, y_stored, o_stored = s.sems("g_stored", 2), s.sems("y_stored", 2), s.sems("o_stored", 2)
        seg_ready, seg_min, decays_done, mix_ready, cb_done, cbm_ready = (
            s.sem(n) for n in "seg_ready seg_min decays_done mix_ready cb_done cbm_ready".split())
        xdt_ready, xdec_ready, xd_ready, off_done, state_done, state_ready, diag_done, y2_ready, y1_ready = (
            s.sem(n) for n in "xdt_ready xdec_ready xd_ready off_done state_done state_ready diag_done y2_ready y1_ready".split())
        gated, sq_done, v_ready, r0_ready, yn_ready, y_turned, y_out = (
            s.sem(n) for n in "gated sq_done v_ready r0_ready yn_ready y_turned y_out".split())
        rotated, qk_turned, q_ready, scored, masked, max_ready, exp_done, sink_done, p_turned, p_ready, pv_done, o_ready, o_turned, o_out = (
            s.sem(n) for n in "rotated qk_turned q_ready scored masked max_ready exp_done sink_done p_turned p_ready pv_done o_ready o_turned o_out".split())
        dve_own, pool_own, act_own = s.sem("dve_own"), s.sem("pool_own"), s.sem("act_own")
        block = s.block()
        LOADS = 8

        @block.sync
        def _(sp):
            def load_step(g, c):
                j = c % 2
                for dst, src in (
                    (qk[:, j, 0:REP].rearrange("p a d -> p (a d)"), rows_s[c, :, bass.ds(Q0 + g * (REP * HD), REP * HD)]),
                    (qk[:, j, REP], rows_s[c, :, bass.ds(K0 + g * HD, HD)]),
                    (qk[:, j, REP + 1], rows_s[c, :, bass.ds(K0 + g * HD, HD)]),
                    (v_in[:, c % 4], rows_s[c, :, bass.ds(V0 + g * HD, HD)]),
                    (a_row[:, j].rearrange("p h l -> p (h l)"),
                     acs_s[bass.ds(c * NH + g * HPG, HPG), :].rearrange("h l -> (h l)").partition_broadcast(P)),
                    (x_in[:, j], tok_s[c, :, bass.ds(g * GW, GW)]),
                    (b_tok[:, j], tok_s[c, :, bass.ds(INNER + g * P, P)]),
                    (bc_f[:, j], feat_s.rearrange("(b g) p n -> g p b n", b=2)[g, :, :, c * P:(c + 1) * P]),
                ):
                    sp.dma_start(dst, src).then_inc(step_in[j], 16)

            def load_z(g, q):
                if q >= 2:
                    sp.wait_ge(z_lo_done, KT * g + 2 * q - 2)
                sp.dma_start(z_raw[:, q % 2], A["w_z"][g, :, 2 * q:2 * q + 2]).then_inc(z_in[q % 2], 16)

            def group(g, first, last):
                if not first:
                    sp.wait_ge(yn_ready, NT * g)
                sp.dma_start(norm_row[:], A["ssd_norm_row"][bass.ds(g * GW, GW)].partition_broadcast(P)).then_inc(norm_in, 16)
                for c in range(NT):
                    if c % 2 == 0 and not (last and c >= 4):
                        u = 4 * g + c // 2
                        sp.wait_ge(g_lo_done, u + 1)
                        sp.dma_start(g_raw[:, (c // 2) % 2], A["w_gate"][u + 2]).then_inc(g_in[(c // 2) % 2], 16)
                    if c == 1 and not last:
                        sp.wait_ge(z_lo_done, KT * g + KT)
                        for q in range(2):
                            load_z(g + 1, q)
                    if c == NT - 1 and not last:
                        for q in range(2, 4):
                            load_z(g + 1, q)
                    if not (last and c >= NT - 2):
                        for sem in (diag_done, xd_ready, rotated, pv_done):
                            sp.wait_ge(sem, NT * g + c + 1)
                        if c < NT - 2:
                            load_step(g, c + 2)
                        else:
                            load_step(g + 1, c + 2 - NT)

            for q in range(2):
                load_z(0, q)
            load_step(0, 0)
            sp.dma_start(g_raw[:, 0], A["w_gate"][0]).then_inc(g_in[0], 16)
            for q in range(2, 4):
                load_z(0, q)
            for dst, src in ((d_row, "d_row"), (sinks, "sink_row")):
                sp.dma_start(dst[:], A[src].partition_broadcast(P)).then_inc(rows_in, 16)
            sp.dma_start(g_raw[:, 1], A["w_gate"][1]).then_inc(g_in[1], 16)
            load_step(0, 1)
            group(0, True, False)
            with sp.Fori(1, NG - 1) as g:
                group(g, False, False)
            group(NG - 1, False, True)

        @block.gpsimd
        def _(pool):
            def group(g, first):
                own = Chain(pool, pool_own, g * OWN)
                heads = bass.ds(g * HPG, HPG)

                def do(ins):
                    own.did(ins)
                    own.wait()

                def rotate(c):
                    pool.wait_ge(step_in[c % 2], 16 * LOADS * (4 * g + c // 2 + 1))
                    if not (first and c == 0):
                        pool.wait_ge(qk_turned, NT * g + c)
                    t1, t2 = qk[:, c % 2, :, 0:R2], qk[:, c % 2, :, R2:HD]
                    cs, sn = (t[:, c].unsqueeze(1).to_broadcast([P, REP + 2, R2]) for t in (cos_t, sin_t))
                    own.did(pool.tensor_tensor(m1[:], t1, cs, ALU.mult))
                    do(pool.tensor_tensor(m2[:], t2, sn, ALU.mult))
                    do(pool.tensor_tensor(qr[:, :, 0:R2], m1[:], m2[:], ALU.subtract))
                    own.did(pool.tensor_tensor(m1[:], t2, cs, ALU.mult))
                    do(pool.tensor_tensor(m2[:], t1, sn, ALU.mult))
                    pool.tensor_tensor(qr[:, :, R2:HD], m1[:], m2[:], ALU.add).then_inc(rotated, 1)

                rotate(0)
                if not first:
                    pool.wait_ge(mix_ready, NT * g)
                pool.wait_ge(rows_in, 32)
                for mine, whole in ((dt_g, dt_v), (acs_g, acs), (decay_g, decay)):
                    pool.tensor_copy(mine[:], whole[:, :, heads])
                do(pool.tensor_copy(d_g[:], d_row[:, heads]))
                for c in range(NT):
                    j, n = c % 2, NT * g + c
                    opening = first and c == 0
                    pool.wait_ge(step_in[j], 16 * LOADS * (4 * g + c // 2 + 1))
                    if not opening:
                        pool.wait_ge(diag_done, n)
                    pool.tensor_tensor(seg[:], a_row[:, j], bcast(acs_g[:, c], P), ALU.subtract).then_inc(seg_ready, 1)
                    x_h = x_in[:, j].rearrange("p (h d) -> p h d", d=HD)
                    pool.tensor_tensor(xdt[:].rearrange("p (h d) -> p h d", d=HD), x_h, bcast(dt_g[:, c], HD),
                                       ALU.mult).then_inc(xdt_ready, 1)
                    if c < NT - 1:
                        pool.wait_ge(xdt_ready, n + 1)
                        if not opening:
                            pool.wait_ge(state_done, (NT - 1) * g + c)
                        pool.tensor_tensor(xdec[:].rearrange("p (h d) -> p h d", d=HD),
                                           xdt[:].rearrange("p (h d) -> p h d", d=HD), bcast(decay_g[:, c], HD),
                                           ALU.mult).then_inc(xdec_ready, 1)
                    if not opening:
                        pool.wait_ge(gated, n)
                    pool.tensor_tensor(xd[:].rearrange("p (h d) -> p h d", d=HD), x_h, bcast(d_g[:], HD),
                                       ALU.mult).then_inc(xd_ready, 1)
                    pool.wait_ge(decays_done, n + 1)
                    pool.wait_ge(cbm_ready, n + 1)
                    pool.tensor_tensor(seg[:], seg[:], cbm[:].unsqueeze(1).to_broadcast([P, HPG, P]),
                                       ALU.mult).then_inc(mix_ready, 1)
                    if c + 1 < NT:
                        rotate(c + 1)
                assert own.n == OWN

            OWN = 1 + 5 * NT
            group(0, True)
            with pool.Fori(1, NG) as g:
                group(g, False)

        @block.scalar
        def _(act):
            def outputs(g, c, opening):
                n, j, before = NT * g + c, c % 2, 16 * (4 * g + c // 2)
                act.wait_ge(y_turned, n + 1)
                if not opening:
                    act.wait_ge(y_stored[j], before)
                act.activation(y_t[:, j], ps_e[:].rearrange("p (a n) -> p a n", a=4), ACT.Copy).then_inc(y_out, 1)
                act.wait_ge(o_turned, n + 1)
                if not opening:
                    act.wait_ge(o_stored[j], before)
                act.activation(o_t[:, j], ps_f[:, 0:2 * P].rearrange("p (a n) -> p a n", a=2), ACT.Copy).then_inc(o_out, 1)
                act.wait_ge(y_out, n + 1)
                act.dma_start(y_s[bass.ds(4 * g, 4), :, c * P:(c + 1) * P].rearrange("a p n -> p a n"),
                              y_t[:, j]).then_inc(y_stored[j], 16)
                act.wait_ge(o_out, n + 1)
                act.dma_start(o_s[bass.ds(2 * g, 2), :, c * P:(c + 1) * P].rearrange("a p n -> p a n"),
                              o_t[:, j]).then_inc(o_stored[j], 16)

            def split_z(g, k):
                q = k // 2
                act.wait_ge(z_in[q % 2], 16 * (2 * g + q // 2 + 1))
                act.activation(z_hi[:, k], z_raw[:, q % 2, k % 2], ACT.Copy).then_inc(z_hi_done, 1)

            def split_gate(w, use):
                act.wait_ge(g_in[w], 16 * (use + 1))
                act.activation(g_hi[:, w], g_raw[:, w], ACT.Copy).then_inc(g_hi_done, 1)

            def group(g, first, last):
                for c in range(NT):
                    j, n = c % 2, NT * g + c
                    opening = first and c == 0
                    act.wait_ge(z_done, n + 1)
                    if not opening:
                        act.wait_ge(sq_done, n)
                    act.activation(silu[:], ps_z[:], ACT.Exp, scale=-1.0).then_inc(z_exp_done, 1)
                    act.wait_ge(seg_min, n + 1)
                    act.activation(seg[:], seg[:], ACT.Exp).then_inc(decays_done, 1)
                    act.wait_ge(qk_turned, n + 1)
                    if not opening:
                        act.wait_ge(scored, n)
                    act.activation(q_t[:], ps_a[:, 0:2 * P].rearrange("p (a n) -> p a n", a=2), ACT.Copy)
                    act.activation(k_t[:, j], ps_a[:, 2 * P:3 * P], ACT.Copy).then_inc(q_ready, 1)
                    if c % 2 == 1 and not (last and c == NT - 1):
                        act.wait_ge(gate_done, n)
                        split_gate((c // 2 + 1) % 2, 2 * g + (c // 2 + 1) // 2)
                    if c == NT - 1 and not last:
                        for k in range(4):
                            split_z(g + 1, k)
                    if not opening:
                        outputs(g if c else g - 1, (c - 1) % NT, first and c <= 2)
                    act.wait_ge(max_ready, n + 1)
                    keys = P if c == 0 else 2 * P
                    for r in range(REP):
                        ins = act.activation(sc[:, r, 0:keys], sc[:, r, 0:keys], ACT.Exp, bias=negm[:, r:r + 1],
                                             accum_out=sums[:, r:r + 1])
                    ins.then_inc(exp_done, 1)
                    act.activation(sink_e[:], mx[:, 1], ACT.Exp).then_inc(sink_done, 1)
                    act.wait_ge(gate_done, n + 1)
                    if not (first and c < 2):
                        act.wait_ge(g_stored[j], 16 * (4 * g + c // 2))
                    act.activation(g_out[:, j], ps_g[:], ACT.Copy).then_inc(gate_out, 1)
                    act.wait_ge(gate_out, n + 1)
                    act.dma_start(gate_s[4 * g + c // 2, :, j * HALF:(j + 1) * HALF], g_out[:, j]).then_inc(g_stored[j], 16)
                    if c == NT - 1 and not last:
                        for k in range(4, KT):
                            split_z(g + 1, k)
                    act.wait_ge(gated, n + 1)
                    act.activation(silu[:], y1[:], ACT.Square, accum_out=stat[:, 0:1]).then_inc(sq_done, 1)
                    act.wait_ge(v_ready, n + 1)
                    act.activation(stat[:, 2:3], stat[:, 1:2], ACT.Ln).then_inc(act_own, 1)
                    act.wait_ge(act_own, n + 1)
                    act.activation(stat[:, 3:4], stat[:, 2:3], ACT.Exp, scale=-0.5).then_inc(r0_ready, 1)
                    act.wait_ge(p_turned, n + 1)
                    if not opening:
                        act.wait_ge(pv_done, n)
                    b = keys // P
                    act.activation(p_t[:, :, 0:b], ps_s[:].rearrange("p a b (k n) -> p (a b) k n", n=P)[:, :, 0:b],
                                   ACT.Copy).then_inc(p_ready, 1)

            act.preload_act_table_set("natural_log_exp_and_others")
            for k in range(KT):
                split_z(0, k)
            split_gate(0, 0)
            group(0, True, False)
            with act.Fori(1, NG - 1) as g:
                group(g, False, False)
            group(NG - 1, False, True)
            outputs(NG - 1, NT - 1, False)
            for sems in (g_stored, y_stored, o_stored):
                for j in range(2):
                    act.wait_ge(sems[j], 16 * NG * NT // 2)

        @block.vector
        def _(dve):
            def split_z(g, k):
                dve.wait_ge(z_hi_done, KT * g + k + 1)
                dve.tensor_tensor(z_lo[:, k], z_raw[:, (k // 2) % 2, k % 2], z_hi[:, k].bitcast(F32), ALU.subtract).then_inc(z_lo_done, 1)

            def split_gate(w, u):
                dve.wait_ge(g_hi_done, u + 1)
                dve.tensor_tensor(g_lo[:, w], g_raw[:, w], g_hi[:, w].bitcast(F32), ALU.subtract).then_inc(g_lo_done, 1)

            def attention_out(n, opening):
                dve.wait_ge(pv_done, n + 1)
                if not opening:
                    dve.wait_ge(o_turned, n)
                dve.tensor_tensor(o_tok[:].rearrange("p (a b d) -> p b a d", a=2, b=2),
                                  ps_a[:, 0:REP * HD].rearrange("p (b a d) -> p b a d", a=2, b=2),
                                  rden[:].rearrange("p (b a) -> p b a", a=2).unsqueeze(3).to_broadcast([P, 2, 2, HD]),
                                  ALU.mult).then_inc(o_ready, 1)

            def group(g, first, last):
                own = Chain(dve, dve_own, g * OWN)
                heads = bass.ds(g * HPG, HPG)

                def do(ins):
                    own.did(ins)
                    own.wait()

                for c in range(NT):
                    j, n = c % 2, NT * g + c
                    opening = first and c == 0
                    dve.wait_ge(seg_ready, n + 1)
                    dve.tensor_scalar(seg[:], seg[:], 0.0, None, ALU.min).then_inc(seg_min, 1)
                    if not opening:
                        attention_out(n - 1, first and c == 1)
                    dve.wait_ge(z_exp_done, n + 1)
                    do(dve.tensor_scalar(silu[:], silu[:], 1.0, None, ALU.add))
                    do(dve.reciprocal(silu[:], silu[:]))
                    dve.tensor_tensor(silu[:], ps_z[:], silu[:], ALU.mult).then_inc(z_used, 1)
                    dve.wait_ge(cb_done, n + 1)
                    if not opening:
                        dve.wait_ge(mix_ready, n)
                    dve.tensor_tensor(cbm[:], ps_d[:, 0:P], utri[:], ALU.mult).then_inc(cbm_ready, 1)
                    if c % 2 == 1 and not (last and c == NT - 1):
                        split_gate((c // 2 + 1) % 2, 4 * g + c // 2 + 1)
                    if c == NT - 1 and not last:
                        for k in range(4):
                            split_z(g + 1, k)
                    keys, start = (P, 1) if c == 0 else (2 * P, 0 if j else 1)
                    mask = band[:, start:start + keys // P].rearrange("p b k -> p (b k)").unsqueeze(1)
                    dve.wait_ge(scored, n + 1)
                    if not opening:
                        dve.wait_ge(p_turned, n)
                    for a in range(2):
                        ins = dve.scalar_tensor_tensor(sc[:, 2 * a:2 * a + 2, 0:keys], ps_s[:, a, :, 0:keys], HD ** -0.5,
                                                       mask.to_broadcast([P, 2, keys]), ALU.mult, ALU.add)
                    ins.then_inc(masked, 1)
                    dve.wait_ge(masked, n + 1)
                    do(dve.tensor_reduce(mx[:, 0], sc[:, :, 0:keys], AX, ALU.max))
                    if opening:
                        dve.wait_ge(rows_in, 32)
                    else:
                        dve.wait_ge(sink_done, n)
                    sink = sinks[:, bass.ds(g * REP, REP)]
                    do(dve.tensor_tensor(mx[:, 0], mx[:, 0], sink, ALU.max))
                    own.did(dve.tensor_scalar(negm[:], mx[:, 0], -1.0, None, ALU.mult))
                    dve.tensor_tensor(mx[:, 1], sink, mx[:, 0], ALU.subtract).then_inc(max_ready, 1)
                    heads_of = lambda t: t.rearrange("p (h d) -> p h d", d=HD)
                    if c:
                        dve.wait_ge(off_done, (NT - 1) * g + c)
                        own.did(dve.tensor_tensor(heads_of(y1[:]), heads_of(ps_e[:]), bcast(ea[:, c, heads], HD), ALU.mult))
                    if c == 0:
                        dve.wait_ge(state_done, (NT - 1) * g + 1)
                        dve.tensor_copy(state[:], ps_f[:]).then_inc(state_ready, 1)
                    elif c < NT - 1:
                        do(dve.tensor_tensor(heads_of(kept[:]), heads_of(state[:]), bcast(cdecay[:, c, heads], HD), ALU.mult))
                        dve.wait_ge(state_done, (NT - 1) * g + c + 1)
                        dve.tensor_tensor(state[:], kept[:], ps_f[:], ALU.add).then_inc(state_ready, 1)
                    dve.wait_ge(diag_done, n + 1)
                    dve.wait_ge(xd_ready, n + 1)
                    dve.tensor_tensor(xd[:], ps_d[:], xd[:], ALU.add).then_inc(y2_ready, 1)
                    dve.wait_ge(y2_ready, n + 1)
                    dve.wait_ge(z_used, n + 1)
                    if c:
                        do(dve.tensor_tensor(xd[:], xd[:], y1[:], ALU.add))
                    dve.tensor_tensor(y1[:], xd[:], silu[:], ALU.mult).then_inc(gated, 1)
                    if c == NT - 1 and not last:
                        for k in range(4, KT):
                            split_z(g + 1, k)
                    dve.wait_ge(sink_done, n + 1)
                    do(dve.tensor_tensor(rden[:], sums[:], sink_e[:], ALU.add))
                    do(dve.reciprocal(rden[:], rden[:]))
                    dve.wait_ge(sq_done, n + 1)
                    dve.tensor_scalar(stat[:, 1:2], stat[:, 0:1], 1.0 / GW, EPS, ALU.mult, ALU.add).then_inc(v_ready, 1)
                    dve.wait_ge(r0_ready, n + 1)
                    newton(dve, own, stat[:, 3:4], stat[:, 1:2], stat[:, 4:5], stat[:, 5:6])
                    if not opening:
                        dve.wait_ge(y_turned, n)
                    if c == 0:
                        dve.wait_ge(norm_in, 16 * (g + 1))
                    dve.scalar_tensor_tensor(yn[:], y1[:], stat[:, 5:6], norm_row[:], ALU.mult,
                                             ALU.mult).then_inc(yn_ready, 1)
                assert own.n == OWN

            OWN = 10 * NT + 2 * (NT - 1) + (NT - 2)
            for k in range(KT):
                split_z(0, k)
            split_gate(0, 0)
            group(0, True, False)
            with dve.Fori(1, NG - 1) as g:
                group(g, False, False)
            group(NG - 1, False, True)
            attention_out(NG * NT - 1, False)

        @block.tensor
        def _(pe):
            def gate(g, c, ks, opening):
                j, w = c % 2, (c // 2) % 2
                if ks[0] == 0:
                    pe.wait_ge(g_lo_done, 4 * g + c // 2 + 1)
                    if not opening:
                        pe.wait_ge(gate_out, NT * g + c)
                for k in ks:
                    last = matmul3(pe, ps_g[:], g_hi[:, w, k], g_lo[:, w, k], u_hi[:, k, j * HALF:(j + 1) * HALF],
                                   u_lo[:, k, j * HALF:(j + 1) * HALF], k == 0, k == KT - 1)
                if ks[-1] == KT - 1:
                    last.then_inc(gate_done, 1)

            def z(g, c, ks, opening):
                if ks[0] == 0 and not opening:
                    pe.wait_ge(z_used, NT * g + c)
                for k in ks:
                    if c == 0:
                        pe.wait_ge(z_lo_done, KT * g + k + 1)
                    last = matmul3(pe, ps_z[:], u_hi[:, k, c * P:(c + 1) * P], u_lo[:, k, c * P:(c + 1) * P],
                                   z_hi[:, k], z_lo[:, k], k == 0, k == KT - 1)
                if ks[-1] == KT - 1:
                    last.then_inc(z_done, 1)

            def next_z(g, c, last, ks):
                if c < NT - 1:
                    z(g, c + 1, ks, False)
                elif not last:
                    z(g + 1, 0, ks, False)

            def values(g, c):
                pe.wait_ge(p_ready, NT * g + c + 1)
                j, blocks = c % 2, 1 if c == 0 else 2
                for r in range(REP):
                    for b in range(blocks):
                        block_of = c if b == j else c - 1
                        last = pe.matmul(ps_a[:, r * HD:(r + 1) * HD], p_t[:, r, b], v_in[:, block_of % 4],
                                         start=(b == 0), stop=(b == blocks - 1))
                last.then_inc(pv_done, 1)

            def turn_outputs(g, c, opening):
                n = NT * g + c
                pe.wait_ge(yn_ready, n + 1)
                if not opening:
                    pe.wait_ge(y_out, n)
                for a in range(4):
                    last = pe.transpose(ps_e[:, a * P:(a + 1) * P], yn[:, a * P:(a + 1) * P], ident[:])
                last.then_inc(y_turned, 1)
                pe.wait_ge(o_ready, n + 1)
                if c < NT - 1:
                    pe.wait_ge(state_ready, (NT - 1) * g + c + 1)
                else:
                    pe.wait_ge(o_out, n)
                for a in range(2):
                    last = pe.transpose(ps_f[:, a * P:(a + 1) * P], o_tok[:, a * P:(a + 1) * P], ident[:])
                last.then_inc(o_turned, 1)

            def group(g, first, last_group):
                for c in range(NT):
                    j, n = c % 2, NT * g + c
                    opening = first and c == 0
                    before = (g if c else g - 1, (c - 1) % NT)
                    if not opening:
                        values(*before)
                    gate(g, c, range(0, 4), opening)
                    pe.wait_ge(step_in[j], 16 * LOADS * (4 * g + c // 2 + 1))
                    pe.wait_ge(rotated, n + 1)
                    if not opening:
                        pe.wait_ge(o_ready, n)
                    for a in range(3):
                        two = qr[:, 2 * a:2 * a + 2].rearrange("p a d -> p (a d)")
                        last = pe.transpose(ps_a[:, a * P:(a + 1) * P], two, ident[:])
                    last.then_inc(qk_turned, 1)
                    if not opening:
                        pe.wait_ge(y2_ready, n)
                    pe.matmul(ps_d[:, 0:P], bc_f[:, j, 0], bc_f[:, j, 1], start=True, stop=True).then_inc(cb_done, 1)
                    gate(g, c, range(4, 6), opening)
                    pe.wait_ge(q_ready, n + 1)
                    if not opening:
                        pe.wait_ge(p_ready, n)
                    keys = P if c == 0 else 2 * P
                    for r in range(REP):
                        lo = (r % 2) * HD
                        last = pe.matmul(ps_s[:, r % 2, r // 2, 0:keys], q_t[lo:lo + HD, r // 2],
                                         k_t[lo:lo + HD].rearrange("p b n -> p (b n)")[:, 0:keys], start=True, stop=True)
                    last.then_inc(scored, 1)
                    if not opening:
                        turn_outputs(*before, first and c == 1)
                    gate(g, c, range(6, KT), opening)
                    if c:
                        pe.wait_ge(state_ready, (NT - 1) * g + c)
                        pe.wait_ge(y_out, n)
                        pe.matmul(ps_e[:], bc_f[:, j, 1], state[:], start=True, stop=True).then_inc(off_done, 1)
                    if c < NT - 1:
                        pe.wait_ge(xdec_ready, (NT - 1) * g + c + 1)
                        if not opening:
                            pe.wait_ge(o_out, n)
                        pe.matmul(ps_f[:], b_tok[:, j], xdec[:], start=True, stop=True).then_inc(state_done, 1)
                    pe.wait_ge(mix_ready, n + 1)
                    pe.wait_ge(xdt_ready, n + 1)
                    for h in range(HPG):
                        last = pe.matmul(ps_d[:, h * HD:(h + 1) * HD], seg[:, h], xdt[:, h * HD:(h + 1) * HD], start=True, stop=True)
                    last.then_inc(diag_done, 1)
                    next_z(g, c, last_group, range(0, 3))
                    pe.wait_ge(exp_done, n + 1)
                    for r in range(REP):
                        for b in range(keys // P):
                            last = pe.transpose(ps_s[:, r // 2, r % 2, b * P:(b + 1) * P], sc[:, r, b * P:(b + 1) * P], ident[:])
                    last.then_inc(p_turned, 1)
                    next_z(g, c, last_group, range(3, KT))

            z(0, 0, range(KT), True)
            group(0, True, False)
            with pe.Fori(1, NG - 1) as g:
                group(g, False, False)
            group(NG - 1, False, True)
            values(NG - 1, NT - 1)
            turn_outputs(NG - 1, NT - 1, False)


def merge(nc, A, gate_s, src_s, merged_s, part, ssd):
    NB = 2 if ssd else 1
    NK = NB * KT
    w_name, gate_0 = ("w_ssd_out", 0) if ssd else ("w_attn_out", KT)
    with Stage(nc, "ms" if ssd else "ma") as s:
        w_raw = s.sb("w_raw", [P, 2, KT, P])
        w_hi = s.sb("w_hi", [P, 2, KT, P], F32R)
        w_lo = s.sb("w_lo", [P, 2, KT, P], F32R)
        src = s.sb("src", [P, 2, SEQ])
        s_hi = s.sb("s_hi", [P, NK, SEQ], F32R)
        s_lo = s.sb("s_lo", [P, NK, SEQ], F32R)
        sig = s.sb("sig", [P, 2, SEQ])
        ps = s.ps("ps", [P, 2, SEQ])
        w_in, s_in, sig_in, stored = s.sems("w_in", 2), s.sems("s_in", 2), s.sems("sig_in", 2), s.sems("stored", 2)
        w_hi_done, w_lo_done, s_hi_done, s_lo_done, sig_done, product_done, scaled, out_done, block_used = (
            s.sem(n) for n in "w_hi_done w_lo_done s_hi_done s_lo_done sig_done product_done scaled out_done block_used".split())
        block = s.block()
        BLOCKS = KT * NB

        @block.sync
        def _(sp):
            for q in range(2):
                sp.dma_start(w_raw[:, q], A[w_name][q]).then_inc(w_in[q], 16)
            for k in range(NK):
                if k >= 2:
                    sp.wait_ge(s_lo_done, k - 1)
                sp.dma_start(src[:, k % 2], src_s[k]).then_inc(s_in[k % 2], 16)
            for j in range(2):
                sp.dma_start(sig[:, j], gate_s[gate_0 + j]).then_inc(sig_in[j], 16)

            def pair(i, last):
                for j in range(2):
                    f = 2 * i + j
                    for b in range(NB):
                        q = f * NB + b
                        if not (last and j * NB + b >= 2 * NB - 2):
                            sp.wait_ge(w_lo_done, q + 1)
                            w = (j * NB + b) % 2
                            sp.dma_start(w_raw[:, w], A[w_name][q + 2]).then_inc(w_in[w], 16)
                    if ssd:
                        sp.wait_ge(out_done, f + 1)
                        sp.dma_start(merged_s[f], sig[:, j]).then_inc(stored[j], 16)
                    if not last:
                        if ssd:
                            sp.wait_ge(stored[j], 16 * (i + 1))
                        else:
                            sp.wait_ge(out_done, f + 1)
                        sp.dma_start(sig[:, j], gate_s[f + (2 + gate_0)]).then_inc(sig_in[j], 16)

            with sp.Fori(0, KT // 2 - 1) as i:
                pair(i, False)
            pair(KT // 2 - 1, True)
            if ssd:
                for j in range(2):
                    sp.wait_ge(stored[j], 16 * KT // 2)

        @block.scalar
        def _(act):
            def split_w(q, w, use):
                act.wait_ge(w_in[w], 16 * (use + 1))
                act.activation(w_hi[:, w], w_raw[:, w], ACT.Copy).then_inc(w_hi_done, 1)

            def pair(i, last):
                for j in range(2):
                    f = 2 * i + j
                    act.wait_ge(sig_in[j], 16 * (i + 1))
                    act.activation(sig[:, j], sig[:, j], ACT.Sigmoid).then_inc(sig_done, 1)
                    for b in range(NB):
                        p = j * NB + b
                        if not (last and p >= 2 * NB - 2):
                            act.wait_ge(block_used, 2 * NB * i + p + 1)
                            split_w(None, p % 2, NB * i + (p + 2) // 2)

            for w in range(2):
                split_w(w, w, 0)
            for k in range(NK):
                act.wait_ge(s_in[k % 2], 16 * (k // 2 + 1))
                act.activation(s_hi[:, k], src[:, k % 2], ACT.Copy).then_inc(s_hi_done, 1)
            with act.Fori(0, KT // 2 - 1) as i:
                pair(i, False)
            pair(KT // 2 - 1, True)

        @block.vector
        def _(dve):
            def split_w(q, w):
                dve.wait_ge(w_hi_done, q + 1)
                dve.tensor_tensor(w_lo[:, w], w_raw[:, w], w_hi[:, w].bitcast(F32), ALU.subtract).then_inc(w_lo_done, 1)

            def pair(i, last):
                for j in range(2):
                    f = 2 * i + j
                    for b in range(NB):
                        p = j * NB + b
                        if not (last and p >= 2 * NB - 2):
                            split_w(2 * NB * i + p + 2, p % 2)
                    dve.wait_ge(product_done, f + 1)
                    dve.wait_ge(sig_done, f + 1)
                    mine = part[:, bass.ds(f, 1)].rearrange("p a n -> p (a n)")
                    if ssd:
                        dve.tensor_tensor(sig[:, j], sig[:, j], ps[:, j], ALU.mult).then_inc(scaled, 1)
                        dve.wait_ge(scaled, f + 1)
                        dve.tensor_tensor(sig[:, j], sig[:, j], mine, ALU.add).then_inc(out_done, 1)
                    else:
                        dve.tensor_tensor(mine, sig[:, j], ps[:, j], ALU.mult).then_inc(out_done, 1)

            for w in range(2):
                split_w(w, w)
            for k in range(NK):
                dve.wait_ge(s_hi_done, k + 1)
                dve.tensor_tensor(s_lo[:, k], src[:, k % 2], s_hi[:, k].bitcast(F32), ALU.subtract).then_inc(s_lo_done, 1)
            with dve.Fori(0, KT // 2 - 1) as i:
                pair(i, False)
            pair(KT // 2 - 1, True)

        @block.tensor
        def _(pe):
            def pair(i, first):
                for j in range(2):
                    f = 2 * i + j
                    if not first:
                        pe.wait_ge(out_done, f - 1)
                    for b in range(NB):
                        p = j * NB + b
                        pe.wait_ge(w_lo_done, 2 * NB * i + p + 1)
                        for h in range(2):
                            for k in range(KT):
                                kk = b * KT + k
                                if first and h == 0 and j == 0:
                                    pe.wait_ge(s_lo_done, kk + 1)
                                last = matmul3(pe, ps[:, j, h * HALF:(h + 1) * HALF], w_hi[:, p % 2, k], w_lo[:, p % 2, k],
                                               s_hi[:, kk, h * HALF:(h + 1) * HALF], s_lo[:, kk, h * HALF:(h + 1) * HALF],
                                               kk == 0, kk == NK - 1)
                        last.then_inc(block_used, 1)
                    pe.wait_ge(block_used, 2 * NB * i + (j + 1) * NB)
                    pe.sem_inc(product_done, 1)

            pair(0, True)
            with pe.Fori(1, KT // 2) as i:
                pair(i, False)


def mix_rows(nc, A, merged_s, x2_s, h_hi, h_lo, ident):
    with Stage(nc, "mr") as s:
        src = s.sb("src", [P, 2, SEQ])
        w_raw = s.sb("w_raw", [P, 2, D])
        w_hi = s.sb("w_hi", [P, KT, D], F32R)
        w_lo = s.sb("w_lo", [P, KT, D], F32R)
        post = s.sb("post", [P, D])
        pre = s.sb("pre", [P, D])
        x_t = s.sb("x_t", [P, 2, D])
        y_t = s.sb("y_t", [P, 2, D])
        stat = s.sb("stat", [P, 2, NT, 6])
        ps = s.ps("ps", [P, 2, D])
        ps_t = s.ps("ps_t", [P, KT, P])
        rows_in, s_in, w_in, x_in, stored = s.sem("rows_in"), s.sems("s_in", 2), s.sems("w_in", 2), s.sems("x_in", 2), s.sems("stored", 2)
        s_hi_done, s_lo_done, w_hi_done, w_lo_done, product_done, sq_done, v_ready, r0_ready, y_ready, x2_ready, h_ready, turned, h_hi_done, h_lo_done, act_own, dve_own = (
            s.sem(n) for n in ("s_hi_done s_lo_done w_hi_done w_lo_done product_done sq_done v_ready r0_ready y_ready "
                               "x2_ready h_ready turned h_hi_done h_lo_done act_own dve_own").split())
        block = s.block()
        x_tiles = A["x"].rearrange("(t p) d -> t p d", p=P)

        @block.sync
        def _(sp):
            for k in range(KT):
                if k >= 2:
                    sp.wait_ge(s_lo_done, k - 1)
                    sp.wait_ge(w_lo_done, k - 1)
                sp.dma_start(src[:, k % 2], merged_s[k]).then_inc(s_in[k % 2], 16)
                sp.dma_start(w_raw[:, k % 2], A["w_mix"][:, k]).then_inc(w_in[k % 2], 16)
            sp.dma_start(post[:], A["mix_post_row"].partition_broadcast(P)).then_inc(rows_in, 16)
            sp.dma_start(pre[:], A["ffn_pre_row"].partition_broadcast(P)).then_inc(rows_in, 16)
            for t in range(NT):
                if t >= 2:
                    sp.wait_ge(stored[t % 2], 16 * (t // 2))
                    sp.wait_ge(h_ready, t - 1)
                sp.dma_start(x_t[:, t % 2], x_tiles[t]).then_inc(x_in[t % 2], 16)

        @block.gpsimd
        def _(pool):
            for t in range(NT):
                pool.wait_ge(x2_ready, t + 1)
                pool.dma_start(x2_s[t], x_t[:, t % 2]).then_inc(stored[t % 2], 16)
            for j in range(2):
                pool.wait_ge(stored[j], 16 * NT // 2)

        @block.scalar
        def _(act):
            def rstd(t, n, src_ap, junk):
                act.activation(junk, src_ap, ACT.Square, accum_out=stat[:, n, t, 0:1]).then_inc(sq_done, 1)
                act.wait_ge(v_ready, 2 * t + n + 1)
                act.activation(stat[:, n, t, 2:3], stat[:, n, t, 1:2], ACT.Ln).then_inc(act_own, 1)
                act.wait_ge(act_own, 2 * t + n + 1)
                act.activation(stat[:, n, t, 3:4], stat[:, n, t, 2:3], ACT.Exp, scale=-0.5).then_inc(r0_ready, 1)

            act.preload_act_table_set("natural_log_exp_and_others")
            for k in range(KT):
                act.wait_ge(s_in[k % 2], 16 * (k // 2 + 1))
                act.activation(h_hi[:, k], src[:, k % 2], ACT.Copy).then_inc(s_hi_done, 1)
                act.wait_ge(w_in[k % 2], 16 * (k // 2 + 1))
                act.activation(w_hi[:, k], w_raw[:, k % 2], ACT.Copy).then_inc(w_hi_done, 1)
            for t in range(NT):
                j = t % 2
                act.wait_ge(product_done, t + 1)
                if t >= 2:
                    act.wait_ge(turned, t - 1)
                rstd(t, 0, ps[:, j], y_t[:, j])
                act.wait_ge(x2_ready, t + 1)
                rstd(t, 1, x_t[:, j], y_t[:, j])
                act.wait_ge(turned, t + 1)
                act.activation(h_hi[:, :, t * P:(t + 1) * P], ps_t[:], ACT.Copy).then_inc(h_hi_done, 1)

        @block.vector
        def _(dve):
            own = Chain(dve, dve_own)

            def rstd(t, n):
                dve.wait_ge(sq_done, 2 * t + n + 1)
                dve.tensor_scalar(stat[:, n, t, 1:2], stat[:, n, t, 0:1], 1.0 / D, EPS, ALU.mult, ALU.add).then_inc(v_ready, 1)
                dve.wait_ge(r0_ready, 2 * t + n + 1)
                newton(dve, own, stat[:, n, t, 3:4], stat[:, n, t, 1:2], stat[:, n, t, 4:5], stat[:, n, t, 5:6])

            for k in range(KT):
                dve.wait_ge(s_hi_done, k + 1)
                dve.tensor_tensor(h_lo[:, k], src[:, k % 2], h_hi[:, k].bitcast(F32), ALU.subtract).then_inc(s_lo_done, 1)
                dve.wait_ge(w_hi_done, k + 1)
                dve.tensor_tensor(w_lo[:, k], w_raw[:, k % 2], w_hi[:, k].bitcast(F32), ALU.subtract).then_inc(w_lo_done, 1)
            dve.wait_ge(rows_in, 32)
            for t in range(NT):
                j = t % 2
                rstd(t, 0)
                dve.scalar_tensor_tensor(y_t[:, j], ps[:, j], stat[:, 0, t, 5:6], post[:], ALU.mult, ALU.mult).then_inc(y_ready, 1)
                dve.wait_ge(y_ready, t + 1)
                dve.wait_ge(x_in[j], 16 * (t // 2 + 1))
                dve.tensor_tensor(x_t[:, j], x_t[:, j], y_t[:, j], ALU.add).then_inc(x2_ready, 1)
                rstd(t, 1)
                dve.scalar_tensor_tensor(y_t[:, j], x_t[:, j], stat[:, 1, t, 5:6], pre[:], ALU.mult, ALU.mult).then_inc(h_ready, 1)
                dve.wait_ge(h_hi_done, t + 1)
                dve.tensor_tensor(h_lo[:, :, t * P:(t + 1) * P], ps_t[:], h_hi[:, :, t * P:(t + 1) * P].bitcast(F32),
                                  ALU.subtract).then_inc(h_lo_done, 1)

        @block.tensor
        def _(pe):
            def turn(t):
                pe.wait_ge(h_ready, t + 1)
                if t:
                    pe.wait_ge(h_lo_done, t)
                for k in range(KT):
                    last = pe.transpose(ps_t[:, k], y_t[:, t % 2, k * P:(k + 1) * P], ident[:])
                last.then_inc(turned, 1)

            for t in range(NT):
                if t >= 2:
                    pe.wait_ge(y_ready, t - 1)
                for k in range(KT):
                    if t == 0:
                        pe.wait_ge(s_lo_done, k + 1)
                        pe.wait_ge(w_lo_done, k + 1)
                    for h in range(2):
                        last = matmul3(pe, ps[:, t % 2, h * HALF:(h + 1) * HALF], h_hi[:, k, t * P:(t + 1) * P],
                                       h_lo[:, k, t * P:(t + 1) * P], w_hi[:, k, h * HALF:(h + 1) * HALF],
                                       w_lo[:, k, h * HALF:(h + 1) * HALF], k == 0, k == KT - 1)
                last.then_inc(product_done, 1)
                if t:
                    turn(t - 1)
            turn(NT - 1)


def ffn_up(nc, A, ff, h_hi, h_lo):
    TAPS = 3
    with Stage(nc, "fu") as s:
        cw = s.sb("cw", [P, FT, 2, TAPS + 1])
        w_raw = s.sb("w_raw", [P, 2, KT, P])
        w_hi = s.sb("w_hi", [P, 2, KT, P], F32R)
        w_lo = s.sb("w_lo", [P, 2, KT, P], F32R)
        xc = s.sb("xc", [P, 2, SEQ])
        ps = s.ps("ps", [P, 2, SEQ])
        cw_in, w_in = s.sem("cw_in"), s.sems("w_in", 2)
        hi_done, lo_done, product_done, tap_done, dve_own, conv_done, gelu_done, ff_done = (
            s.sem(n) for n in "hi_done lo_done product_done tap_done dve_own conv_done gelu_done ff_done".split())
        block = s.block()

        @block.sync
        def _(sp):
            sp.dma_start(cw[:], A["ffn_conv"]).then_inc(cw_in, 16)
            for j in range(2):
                sp.dma_start(w_raw[:, j], A["w_up"][j]).then_inc(w_in[j], 16)
            with sp.Fori(0, FT - 1) as i:
                for j in range(2):
                    sp.wait_ge(lo_done, 2 * i + j + 1)
                    sp.dma_start(w_raw[:, j], A["w_up"][2 * i + (j + 2)]).then_inc(w_in[j], 16)

        @block.scalar
        def _(act):
            def split(i, j):
                act.wait_ge(w_in[j], 16 * (i + 1))
                act.activation(w_hi[:, j], w_raw[:, j], ACT.Copy).then_inc(hi_done, 1)

            def pair(i, first, last):
                for j in range(2):
                    act.wait_ge(product_done, 2 * i + j + 1)
                    if j == 0 and not first:
                        act.wait_ge(ff_done, i)
                    act.activation(xc[:, j], ps[:, j], ACT.Identity, scale=cw[:, bass.ds(i, 1), j, TAPS - 1],
                                   bias=cw[:, bass.ds(i, 1), j, TAPS]).then_inc(tap_done, 1)
                    if not last:
                        split(i + 1, j)
                    if j == 0:
                        act.wait_ge(conv_done, 2 * i + 1)
                        act.activation(xc[:, 0], xc[:, 0], ACT.Gelu_apprx_tanh).then_inc(gelu_done, 1)

            for j in range(2):
                split(0, j)
            act.wait_ge(cw_in, 16)
            pair(0, True, False)
            with act.Fori(1, FT - 1) as i:
                pair(i, False, False)
            pair(FT - 1, False, True)

        @block.vector
        def _(dve):
            def split(i, j):
                dve.wait_ge(hi_done, 2 * i + j + 1)
                dve.tensor_tensor(w_lo[:, j], w_raw[:, j], w_hi[:, j].bitcast(F32), ALU.subtract).then_inc(lo_done, 1)

            def pair(i, last):
                for j in range(2):
                    f = 2 * i + j
                    dve.wait_ge(tap_done, f + 1)
                    dve.scalar_tensor_tensor(xc[:, j, 1:SEQ], ps[:, j, 0:SEQ - 1], cw[:, bass.ds(i, 1), j, 1],
                                             xc[:, j, 1:SEQ], ALU.mult, ALU.add).then_inc(dve_own, 1)
                    dve.wait_ge(dve_own, f + 1)
                    dve.scalar_tensor_tensor(xc[:, j, 2:SEQ], ps[:, j, 0:SEQ - 2], cw[:, bass.ds(i, 1), j, 0],
                                             xc[:, j, 2:SEQ], ALU.mult, ALU.add).then_inc(conv_done, 1)
                    if not last:
                        split(i + 1, j)
                dve.wait_ge(gelu_done, i + 1)
                dve.wait_ge(conv_done, 2 * i + 2)
                dve.tensor_tensor(ff[:, bass.ds(i, 1)].rearrange("p a n -> p (a n)"), xc[:, 0], xc[:, 1],
                                  ALU.mult).then_inc(ff_done, 1)

            for j in range(2):
                split(0, j)
            dve.wait_ge(cw_in, 16)
            with dve.Fori(0, FT - 1) as i:
                pair(i, False)
            pair(FT - 1, True)

        @block.tensor
        def _(pe):
            def pair(i, first):
                for j in range(2):
                    f = 2 * i + j
                    pe.wait_ge(lo_done, f + 1)
                    if not first:
                        pe.wait_ge(conv_done, f - 1)
                    for h in range(2):
                        for k in range(KT):
                            last = matmul3(pe, ps[:, j, h * HALF:(h + 1) * HALF], w_hi[:, j, k], w_lo[:, j, k],
                                           h_hi[:, k, h * HALF:(h + 1) * HALF], h_lo[:, k, h * HALF:(h + 1) * HALF],
                                           k == 0, k == KT - 1)
                    last.then_inc(product_done, 1)

            pair(0, True)
            with pe.Fori(1, FT) as i:
                pair(i, False)


def ffn_down(nc, A, ff, x2_s, out, ident):
    BLK = ((0, 6), (6, 6), (12, 5), (17, 5))
    NBK = len(BLK)
    WK = max(n for _, n in BLK)
    PB = 2 * NBK
    PAIRS = KT // 2
    TH = NT // 2
    with Stage(nc, "fd") as s:
        w_raw = s.sb("w_raw", [P, 2, WK, P])
        w_hi = s.sb("w_hi", [P, 2, WK, P], F32R)
        w_lo = s.sb("w_lo", [P, 2, WK, P], F32R)
        s_hi = s.sb("s_hi", [P, FT, HALF], F32R)
        s_lo = s.sb("s_lo", [P, FT, HALF], F32R)
        d_f = s.sb("d_f", [P, 2, HALF])
        post = s.sb("post", [P, D])
        ssq = s.sb("ssq", [P, 2, TH, KT])
        v, r0, tmp, r = (s.sb(n, [P, 2, TH]) for n in ("v", "r0", "tmp", "r"))
        ps = s.ps("ps", [P, 2, HALF])
        ps_t = s.ps("ps_t", [P, 2, TH, P])
        junk = s.ps("junk", [P, HALF])
        row_in, w_in, x2_in, late_in = s.sem("row_in"), s.sems("w_in", 2), s.sem("x2_in"), s.sem("late_in")
        stored, late_stored = s.sem("stored"), s.sem("late_stored")
        w_hi_done, w_lo_done, block_used, s_hi_done, s_lo_done, product_done, f_out, turned, t_out = (
            s.sem(n) for n in "w_hi_done w_lo_done block_used s_hi_done s_lo_done product_done f_out turned t_out".split())
        sq_done, v_ready, ln_done, r0_ready, out_ready, dve_own = (
            s.sem(n) for n in "sq_done v_ready ln_done r0_ready out_ready dve_own".split())
        block = s.block()
        out_tiles = out.rearrange("(t p) d -> t p d", p=P)

        def ahead(j, b):
            p = j * NBK + b + 2
            return p // NBK - j, p % NBK

        def ff_of(h, k):
            return ff[:, k, h * HALF:(h + 1) * HALF]

        def product(h, t):
            return ff[:, h * KT:(h + 1) * KT, t * P:(t + 1) * P].rearrange("p (a b) c -> p a b c", a=2)

        def residual(h, t):
            if h:
                return product(0, t)
            k = 2 * KT + 2 * t if t < 3 else KT
            return ff[:, k:k + 2, 0:HALF].rearrange("p a (b c) -> p a b c", b=4)

        def row_tile(ap):
            return ap.rearrange("p (a b c) -> p a b c", a=2, b=4)

        @block.sync
        def _(sp):
            def load_w(f, b, slot):
                k0, n = BLK[b]
                sp.dma_start(w_raw[:, slot, 0:n], A["w_down"][f, :, k0:k0 + n]).then_inc(w_in[slot], 16)

            def pair(h, i, last):
                for j in range(2):
                    for b in range(NBK):
                        p = j * NBK + b
                        more, nb = ahead(j, b)
                        if last and j + more == 2:
                            if h == 0:
                                sp.wait_ge(w_lo_done, PB * (h * PAIRS + i) + p + 1)
                                load_w(0, nb, p % 2)
                        else:
                            sp.wait_ge(w_lo_done, PB * (h * PAIRS + i) + p + 1)
                            load_w(2 * i + (j + more), nb, p % 2)

            for b in range(2):
                load_w(0, b, b)
            sp.dma_start(post[:], A["ffn_post_row"].partition_broadcast(P)).then_inc(row_in, 16)
            for h in range(2):
                with sp.Fori(0, PAIRS - 1) as i:
                    pair(h, i, False)
                pair(h, PAIRS - 1, True)
            for t in range(TH):
                sp.wait_ge(out_ready, TH + t + 1)
                sp.dma_start(row_tile(out_tiles[TH + t]), product(1, t)).then_inc(late_stored, 16)
            sp.wait_ge(late_stored, 16 * TH)

        @block.gpsimd
        def _(pool):
            pool.wait_ge(s_lo_done, FT)
            for t in range(TH):
                pool.dma_start(residual(0, t), row_tile(x2_s[t])).then_inc(x2_in, 16)
            for t in range(TH):
                pool.wait_ge(out_ready, t + 1)
                pool.dma_start(row_tile(out_tiles[t]), product(0, t)).then_inc(stored, 16)
            pool.wait_ge(stored, 16 * TH)
            for t in range(TH):
                pool.dma_start(residual(1, t), row_tile(x2_s[TH + t])).then_inc(late_in, 16)

        @block.scalar
        def _(act):
            def split_w(use, slot, b):
                n = BLK[b][1]
                act.wait_ge(w_in[slot], 16 * (use + 1))
                act.activation(w_hi[:, slot, 0:n], w_raw[:, slot, 0:n], ACT.Copy).then_inc(w_hi_done, 1)

            def split_s(h, k):
                act.activation(s_hi[:, k], ff_of(h, k), ACT.Copy).then_inc(s_hi_done, 1)

            def squares(h, f, j):
                act.wait_ge(t_out, h * KT + f + 1)
                for t in range(TH):
                    ins = act.activation(junk[:, t * P:(t + 1) * P], ps_t[:, j, t], ACT.Square,
                                         accum_out=ssq[:, h, t, bass.ds(f, 1)])
                ins.then_inc(sq_done, 1)

            def pair(h, i, first, last):
                for j in range(2):
                    f = h * KT + 2 * i + j
                    for b in range(NBK):
                        p = j * NBK + b
                        if not (h == 1 and last and p >= PB - 2):
                            act.wait_ge(block_used, PB * (h * PAIRS + i) + p + 1)
                            split_w(NBK * (h * PAIRS + i) + (p + 2) // 2, p % 2, ahead(j, b)[1])
                        if h == 0 and last and j == 1:
                            for k in range(BLK[b][0], BLK[b][0] + BLK[b][1]):
                                split_s(1, k)
                        if b == 1 and not (first and j == 0):
                            squares(h, 2 * i + j - 1, 1 - j)
                        if b == 1 and h == 1 and first and j == 0:
                            squares(0, KT - 1, 1)
                            root(0)
                    act.wait_ge(product_done, f + 1)
                    if not (h == 0 and first and j == 0):
                        act.wait_ge(turned, f)
                    act.activation(d_f[:, j], ps[:, j], ACT.Copy).then_inc(f_out, 1)

            def root(h):
                act.wait_ge(v_ready, h + 1)
                act.activation(tmp[:, h], v[:, h], ACT.Ln).then_inc(ln_done, 1)
                act.wait_ge(ln_done, h + 1)
                act.activation(r0[:, h], tmp[:, h], ACT.Exp, scale=-0.5).then_inc(r0_ready, 1)

            act.preload_act_table_set("natural_log_exp_and_others")
            for k in range(FT):
                if k in (3, 6):
                    split_w(0, k // 3 - 1, k // 3 - 1)
                split_s(0, k)
            pair(0, 0, True, False)
            with act.Fori(1, PAIRS - 1) as i:
                pair(0, i, False, False)
            pair(0, PAIRS - 1, False, True)
            pair(1, 0, True, False)
            with act.Fori(1, PAIRS - 1) as i:
                pair(1, i, False, False)
            pair(1, PAIRS - 1, False, True)
            squares(1, KT - 1, 1)
            root(1)

        @block.vector
        def _(dve):
            own = Chain(dve, dve_own)

            def do(ins):
                own.did(ins)
                own.wait()

            def split_w(q, slot, b):
                n = BLK[b][1]
                dve.wait_ge(w_hi_done, q + 1)
                dve.tensor_tensor(w_lo[:, slot, 0:n], w_raw[:, slot, 0:n], w_hi[:, slot, 0:n].bitcast(F32),
                                  ALU.subtract).then_inc(w_lo_done, 1)

            def split_s(h, k):
                dve.wait_ge(s_hi_done, h * FT + k + 1)
                dve.tensor_tensor(s_lo[:, k], ff_of(h, k), s_hi[:, k].bitcast(F32),
                                  ALU.subtract).then_inc(s_lo_done, 1)

            def to_tokens(h, f, j):
                dve.wait_ge(turned, h * KT + f + 1)
                if h:
                    dve.wait_ge(out_ready, TH)
                place = ff[:, bass.ds(h * KT + f, 1), 0:HALF].rearrange("p a (t c) -> p (a t) c", c=P)
                dve.tensor_tensor(place, ps_t[:, j], post[:, bass.ds(f * P, P)].unsqueeze(1).to_broadcast([P, TH, P]),
                                  ALU.mult).then_inc(t_out, 1)

            def pair(h, i, first, last):
                for j in range(2):
                    for b in range(NBK):
                        p = j * NBK + b
                        if not (h == 1 and last and p >= PB - 2):
                            split_w(PB * (h * PAIRS + i) + p + 2, p % 2, ahead(j, b)[1])
                        if h == 0 and last and j == 1:
                            for k in range(BLK[b][0], BLK[b][0] + BLK[b][1]):
                                split_s(1, k)
                        if b == 1 and not (first and j == 0):
                            to_tokens(h, 2 * i + j - 1, 1 - j)
                        if b == 1 and h == 1 and first and j == 0:
                            to_tokens(0, KT - 1, 1)
                            rstd(0)
                        if b >= 2 and h == 1 and first and j == 0:
                            dve.wait_ge(x2_in, 16 * TH)
                            for t in range(2 * b - 4, 2 * b - 2):
                                output(0, t)

            def rstd(h):
                dve.wait_ge(sq_done, KT * (h + 1))
                do(dve.tensor_reduce(v[:, h], ssq[:, h], AX, ALU.add))
                dve.tensor_scalar(v[:, h], v[:, h], 1.0 / D, EPS, ALU.mult, ALU.add).then_inc(v_ready, 1)
                dve.wait_ge(r0_ready, h + 1)
                do(dve.tensor_tensor(tmp[:, h], r0[:, h], r0[:, h], ALU.mult))
                do(dve.tensor_tensor(tmp[:, h], tmp[:, h], v[:, h], ALU.mult))
                do(dve.tensor_scalar(tmp[:, h], tmp[:, h], -0.5, 1.5, ALU.mult, ALU.add))
                do(dve.tensor_tensor(r[:, h], r0[:, h], tmp[:, h], ALU.mult))

            def output(h, t):
                dve.scalar_tensor_tensor(product(h, t), product(h, t), r[:, h, t:t + 1], residual(h, t), ALU.mult,
                                         ALU.add).then_inc(out_ready, 1)

            for k in range(FT):
                if k in (3, 6):
                    split_w(k // 3 - 1, k // 3 - 1, k // 3 - 1)
                split_s(0, k)
            dve.wait_ge(row_in, 16)
            pair(0, 0, True, False)
            with dve.Fori(1, PAIRS - 1) as i:
                pair(0, i, False, False)
            pair(0, PAIRS - 1, False, True)
            pair(1, 0, True, False)
            with dve.Fori(1, PAIRS - 1) as i:
                pair(1, i, False, False)
            pair(1, PAIRS - 1, False, True)
            to_tokens(1, KT - 1, 1)
            rstd(1)
            dve.wait_ge(late_in, 16 * TH)
            for t in range(TH):
                dve.wait_ge(t_out, 2 * KT)
                output(1, t)

        @block.tensor
        def _(pe):
            def turn(f, j):
                pe.wait_ge(f_out, f + 1)
                for t in range(TH):
                    last = pe.transpose(ps_t[:, j, t], d_f[:, j, t * P:(t + 1) * P], ident[:])
                last.then_inc(turned, 1)

            def pair(h, i, first):
                for j in range(2):
                    f = h * KT + 2 * i + j
                    if not (first and h == 0):
                        pe.wait_ge(f_out, f - 1)
                        pe.wait_ge(t_out, f - 1)
                        pe.wait_ge(sq_done, f - 1)
                    for b, (k0, n) in enumerate(BLK):
                        p = j * NBK + b
                        pe.wait_ge(w_lo_done, PB * (h * PAIRS + i) + p + 1)
                        for k in range(k0, k0 + n):
                            if first and j == 0:
                                pe.wait_ge(s_lo_done, h * FT + k + 1)
                            last = matmul3(pe, ps[:, j], w_hi[:, p % 2, k - k0], w_lo[:, p % 2, k - k0], s_hi[:, k],
                                           s_lo[:, k], k == 0, k == FT - 1)
                        last.then_inc(block_used, 1)
                        if b == 0 and not (h == 0 and first and j == 0):
                            turn(f - 1, 1 - j)
                    pe.wait_ge(block_used, PB * (h * PAIRS + i) + (j + 1) * NBK)
                    pe.sem_inc(product_done, 1)

            for h in range(2):
                pair(h, 0, True)
                with pe.Fori(1, PAIRS) as i:
                    pair(h, i, False)
            turn(2 * KT - 1, 1)


def lay_out(x, positions, norm_mix_pre_w, w_in, ssd_conv_w, ssd_conv_b, ssd_dt_bias, ssd_a_log, ssd_d,
            ssd_norm_w, ssd_w_out, attn_sinks, attn_w_out, w_mix_out, norm_mix_post_w,
            norm_ffn_pre_w, ffn_w_up, ffn_conv_w, ffn_conv_b, ffn_w_down, norm_ffn_post_w):
    import numpy as np

    def tiles(w, width):
        k, n = w.shape
        return np.ascontiguousarray(w.reshape(k // P, P, n // width, width).transpose(2, 1, 0, 3))

    def columns(*rows):
        return np.ascontiguousarray(np.stack([r.reshape(-1, P).T for r in rows], axis=2))

    w = w_in[0]
    xbc_0, rows_0, gate_0 = INNER, INNER + CONV_DIM, INNER + CONV_DIM + ROWS
    w_ssd = ssd_w_out[0]
    w_up = ffn_w_up[0].reshape(D, 2, FT, P).transpose(0, 2, 1, 3).reshape(D, 2 * FF)
    conv = [r.reshape(2, FT, P) for r in (*ffn_conv_w[0], ffn_conv_b[0])]
    head_order = [(h % 2) * 2 + h // 2 for h in range(REP)]
    freq = (10000.0 ** (-np.arange(HD // 2, dtype=np.float32) * 2.0 / HD)).astype(np.float32)
    return {
        "x": x[0],
        "pos": np.ascontiguousarray(positions[0].reshape(NT, P).T),
        "mix_pre_row": norm_mix_pre_w[0],
        "w_rows": tiles(w[:, rows_0:gate_0], RW),
        "w_xbc": tiles(w[:, xbc_0:rows_0], P),
        "w_z": tiles(w[:, 0:INNER], GW),
        "w_gate": tiles(w[:, gate_0:], P),
        "ssd_conv": columns(*ssd_conv_w[0], ssd_conv_b[0]),
        "dt_bias_row": ssd_dt_bias[0],
        "a_log_row": ssd_a_log[0],
        "d_row": ssd_d[0],
        "freq_row": freq,
        "ssd_norm_row": ssd_norm_w[0],
        "w_ssd_out": np.ascontiguousarray(w_ssd.reshape(2, KT, P, KT, P).transpose(3, 0, 2, 1, 4)).reshape(2 * KT, P, KT, P),
        "sink_row": np.ascontiguousarray(attn_sinks[0].reshape(NG, REP)[:, head_order]).reshape(-1),
        "w_attn_out": tiles(attn_w_out[0], P),
        "w_mix": np.ascontiguousarray(w_mix_out[0].reshape(KT, P, D).transpose(1, 0, 2)),
        "mix_post_row": norm_mix_post_w[0],
        "ffn_pre_row": norm_ffn_pre_w[0],
        "w_up": tiles(w_up, P),
        "ffn_conv": np.ascontiguousarray(np.stack(conv, axis=3).transpose(2, 1, 0, 3)),
        "w_down": tiles(ffn_w_down[0], P),
        "ffn_post_row": norm_ffn_post_w[0],
    }


def kernel(**inputs):
    import numpy as np
    import concourse.bacc as bacc
    from concourse.bass_utils import run_bass_kernel_spmd

    arrays = lay_out(**{k: np.asarray(v) for k, v in inputs.items()})
    arrays = {f"in_{k}": np.ascontiguousarray(v) for k, v in arrays.items()}
    nc = bacc.Bacc("TRN2", target_bir_lowering=False, num_devices=1)
    aps = {k[3:]: nc.dram_tensor(k, v.shape, mybir.dt.from_np(v.dtype), kind="ExternalInput").ap()
           for k, v in arrays.items()}
    out = nc.dram_tensor("out", (SEQ, D), F32, kind="ExternalOutput").ap()
    hybrid_block_kernel(nc, aps, out)
    got = run_bass_kernel_spmd(nc, [arrays], core_ids=[0])
    return got.results[0]["out"].reshape(1, SEQ, D)
```

```python
from contextlib import ExitStack

import concourse.bass as bass
from concourse import mybir

P = 128
SEQ = 1024
D = 1024
KT = D // P
NT = SEQ // P
HALF = 512
INNER = 2048
NH = 32
NG = 4
HPG = NH // NG
HD = 64
GW = HPG * HD
CONV_DIM = INNER + 2 * NG * P
XT = CONV_DIM // P
AH = 16
REP = AH // NG
ROWS = NH + D + 2 * NG * HD
RC = 4
RW = ROWS // RC
Q0 = NH
K0 = Q0 + D
V0 = K0 + NG * HD
FF = 2816
FT = FF // P
EPS = 1e-6
NEG = -1.0e30
MAGIC = 1.5 * 2.0 ** 23
FAR = 4096.0

F32 = mybir.dt.float32
F32R = mybir.dt.float32r
I32 = mybir.dt.int32
ALU = mybir.AluOpType
ACT = mybir.ActivationFunctionType
AX = mybir.AxisListType.X


def turn_parts(count):
    digits = 314159265358979323846264338327950288419716939937510582097494459230781640628620899
    rest = 2 * digits * 2 ** 400 // 10 ** (len(str(digits)) - 1)
    parts = []
    for _ in range(count):
        shift = rest.bit_length() - 7
        top = rest >> shift
        parts.append(float(top) * 2.0 ** (shift - 400))
        rest -= top << shift
    return parts


TURN = turn_parts(9)


def hybrid_block_kernel(nc, A, out):
    def scratch(name, shape):
        return nc.dram_tensor(name, shape, F32, kind="Internal").ap()

    rows_s = scratch("rows_s", (NT, P, ROWS))
    acs_s = scratch("acs_s", (NT * NH, P))
    feat_s = scratch("feat_s", (2 * NG, P, SEQ))
    tok_s = scratch("tok_s", (NT, P, CONV_DIM))
    gate_s = scratch("gate_s", (2 * KT, P, SEQ))
    o_s = scratch("o_s", (KT, P, SEQ))
    y_s = scratch("y_s", (2 * KT, P, SEQ))
    x2_s = scratch("x2_s", (NT, P, D))

    with ExitStack() as whole:
        def hold(ctx, name, shape, dt=F32):
            return ctx.enter_context(nc.sbuf_tensor(name, shape, dt))

        ident = hold(whole, "ident", [P, P])
        consts_done = whole.enter_context(nc.semaphore("consts_done"))

        with ExitStack() as early:
            utri = hold(early, "utri", [P, P])
            band = hold(early, "band", [P, 3, P])
            ones = hold(early, "ones", [P, P])
            u_hi = hold(early, "u_hi", [P, KT, SEQ], F32R)
            u_lo = hold(early, "u_lo", [P, KT, SEQ], F32R)
            dt_v = hold(early, "dt_v", [P, NT, NH])
            acs = hold(early, "acs", [P, NT, NH])
            ea = hold(early, "ea", [P, NT, NH])
            decay = hold(early, "decay", [P, NT, NH])
            cdecay = hold(early, "cdecay", [P, NT, NH])
            cos_t = hold(early, "cos_t", [P, NT, HD // 2])
            sin_t = hold(early, "sin_t", [P, NT, HD // 2])
            projection_rows(nc, A, rows_s, ident, utri, band, ones, consts_done, u_hi, u_lo)
            conv_features(nc, A, rows_s, acs_s, feat_s, tok_s, ident, utri, ones, u_hi, u_lo,
                          dt_v, acs, ea, decay, cdecay, cos_t, sin_t)
            mixers(nc, A, rows_s, acs_s, feat_s, tok_s, gate_s, o_s, y_s, ident, utri, band, u_hi, u_lo,
                   dt_v, acs, ea, decay, cdecay, cos_t, sin_t)
        with ExitStack() as late:
            with nc.sbuf_tensor("merged", [P, KT, SEQ], F32, side="right") as merged:
                merge(nc, A, gate_s, o_s, y_s, merged)
                h_hi = hold(late, "h_hi", [P, KT, SEQ], F32R)
                h_lo = hold(late, "h_lo", [P, KT, SEQ], F32R)
                mix_rows(nc, A, merged, x2_s, h_hi, h_lo, ident)
            ff = whole.enter_context(nc.sbuf_tensor("ff", [P, FT, SEQ], F32, side="right"))
            ffn_up(nc, A, ff, h_hi, h_lo)
        ffn_down(nc, A, ff, x2_s, out, ident)


class Stage:

    def __init__(self, nc, tag):
        self.nc, self.tag, self.ctx, self.used = nc, tag, ExitStack(), []

    def __enter__(self):
        self.ctx.__enter__()
        return self

    def __exit__(self, *a):
        self.ctx.__exit__(*a)
        self.nc.clear_and_free_semaphores(self.used)
        self.nc.all_engine_barrier()

    def sb(self, name, shape, dt=F32):
        return self.ctx.enter_context(self.nc.sbuf_tensor(f"{self.tag}_{name}", shape, dt))

    def ps(self, name, shape):
        return self.ctx.enter_context(self.nc.psum_tensor(f"{self.tag}_{name}", shape, F32))

    def sem(self, name):
        self.used.append(self.nc.alloc_semaphore(name=f"{self.tag}_{name}"))
        return self.used[-1]

    def sems(self, name, n):
        return [self.sem(f"{name}{i}") for i in range(n)]

    def block(self):
        return self.ctx.enter_context(self.nc.Block())


class Chain:

    def __init__(self, eng, sem, base=0):
        self.eng, self.sem, self.n, self.base = eng, sem, 0, base

    def did(self, ins):
        ins.then_inc(self.sem, 1)
        self.n += 1
        return self.n

    def wait(self, n=None):
        self.eng.wait_ge(self.sem, self.base + (self.n if n is None else n))


def matmul3(pe, dst, s_hi, s_lo, m_hi, m_lo, first, last):
    pe.matmul(dst, s_hi, m_hi, start=first, stop=False)
    pe.matmul(dst, s_hi, m_lo, start=False, stop=False)
    return pe.matmul(dst, s_lo, m_hi, start=False, stop=last)


def bcast(ap, n):
    return ap.unsqueeze(2).to_broadcast([ap.shape[0], ap.shape[1], n])


def projection_rows(nc, A, rows_s, ident, utri, band, ones, consts_done, u_hi, u_lo):
    with Stage(nc, "pr") as s:
        x_t = s.sb("x_t", [P, 2, D])
        sq = s.sb("sq", [P, D])
        w_row = s.sb("w_row", [P, D])
        stat = s.sb("stat", [P, NT, 6])
        w_raw = s.sb("w_raw", [P, 2, KT // 2, RW])
        w_hi = s.sb("w_hi", [P, RC, KT, RW], F32R)
        w_lo = s.sb("w_lo", [P, RC, KT, RW], F32R)
        o_t = s.sb("o_t", [P, RC, RW])
        ps_t = s.ps("ps_t", [P, KT, P])
        ps_o = s.ps("ps_o", [P, RC, HALF])
        x_in = s.sems("x_in", 2)
        row_in, sq_done, v_ready, r0_ready, xn_ready = (s.sem(n) for n in "row_in sq_done v_ready r0_ready xn_ready".split())
        act_own, dve_own = s.sem("act_own"), s.sem("dve_own")
        w_in = s.sems("w_in", 2)
        w_hi_done, w_lo_done, t_done, u_hi_done, u_lo_done = (s.sem(n) for n in "w_hi_done w_lo_done t_done u_hi_done u_lo_done".split())
        rows_done, rows_out = s.sem("rows_done"), s.sem("rows_out")
        stored = s.sems("stored", RC)
        block = s.block()
        x_tiles = A["x"].rearrange("(t p) d -> t p d", p=P)

        @block.sync
        def _(sp):
            for t in range(2):
                sp.dma_start(x_t[:, t], x_tiles[t]).then_inc(x_in[t], 16)
            sp.dma_start(w_row[:], A["mix_pre_row"].partition_broadcast(P)).then_inc(row_in, 16)
            for h in range(2 * RC):
                if h >= 2:
                    sp.wait_ge(w_lo_done, h - 1)
                sp.dma_start(w_raw[:, h % 2], A["w_rows"][h // 2, :, (h % 2) * 4:(h % 2) * 4 + 4]).then_inc(w_in[h % 2], 16)
            for t in range(2, NT):
                sp.wait_ge(t_done, t - 1)
                sp.dma_start(x_t[:, t % 2], x_tiles[t]).then_inc(x_in[t % 2], 16)

        @block.gpsimd
        def _(pool):
            pool.memset(ident[:], 0.0).then_inc(consts_done, 1)
            pool.memset(utri[:], 1.0).then_inc(consts_done, 1)
            pool.memset(band[:], 0.0).then_inc(consts_done, 1)
            pool.memset(ones[:], 1.0).then_inc(consts_done, 1)
            pool.wait_ge(consts_done, 4)
            pool.affine_select(out=ident[:], in_=ident[:], compare_op=ALU.not_equal, fill=1.0, base=0,
                               pattern=[[-1, P]], channel_multiplier=1).then_inc(consts_done, 1)
            pool.affine_select(out=utri[:], in_=utri[:], compare_op=ALU.is_ge, fill=0.0, base=0,
                               pattern=[[1, P]], channel_multiplier=-1).then_inc(consts_done, 1)
            for b, (sign, base) in enumerate([(1, -1), (-1, 0), (1, -1)]):
                pool.affine_select(out=band[:, b], in_=band[:, b], compare_op=ALU.is_ge, fill=NEG, base=base,
                                   pattern=[[sign, P]], channel_multiplier=-sign).then_inc(consts_done, 1)
            for t in range(NT):
                for c in range(RC):
                    pool.wait_ge(rows_out, t * RC + c + 1)
                    pool.dma_start(rows_s[t, :, c * RW:(c + 1) * RW], o_t[:, c]).then_inc(stored[c], 16)
            for c in range(RC):
                pool.wait_ge(stored[c], 16 * NT)

        @block.scalar
        def _(act):
            own = Chain(act, act_own)

            def square(t):
                act.wait_ge(x_in[t % 2], 16 * (t // 2 + 1))
                if t:
                    act.wait_ge(sq_done, t)
                act.activation(sq[:], x_t[:, t % 2], ACT.Square, accum_out=stat[:, t, 0:1]).then_inc(sq_done, 1)

            def root(t):
                act.wait_ge(v_ready, t + 1)
                own.did(act.activation(stat[:, t, 2:3], stat[:, t, 1:2], ACT.Ln))
                own.wait()
                act.activation(stat[:, t, 3:4], stat[:, t, 2:3], ACT.Exp, scale=-0.5).then_inc(r0_ready, 1)

            def split_w(h):
                act.wait_ge(w_in[h % 2], 16 * (h // 2 + 1))
                c, k = h // 2, (h % 2) * 4
                act.activation(w_hi[:, c, k:k + 4], w_raw[:, h % 2], ACT.Copy).then_inc(w_hi_done, 1)

            def split_u(t):
                act.wait_ge(t_done, t + 1)
                act.activation(u_hi[:, :, t * P:(t + 1) * P], ps_t[:], ACT.Copy).then_inc(u_hi_done, 1)

            square(0)
            split_w(0)
            root(0)
            split_w(1)
            square(1)
            split_u(0)
            split_w(2)
            root(1)
            for h in range(3, 8):
                split_w(h)
            split_u(1)
            for t in range(2, NT):
                square(t)
                root(t)
                split_u(t)

        @block.vector
        def _(dve):
            own = Chain(dve, dve_own)

            def norm(t):
                dve.wait_ge(sq_done, t + 1)
                dve.tensor_scalar(stat[:, t, 1:2], stat[:, t, 0:1], 1.0 / D, EPS, ALU.mult, ALU.add).then_inc(v_ready, 1)
                dve.wait_ge(r0_ready, t + 1)
                newton(dve, own, stat[:, t, 3:4], stat[:, t, 1:2], stat[:, t, 4:5], stat[:, t, 5:6])
                if t == 0:
                    dve.wait_ge(row_in, 16)
                dve.scalar_tensor_tensor(x_t[:, t % 2], x_t[:, t % 2], stat[:, t, 5:6], w_row[:], ALU.mult,
                                         ALU.mult).then_inc(xn_ready, 1)

            def split_w(h):
                dve.wait_ge(w_hi_done, h + 1)
                c, k = h // 2, (h % 2) * 4
                dve.tensor_tensor(w_lo[:, c, k:k + 4], w_raw[:, h % 2], w_hi[:, c, k:k + 4].bitcast(F32),
                                  ALU.subtract).then_inc(w_lo_done, 1)

            def split_u(t):
                dve.wait_ge(u_hi_done, t + 1)
                dve.tensor_tensor(u_lo[:, :, t * P:(t + 1) * P], ps_t[:], u_hi[:, :, t * P:(t + 1) * P].bitcast(F32),
                                  ALU.subtract).then_inc(u_lo_done, 1)

            def rows(t):
                for c in range(RC):
                    dve.wait_ge(rows_done, t * RC + c + 1)
                    if t:
                        dve.wait_ge(stored[c], 16 * t)
                    dve.tensor_copy(o_t[:, c], ps_o[:, c, 0:RW]).then_inc(rows_out, 1)

            norm(0)
            split_w(0)
            split_u(0)
            split_w(1)
            split_w(2)
            norm(1)
            for h in range(3, 8):
                split_w(h)
            split_u(1)
            for t in range(NT):
                if t + 2 < NT:
                    norm(t + 2)
                rows(t)
                if t + 2 < NT:
                    split_u(t + 2)

        @block.tensor
        def _(pe):
            pe.wait_ge(consts_done, 5)

            def turn(t):
                pe.wait_ge(xn_ready, t + 1)
                if t:
                    pe.wait_ge(u_lo_done, t)
                for k in range(KT):
                    last = pe.transpose(ps_t[:, k], x_t[:, t % 2, k * P:(k + 1) * P], ident[:])
                last.then_inc(t_done, 1)

            turn(0)
            for t in range(NT):
                if t == 0:
                    turn(1)
                elif t + 1 < NT:
                    turn(t + 1)
                pe.wait_ge(u_lo_done, t + 1)
                for c in range(RC):
                    if t:
                        pe.wait_ge(rows_out, (t - 1) * RC + c + 1)
                    for k in range(KT):
                        if t == 0 and k % 4 == 0:
                            pe.wait_ge(w_lo_done, 2 * c + k // 4 + 1)
                        last = matmul3(pe, ps_o[:, c, 0:RW], u_hi[:, k, t * P:(t + 1) * P], u_lo[:, k, t * P:(t + 1) * P],
                                       w_hi[:, c, k], w_lo[:, c, k], k == 0, k == KT - 1)
                    last.then_inc(rows_done, 1)


def newton(dve, own, r0, v, tmp, r):
    own.did(dve.tensor_scalar(tmp, r0, r0, v, ALU.mult, ALU.mult))
    own.wait()
    own.did(dve.tensor_scalar(tmp, tmp, -0.5, 1.5, ALU.mult, ALU.add))
    own.wait()
    own.did(dve.tensor_tensor(r, r0, tmp, ALU.mult))
    own.wait()


def conv_features(nc, A, rows_s, acs_s, feat_s, tok_s, ident, utri, ones, u_hi, u_lo,
                  dt_v, acs, ea, decay, cdecay, cos_t, sin_t):
    TAPS = 4
    W = NT * NH
    with Stage(nc, "cf") as s:
        cw = s.sb("cw", [P, XT, TAPS + 1])
        w_raw = s.sb("w_raw", [P, 2, KT, P])
        w_hi = s.sb("w_hi", [P, 2, KT, P], F32R)
        w_lo = s.sb("w_lo", [P, 2, KT, P], F32R)
        xc = s.sb("xc", [P, 2, SEQ])
        xt = s.sb("xt", [P, 2, NT, P])
        ps = s.ps("ps", [P, 2, SEQ])
        ps_t = s.ps("ps_t", [P, NT, P])
        raw = s.sb("raw", [P, NT, NH])
        bias = s.sb("bias", [P, NH])
        alog = s.sb("alog", [P, NH])
        a_neg = s.sb("a_neg", [P, NH])
        freq = s.sb("freq", [P, HD // 2])
        pos = s.sb("pos", [P, NT], I32)
        posf = s.sb("posf", [P, NT])
        adt = s.sb("adt", [P, NT, NH])
        t1 = s.sb("t1", [P, NT, NH])
        t2 = s.sb("t2", [P, NT, NH])
        t3 = s.sb("t3", [P, NT, NH])
        mx = s.sb("mx", [P, NT, NH])
        ang = s.sb("ang", [P, NT, HD // 2])
        k_t = s.sb("k_t", [P, NT, HD // 2])
        m_t = s.sb("m_t", [P, NT, HD // 2])
        half_pi = s.sb("half_pi", [P, 1])
        tot = s.sb("tot", [P, NT, NH])
        acs_f = s.sb("acs_f", [P, 2, P])
        ps_ab = s.ps("ps_ab", [P, 2, W])
        ps_c = s.ps("ps_c", [P, 2, P])
        ins_in, raw_in = s.sem("ins_in"), s.sem("raw_in")
        u_need, u_ready, a_ready, adt_ready, sums_done = (s.sem(n) for n in "u_need u_ready a_ready adt_ready sums_done".split())
        table_own, exps_done, ang_ready, acs_ready, acs_turned, flat = (s.sem(n) for n in "table_own exps_done ang_ready acs_ready acs_turned flat".split())
        diff_ready, acs_stored = s.sem("diff_ready"), s.sem("acs_stored")
        cw_in = s.sem("cw_in")
        w_in, f_stored, t_stored = s.sems("w_in", 2), s.sems("f_stored", 2), s.sems("t_stored", 2)
        hi_done, lo_done, product_done, tap_done, dve_own, conv_done, silu_done, turned, t_out = (
            s.sem(n) for n in "hi_done lo_done product_done tap_done dve_own conv_done silu_done turned t_out".split())
        block = s.block()
        n_pairs = XT // 2
        feature_pairs = (INNER // P) // 2

        @block.sync
        def _(sp):
            for j in range(2):
                sp.dma_start(w_raw[:, j], A["w_xbc"][j]).then_inc(w_in[j], 16)
            sp.dma_start(raw[:], rows_s.rearrange("t p n -> p t n")[:, :, 0:NH]).then_inc(raw_in, 16)
            sp.dma_start(bias[:], A["dt_bias_row"].partition_broadcast(P)).then_inc(ins_in, 16)
            sp.dma_start(alog[:], A["a_log_row"].partition_broadcast(P)).then_inc(ins_in, 16)
            sp.dma_start(freq[:], A["freq_row"].partition_broadcast(P)).then_inc(ins_in, 16)
            sp.dma_start(pos[:], A["pos"]).then_inc(ins_in, 16)
            sp.dma_start(cw[:], A["ssd_conv"]).then_inc(cw_in, 16)
            with sp.Fori(0, n_pairs - 1) as i:
                for j in range(2):
                    sp.wait_ge(lo_done, 2 * i + j + 1)
                    sp.dma_start(w_raw[:, j], A["w_xbc"][2 * i + (j + 2)]).then_inc(w_in[j], 16)

        @block.gpsimd
        def _(pool):
            def store(i, j, features):
                f = 2 * i + j
                if features:
                    pool.wait_ge(silu_done, f + 1)
                    pool.dma_start(feat_s[f - INNER // P], xc[:, j]).then_inc(f_stored[j], 16)
                pool.wait_ge(t_out, f + 1)
                pool.dma_start(tok_s[:, :, bass.ds(f * P, P)].rearrange("t p n -> p t n"), xt[:, j]).then_inc(t_stored[j], 16)

            for i in range(2):
                for j in range(2):
                    store(i, j, False)
            pool.wait_ge(flat, 1)
            pool.dma_start(acs_s.rearrange("(a r) l -> r a l", r=P), acs_f[:]).then_inc(acs_stored, 16)
            with pool.Fori(2, feature_pairs) as i:
                for j in range(2):
                    store(i, j, False)
            with pool.Fori(feature_pairs, n_pairs) as i:
                for j in range(2):
                    store(i, j, True)
            pool.wait_ge(acs_stored, 16)
            for j in range(2):
                pool.wait_ge(t_stored[j], 16 * n_pairs)
                pool.wait_ge(f_stored[j], 16 * (n_pairs - feature_pairs))

        @block.scalar
        def _(act):
            def split(i, j):
                f = 2 * i + j
                act.wait_ge(w_in[j], 16 * (i + 1))
                act.activation(w_hi[:, j], w_raw[:, j], ACT.Copy).then_inc(hi_done, 1)

            def tile(i, j, first, features, last):
                f = 2 * i + j
                act.wait_ge(product_done, f + 1)
                if not first:
                    act.wait_ge(turned, f - 1)
                    if features:
                        act.wait_ge(f_stored[j], 16 * (i - feature_pairs))
                act.activation(xc[:, j], ps[:, j], ACT.Identity, scale=cw[:, bass.ds(f, 1), TAPS - 1],
                               bias=cw[:, bass.ds(f, 1), TAPS]).then_inc(tap_done, 1)
                if not last:
                    split(i + 1, j)
                act.wait_ge(conv_done, f + 1)
                act.activation(xc[:, j], xc[:, j], ACT.Silu).then_inc(silu_done, 1)

            def table_u():
                act.wait_ge(ins_in, 64)
                act.activation(a_neg[:], alog[:], ACT.Exp).then_inc(a_ready, 1)
                act.wait_ge(u_need, 1)
                act.activation(t3[:], t2[:], ACT.Exp).then_inc(u_ready, 1)

            def table_exps():
                act.wait_ge(diff_ready, 1)
                act.activation(decay[:], decay[:], ACT.Exp)
                act.activation(ea[:], acs[:], ACT.Exp)
                act.activation(cdecay[:], tot[:], ACT.Exp).then_inc(exps_done, 1)

            def table_sin():
                act.wait_ge(ang_ready, 1)
                act.activation(sin_t[:], ang[:], ACT.Sin)
                act.activation(cos_t[:], m_t[:], ACT.Sin, scale=-1.0, bias=half_pi[:]).then_inc(exps_done, 1)
                act.wait_ge(exps_done, 2)

            for j in range(2):
                split(0, j)
            table_u()
            act.wait_ge(cw_in, 16)
            for j in range(2):
                tile(0, j, True, False, False)
            tile(1, 0, False, False, False)
            table_exps()
            tile(1, 1, False, False, False)
            table_sin()
            with act.Fori(2, feature_pairs) as i:
                for j in range(2):
                    tile(i, j, False, False, False)
            for j in range(2):
                tile(feature_pairs, j, False, False, False)
            with act.Fori(feature_pairs + 1, n_pairs - 1) as i:
                for j in range(2):
                    tile(i, j, False, True, False)
            for j in range(2):
                tile(n_pairs - 1, j, False, True, True)

        @block.vector
        def _(dve):
            def split(i, j):
                f = 2 * i + j
                dve.wait_ge(hi_done, f + 1)
                dve.tensor_tensor(w_lo[:, j], w_raw[:, j], w_hi[:, j].bitcast(F32), ALU.subtract).then_inc(lo_done, 1)

            def conv(i, j, last):
                f = 2 * i + j
                dve.wait_ge(tap_done, f + 1)
                for n in range(1, TAPS):
                    if n > 1:
                        dve.wait_ge(dve_own, f * (TAPS - 2) + n - 1)
                    ins = dve.scalar_tensor_tensor(xc[:, j, n:SEQ], ps[:, j, 0:SEQ - n], cw[:, bass.ds(f, 1), TAPS - 1 - n],
                                                   xc[:, j, n:SEQ], ALU.mult, ALU.add)
                    ins.then_inc(dve_own if n < TAPS - 1 else conv_done, 1)
                if not last:
                    split(i + 1, j)

            def by_tokens(i, j, first):
                f = 2 * i + j
                dve.wait_ge(turned, f + 1)
                if not first:
                    dve.wait_ge(t_stored[j], 16 * i)
                dve.tensor_copy(xt[:, j], ps_t[:]).then_inc(t_out, 1)

            own = Chain(dve, table_own)

            def do(ins):
                own.did(ins)
                own.wait()

            def table_dt():
                dve.wait_ge(raw_in, 16)
                dve.wait_ge(ins_in, 64)
                do(dve.tensor_tensor(t1[:], raw[:], bias[:].unsqueeze(1).to_broadcast([P, NT, NH]), ALU.add))
                do(dve.tensor_scalar(mx[:], t1[:], 0.0, None, ALU.max))
                dve.scalar_tensor_tensor(t2[:], mx[:], -2.0, t1[:], ALU.mult, ALU.add).then_inc(u_need, 1)
                dve.wait_ge(u_ready, 1)
                do(dve.tensor_scalar(t1[:], t3[:], 2.0, None, ALU.add))
                do(dve.reciprocal(t1[:], t1[:]))
                do(dve.tensor_tensor(t3[:], t3[:], t1[:], ALU.mult))
                do(dve.tensor_tensor(t1[:], t3[:], t3[:], ALU.mult))
                do(dve.tensor_scalar(t2[:], t1[:], 1.0 / 19, 1.0 / 17, ALU.mult, ALU.add))
                for n in (15, 13, 11, 9, 7, 5, 3, 1):
                    do(dve.tensor_tensor(t2[:], t2[:], t1[:], ALU.mult))
                    do(dve.tensor_scalar(t2[:], t2[:], 1.0 / n, None, ALU.add))
                do(dve.tensor_tensor(t2[:], t2[:], t3[:], ALU.mult))
                do(dve.scalar_tensor_tensor(dt_v[:], t2[:], 2.0, mx[:], ALU.mult, ALU.add))
                dve.wait_ge(a_ready, 1)
                dve.scalar_tensor_tensor(adt[:], dt_v[:], -1.0, a_neg[:].unsqueeze(1).to_broadcast([P, NT, NH]),
                                         ALU.mult, ALU.mult).then_inc(adt_ready, 1)

            def table_angles():
                do(dve.memset(half_pi[:], 1.5707963267948966))
                do(dve.tensor_copy(posf[:], pos[:]))
                do(dve.tensor_tensor(ang[:], posf[:].unsqueeze(2).to_broadcast([P, NT, HD // 2]),
                                     freq[:].unsqueeze(1).to_broadcast([P, NT, HD // 2]), ALU.mult))

            def table_turns(scale):
                turn = sum(TURN)
                do(dve.tensor_scalar(k_t[:], ang[:], 1.0 / (turn * scale), MAGIC, ALU.mult, ALU.add))
                do(dve.tensor_scalar(k_t[:], k_t[:], MAGIC, None, ALU.subtract))
                for part in TURN:
                    do(dve.scalar_tensor_tensor(ang[:], k_t[:], -part * scale, ang[:], ALU.mult, ALU.add))

            def table_range():
                do(dve.tensor_scalar(ang[:], ang[:], 3.1415925, -3.1415925, ALU.min, ALU.max))
                do(dve.tensor_scalar(m_t[:], ang[:], -1.0, None, ALU.mult))
                dve.tensor_tensor(m_t[:], m_t[:], ang[:], ALU.max).then_inc(ang_ready, 1)

            def table_sums():
                dve.wait_ge(sums_done, 1)
                dve.tensor_copy(acs[:].rearrange("p t h -> p (t h)"), ps_ab[:, 0]).then_inc(acs_ready, 1)
                do(dve.tensor_copy(tot[:].rearrange("p t h -> p (t h)"), ps_ab[:, 1]))
                dve.tensor_tensor(decay[:], tot[:], acs[:], ALU.subtract).then_inc(diff_ready, 1)

            def table_by_heads():
                dve.wait_ge(acs_turned, 1)
                dve.tensor_copy(acs_f[:], ps_c[:]).then_inc(flat, 1)

            for j in range(2):
                split(0, j)
            table_dt()
            dve.wait_ge(cw_in, 16)
            conv(0, 0, False)
            table_angles()
            table_turns(FAR)
            conv(0, 1, False)
            table_sums()
            by_tokens(0, 0, True)
            conv(1, 0, False)
            table_turns(1.0)
            table_range()
            by_tokens(0, 1, True)
            conv(1, 1, False)
            table_by_heads()
            by_tokens(1, 0, False)
            with dve.Fori(2, n_pairs - 1) as i:
                conv(i, 0, False)
                by_tokens(i - 1, 1, False)
                conv(i, 1, False)
                by_tokens(i, 0, False)
            conv(n_pairs - 1, 0, True)
            by_tokens(n_pairs - 2, 1, False)
            conv(n_pairs - 1, 1, True)
            by_tokens(n_pairs - 1, 0, False)
            by_tokens(n_pairs - 1, 1, False)

        @block.tensor
        def _(pe):
            def half(i, j, h):
                for k in range(KT):
                    last = matmul3(pe, ps[:, j, h * HALF:(h + 1) * HALF], w_hi[:, j, k], w_lo[:, j, k],
                                   u_hi[:, k, h * HALF:(h + 1) * HALF], u_lo[:, k, h * HALF:(h + 1) * HALF], k == 0, k == KT - 1)
                return last

            def turn(f, j, first):
                pe.wait_ge(silu_done, f + 1)
                if not first:
                    pe.wait_ge(t_out, f)
                for t in range(NT):
                    last = pe.transpose(ps_t[:, t], xc[:, j, t * P:(t + 1) * P], ident[:])
                last.then_inc(turned, 1)

            def tile(i, j, first):
                f = 2 * i + j
                pe.wait_ge(lo_done, f + 1)
                if not first:
                    pe.wait_ge(conv_done, f - 1)
                half(i, j, 0)
                half(i, j, 1).then_inc(product_done, 1)
                if not (first and j == 0):
                    turn(f - 1, 1 - j, first and j == 1)

            def table_sums():
                pe.wait_ge(adt_ready, 1)
                flat_adt = adt[:].rearrange("p t h -> p (t h)")
                pe.matmul(ps_ab[:, 0], utri[:], flat_adt, start=True, stop=True)
                pe.matmul(ps_ab[:, 1], ones[:], flat_adt, start=True, stop=True).then_inc(sums_done, 1)

            def table_by_heads():
                pe.wait_ge(acs_ready, 1)
                flat_acs = acs[:].rearrange("p t h -> p (t h)")
                for i in range(2):
                    last = pe.transpose(ps_c[:, i], flat_acs[:, i * P:(i + 1) * P], ident[:])
                last.then_inc(acs_turned, 1)

            tile(0, 0, True)
            table_sums()
            tile(0, 1, True)
            tile(1, 0, False)
            table_by_heads()
            tile(1, 1, False)
            with pe.Fori(2, n_pairs) as i:
                for j in range(2):
                    tile(i, j, False)
            turn(XT - 1, 1, False)


def mixers(nc, A, rows_s, acs_s, feat_s, tok_s, gate_s, o_s, y_s, ident, utri, band, u_hi, u_lo,
           dt_v, acs, ea, decay, cdecay, cos_t, sin_t):
    R2 = HD // 2
    with Stage(nc, "mx") as s:
        z_raw = s.sb("z_raw", [P, 2, 2, GW])
        z_hi = s.sb("z_hi", [P, KT, GW], F32R)
        z_lo = s.sb("z_lo", [P, KT, GW], F32R)
        g_raw = s.sb("g_raw", [P, 2, KT, P])
        g_hi = s.sb("g_hi", [P, 2, KT, P], F32R)
        g_lo = s.sb("g_lo", [P, 2, KT, P], F32R)
        g_out = s.sb("g_out", [P, 2, HALF])
        x_in = s.sb("x_in", [P, 2, GW])
        b_tok = s.sb("b_tok", [P, 2, P])
        bc_f = s.sb("bc_f", [P, 2, 2, P])
        a_row = s.sb("a_row", [P, 2, HPG, P])
        dt_g, acs_g, decay_g = (s.sb(n, [P, NT, HPG]) for n in ("dt_g", "acs_g", "decay_g"))
        d_g = s.sb("d_g", [P, HPG])
        seg = s.sb("seg", [P, HPG, P])
        cbm = s.sb("cbm", [P, P])
        xdt = s.sb("xdt", [P, GW])
        xdec = s.sb("xdec", [P, GW])
        xd = s.sb("xd", [P, GW])
        state = s.sb("state", [P, GW])
        kept = s.sb("kept", [P, GW])
        y1 = s.sb("y1", [P, GW])
        silu = s.sb("silu", [P, GW])
        yn = s.sb("yn", [P, GW])
        y_t = s.sb("y_t", [P, 2, 4, P])
        stat = s.sb("stat", [P, 6])
        norm_row = s.sb("norm_row", [P, GW])
        d_row = s.sb("d_row", [P, NH])
        qk = s.sb("qk", [P, 2, REP + 2, HD])
        v_in = s.sb("v_in", [P, 4, HD])
        m1 = s.sb("m1", [P, REP + 2, R2])
        m2 = s.sb("m2", [P, REP + 2, R2])
        qr = s.sb("qr", [P, REP + 2, HD])
        q_t = s.sb("q_t", [P, 2, P])
        k_t = s.sb("k_t", [P, 2, P])
        sc = s.sb("sc", [P, REP, 2 * P])
        mx = s.sb("mx", [P, 2, REP])
        negm = s.sb("negm", [P, REP])
        sums = s.sb("sums", [P, REP])
        sink_e = s.sb("sink_e", [P, REP])
        rden = s.sb("rden", [P, REP])
        sinks = s.sb("sinks", [P, AH])
        p_t = s.sb("p_t", [P, REP, 2, P])
        o_tok = s.sb("o_tok", [P, REP * HD])
        o_t = s.sb("o_t", [P, 2, 2, P])
        ps_z = s.ps("ps_z", [P, HALF])
        ps_g = s.ps("ps_g", [P, HALF])
        ps_a = s.ps("ps_a", [P, HALF])
        ps_s = s.ps("ps_s", [P, 2, 2, 2 * P])
        ps_d = s.ps("ps_d", [P, HALF])
        ps_e = s.ps("ps_e", [P, HALF])
        ps_f = s.ps("ps_f", [P, HALF])

        rows_in, norm_in, step_in, z_in, g_in = s.sem("rows_in"), s.sem("norm_in"), s.sems("step_in", 2), s.sems("z_in", 2), s.sems("g_in", 2)
        z_hi_done, z_lo_done, g_hi_done, g_lo_done = (s.sem(n) for n in "z_hi_done z_lo_done g_hi_done g_lo_done".split())
        z_done, z_exp_done, z_used, gate_done, gate_out = (s.sem(n) for n in "z_done z_exp_done z_used gate_done gate_out".split())
        g_stored, y_stored, o_stored = s.sems("g_stored", 2), s.sems("y_stored", 2), s.sems("o_stored", 2)
        seg_ready, seg_min, decays_done, mix_ready, cb_done, cbm_ready = (
            s.sem(n) for n in "seg_ready seg_min decays_done mix_ready cb_done cbm_ready".split())
        xdt_ready, xdec_ready, xd_ready, off_done, state_done, state_ready, diag_done, y2_ready, y1_ready = (
            s.sem(n) for n in "xdt_ready xdec_ready xd_ready off_done state_done state_ready diag_done y2_ready y1_ready".split())
        gated, sq_done, v_ready, r0_ready, yn_ready, y_turned, y_out = (
            s.sem(n) for n in "gated sq_done v_ready r0_ready yn_ready y_turned y_out".split())
        rotated, qk_turned, q_ready, scored, masked, max_ready, exp_done, sink_done, p_turned, p_ready, pv_done, o_ready, o_turned, o_out = (
            s.sem(n) for n in "rotated qk_turned q_ready scored masked max_ready exp_done sink_done p_turned p_ready pv_done o_ready o_turned o_out".split())
        dve_own, pool_own, act_own = s.sem("dve_own"), s.sem("pool_own"), s.sem("act_own")
        block = s.block()
        LOADS = 8

        @block.sync
        def _(sp):
            def load_step(g, c):
                j = c % 2
                for dst, src in (
                    (qk[:, j, 0:REP].rearrange("p a d -> p (a d)"), rows_s[c, :, bass.ds(Q0 + g * (REP * HD), REP * HD)]),
                    (qk[:, j, REP], rows_s[c, :, bass.ds(K0 + g * HD, HD)]),
                    (qk[:, j, REP + 1], rows_s[c, :, bass.ds(K0 + g * HD, HD)]),
                    (v_in[:, c % 4], rows_s[c, :, bass.ds(V0 + g * HD, HD)]),
                    (a_row[:, j].rearrange("p h l -> p (h l)"),
                     acs_s[bass.ds(c * NH + g * HPG, HPG), :].rearrange("h l -> (h l)").partition_broadcast(P)),
                    (x_in[:, j], tok_s[c, :, bass.ds(g * GW, GW)]),
                    (b_tok[:, j], tok_s[c, :, bass.ds(INNER + g * P, P)]),
                    (bc_f[:, j], feat_s.rearrange("(b g) p n -> g p b n", b=2)[g, :, :, c * P:(c + 1) * P]),
                ):
                    sp.dma_start(dst, src).then_inc(step_in[j], 16)

            def load_z(g, q):
                if q >= 2:
                    sp.wait_ge(z_lo_done, KT * g + 2 * q - 2)
                sp.dma_start(z_raw[:, q % 2], A["w_z"][g, :, 2 * q:2 * q + 2]).then_inc(z_in[q % 2], 16)

            def group(g, first, last):
                if not first:
                    sp.wait_ge(yn_ready, NT * g)
                sp.dma_start(norm_row[:], A["ssd_norm_row"][bass.ds(g * GW, GW)].partition_broadcast(P)).then_inc(norm_in, 16)
                for c in range(NT):
                    if c % 2 == 0 and not (last and c >= 4):
                        u = 4 * g + c // 2
                        sp.wait_ge(g_lo_done, u + 1)
                        sp.dma_start(g_raw[:, (c // 2) % 2], A["w_gate"][u + 2]).then_inc(g_in[(c // 2) % 2], 16)
                    if c == 1 and not last:
                        sp.wait_ge(z_lo_done, KT * g + KT)
                        for q in range(2):
                            load_z(g + 1, q)
                    if c == NT - 1 and not last:
                        for q in range(2, 4):
                            load_z(g + 1, q)
                    if not (last and c >= NT - 2):
                        for sem in (diag_done, xd_ready, rotated, pv_done):
                            sp.wait_ge(sem, NT * g + c + 1)
                        if c < NT - 2:
                            load_step(g, c + 2)
                        else:
                            load_step(g + 1, c + 2 - NT)

            for q in range(2):
                load_z(0, q)
            load_step(0, 0)
            sp.dma_start(g_raw[:, 0], A["w_gate"][0]).then_inc(g_in[0], 16)
            for q in range(2, 4):
                load_z(0, q)
            for dst, src in ((d_row, "d_row"), (sinks, "sink_row")):
                sp.dma_start(dst[:], A[src].partition_broadcast(P)).then_inc(rows_in, 16)
            sp.dma_start(g_raw[:, 1], A["w_gate"][1]).then_inc(g_in[1], 16)
            load_step(0, 1)
            group(0, True, False)
            with sp.Fori(1, NG - 1) as g:
                group(g, False, False)
            group(NG - 1, False, True)

        @block.gpsimd
        def _(pool):
            def group(g, first):
                own = Chain(pool, pool_own, g * OWN)
                heads = bass.ds(g * HPG, HPG)

                def do(ins):
                    own.did(ins)
                    own.wait()

                def rotate(c):
                    pool.wait_ge(step_in[c % 2], 16 * LOADS * (4 * g + c // 2 + 1))
                    if not (first and c == 0):
                        pool.wait_ge(qk_turned, NT * g + c)
                    t1, t2 = qk[:, c % 2, :, 0:R2], qk[:, c % 2, :, R2:HD]
                    cs, sn = (t[:, c].unsqueeze(1).to_broadcast([P, REP + 2, R2]) for t in (cos_t, sin_t))
                    own.did(pool.tensor_tensor(m1[:], t1, cs, ALU.mult))
                    do(pool.tensor_tensor(m2[:], t2, sn, ALU.mult))
                    do(pool.tensor_tensor(qr[:, :, 0:R2], m1[:], m2[:], ALU.subtract))
                    own.did(pool.tensor_tensor(m1[:], t2, cs, ALU.mult))
                    do(pool.tensor_tensor(m2[:], t1, sn, ALU.mult))
                    pool.tensor_tensor(qr[:, :, R2:HD], m1[:], m2[:], ALU.add).then_inc(rotated, 1)

                rotate(0)
                if not first:
                    pool.wait_ge(mix_ready, NT * g)
                pool.wait_ge(rows_in, 32)
                for mine, whole in ((dt_g, dt_v), (acs_g, acs), (decay_g, decay)):
                    pool.tensor_copy(mine[:], whole[:, :, heads])
                do(pool.tensor_copy(d_g[:], d_row[:, heads]))
                for c in range(NT):
                    j, n = c % 2, NT * g + c
                    opening = first and c == 0
                    pool.wait_ge(step_in[j], 16 * LOADS * (4 * g + c // 2 + 1))
                    if not opening:
                        pool.wait_ge(diag_done, n)
                    pool.tensor_tensor(seg[:], a_row[:, j], bcast(acs_g[:, c], P), ALU.subtract).then_inc(seg_ready, 1)
                    x_h = x_in[:, j].rearrange("p (h d) -> p h d", d=HD)
                    pool.tensor_tensor(xdt[:].rearrange("p (h d) -> p h d", d=HD), x_h, bcast(dt_g[:, c], HD),
                                       ALU.mult).then_inc(xdt_ready, 1)
                    if c < NT - 1:
                        pool.wait_ge(xdt_ready, n + 1)
                        if not opening:
                            pool.wait_ge(state_done, (NT - 1) * g + c)
                        pool.tensor_tensor(xdec[:].rearrange("p (h d) -> p h d", d=HD),
                                           xdt[:].rearrange("p (h d) -> p h d", d=HD), bcast(decay_g[:, c], HD),
                                           ALU.mult).then_inc(xdec_ready, 1)
                    if not opening:
                        pool.wait_ge(gated, n)
                    pool.tensor_tensor(xd[:].rearrange("p (h d) -> p h d", d=HD), x_h, bcast(d_g[:], HD),
                                       ALU.mult).then_inc(xd_ready, 1)
                    pool.wait_ge(decays_done, n + 1)
                    pool.wait_ge(cbm_ready, n + 1)
                    pool.tensor_tensor(seg[:], seg[:], cbm[:].unsqueeze(1).to_broadcast([P, HPG, P]),
                                       ALU.mult).then_inc(mix_ready, 1)
                    if c + 1 < NT:
                        rotate(c + 1)
                assert own.n == OWN

            OWN = 1 + 5 * NT
            group(0, True)
            with pool.Fori(1, NG) as g:
                group(g, False)

        @block.scalar
        def _(act):
            def outputs(g, c, opening):
                n, j, before = NT * g + c, c % 2, 16 * (4 * g + c // 2)
                act.wait_ge(y_turned, n + 1)
                if not opening:
                    act.wait_ge(y_stored[j], before)
                act.activation(y_t[:, j], ps_e[:].rearrange("p (a n) -> p a n", a=4), ACT.Copy).then_inc(y_out, 1)
                act.wait_ge(o_turned, n + 1)
                if not opening:
                    act.wait_ge(o_stored[j], before)
                act.activation(o_t[:, j], ps_f[:, 0:2 * P].rearrange("p (a n) -> p a n", a=2), ACT.Copy).then_inc(o_out, 1)
                act.wait_ge(y_out, n + 1)
                act.dma_start(y_s[bass.ds(4 * g, 4), :, c * P:(c + 1) * P].rearrange("a p n -> p a n"),
                              y_t[:, j]).then_inc(y_stored[j], 16)
                act.wait_ge(o_out, n + 1)
                act.dma_start(o_s[bass.ds(2 * g, 2), :, c * P:(c + 1) * P].rearrange("a p n -> p a n"),
                              o_t[:, j]).then_inc(o_stored[j], 16)

            def split_z(g, k):
                q = k // 2
                act.wait_ge(z_in[q % 2], 16 * (2 * g + q // 2 + 1))
                act.activation(z_hi[:, k], z_raw[:, q % 2, k % 2], ACT.Copy).then_inc(z_hi_done, 1)

            def split_gate(w, use):
                act.wait_ge(g_in[w], 16 * (use + 1))
                act.activation(g_hi[:, w], g_raw[:, w], ACT.Copy).then_inc(g_hi_done, 1)

            def group(g, first, last):
                for c in range(NT):
                    j, n = c % 2, NT * g + c
                    opening = first and c == 0
                    act.wait_ge(z_done, n + 1)
                    if not opening:
                        act.wait_ge(sq_done, n)
                    act.activation(silu[:], ps_z[:], ACT.Exp, scale=-1.0).then_inc(z_exp_done, 1)
                    act.wait_ge(seg_min, n + 1)
                    act.activation(seg[:], seg[:], ACT.Exp).then_inc(decays_done, 1)
                    act.wait_ge(qk_turned, n + 1)
                    if not opening:
                        act.wait_ge(scored, n)
                    act.activation(q_t[:], ps_a[:, 0:2 * P].rearrange("p (a n) -> p a n", a=2), ACT.Copy)
                    act.activation(k_t[:, j], ps_a[:, 2 * P:3 * P], ACT.Copy).then_inc(q_ready, 1)
                    if c % 2 == 1 and not (last and c == NT - 1):
                        act.wait_ge(gate_done, n)
                        split_gate((c // 2 + 1) % 2, 2 * g + (c // 2 + 1) // 2)
                    if c == NT - 1 and not last:
                        for k in range(4):
                            split_z(g + 1, k)
                    if not opening:
                        outputs(g if c else g - 1, (c - 1) % NT, first and c <= 2)
                    act.wait_ge(max_ready, n + 1)
                    keys = P if c == 0 else 2 * P
                    for r in range(REP):
                        ins = act.activation(sc[:, r, 0:keys], sc[:, r, 0:keys], ACT.Exp, bias=negm[:, r:r + 1],
                                             accum_out=sums[:, r:r + 1])
                    ins.then_inc(exp_done, 1)
                    act.activation(sink_e[:], mx[:, 1], ACT.Exp).then_inc(sink_done, 1)
                    act.wait_ge(gate_done, n + 1)
                    if not (first and c < 2):
                        act.wait_ge(g_stored[j], 16 * (4 * g + c // 2))
                    act.activation(g_out[:, j], ps_g[:], ACT.Copy).then_inc(gate_out, 1)
                    act.wait_ge(gate_out, n + 1)
                    act.dma_start(gate_s[4 * g + c // 2, :, j * HALF:(j + 1) * HALF], g_out[:, j]).then_inc(g_stored[j], 16)
                    if c == NT - 1 and not last:
                        for k in range(4, KT):
                            split_z(g + 1, k)
                    act.wait_ge(gated, n + 1)
                    act.activation(silu[:], y1[:], ACT.Square, accum_out=stat[:, 0:1]).then_inc(sq_done, 1)
                    act.wait_ge(v_ready, n + 1)
                    act.activation(stat[:, 2:3], stat[:, 1:2], ACT.Ln).then_inc(act_own, 1)
                    act.wait_ge(act_own, n + 1)
                    act.activation(stat[:, 3:4], stat[:, 2:3], ACT.Exp, scale=-0.5).then_inc(r0_ready, 1)
                    act.wait_ge(p_turned, n + 1)
                    if not opening:
                        act.wait_ge(pv_done, n)
                    b = keys // P
                    act.activation(p_t[:, :, 0:b], ps_s[:].rearrange("p a b (k n) -> p (a b) k n", n=P)[:, :, 0:b],
                                   ACT.Copy).then_inc(p_ready, 1)

            act.preload_act_table_set("natural_log_exp_and_others")
            for k in range(KT):
                split_z(0, k)
            split_gate(0, 0)
            group(0, True, False)
            with act.Fori(1, NG - 1) as g:
                group(g, False, False)
            group(NG - 1, False, True)
            outputs(NG - 1, NT - 1, False)
            for sems in (g_stored, y_stored, o_stored):
                for j in range(2):
                    act.wait_ge(sems[j], 16 * NG * NT // 2)

        @block.vector
        def _(dve):
            def split_z(g, k):
                dve.wait_ge(z_hi_done, KT * g + k + 1)
                dve.tensor_tensor(z_lo[:, k], z_raw[:, (k // 2) % 2, k % 2], z_hi[:, k].bitcast(F32), ALU.subtract).then_inc(z_lo_done, 1)

            def split_gate(w, u):
                dve.wait_ge(g_hi_done, u + 1)
                dve.tensor_tensor(g_lo[:, w], g_raw[:, w], g_hi[:, w].bitcast(F32), ALU.subtract).then_inc(g_lo_done, 1)

            def attention_out(n, opening):
                dve.wait_ge(pv_done, n + 1)
                if not opening:
                    dve.wait_ge(o_turned, n)
                dve.tensor_tensor(o_tok[:].rearrange("p (a b d) -> p b a d", a=2, b=2),
                                  ps_a[:, 0:REP * HD].rearrange("p (b a d) -> p b a d", a=2, b=2),
                                  rden[:].rearrange("p (b a) -> p b a", a=2).unsqueeze(3).to_broadcast([P, 2, 2, HD]),
                                  ALU.mult).then_inc(o_ready, 1)

            def group(g, first, last):
                own = Chain(dve, dve_own, g * OWN)
                heads = bass.ds(g * HPG, HPG)

                def do(ins):
                    own.did(ins)
                    own.wait()

                for c in range(NT):
                    j, n = c % 2, NT * g + c
                    opening = first and c == 0
                    dve.wait_ge(seg_ready, n + 1)
                    dve.tensor_scalar(seg[:], seg[:], 0.0, None, ALU.min).then_inc(seg_min, 1)
                    if not opening:
                        attention_out(n - 1, first and c == 1)
                    dve.wait_ge(z_exp_done, n + 1)
                    do(dve.tensor_scalar(silu[:], silu[:], 1.0, None, ALU.add))
                    do(dve.reciprocal(silu[:], silu[:]))
                    dve.tensor_tensor(silu[:], ps_z[:], silu[:], ALU.mult).then_inc(z_used, 1)
                    dve.wait_ge(cb_done, n + 1)
                    if not opening:
                        dve.wait_ge(mix_ready, n)
                    dve.tensor_tensor(cbm[:], ps_d[:, 0:P], utri[:], ALU.mult).then_inc(cbm_ready, 1)
                    if c % 2 == 1 and not (last and c == NT - 1):
                        split_gate((c // 2 + 1) % 2, 4 * g + c // 2 + 1)
                    if c == NT - 1 and not last:
                        for k in range(4):
                            split_z(g + 1, k)
                    keys, start = (P, 1) if c == 0 else (2 * P, 0 if j else 1)
                    mask = band[:, start:start + keys // P].rearrange("p b k -> p (b k)").unsqueeze(1)
                    dve.wait_ge(scored, n + 1)
                    if not opening:
                        dve.wait_ge(p_turned, n)
                    for a in range(2):
                        ins = dve.scalar_tensor_tensor(sc[:, 2 * a:2 * a + 2, 0:keys], ps_s[:, a, :, 0:keys], HD ** -0.5,
                                                       mask.to_broadcast([P, 2, keys]), ALU.mult, ALU.add)
                    ins.then_inc(masked, 1)
                    dve.wait_ge(masked, n + 1)
                    do(dve.tensor_reduce(mx[:, 0], sc[:, :, 0:keys], AX, ALU.max))
                    if opening:
                        dve.wait_ge(rows_in, 32)
                    else:
                        dve.wait_ge(sink_done, n)
                    sink = sinks[:, bass.ds(g * REP, REP)]
                    do(dve.tensor_tensor(mx[:, 0], mx[:, 0], sink, ALU.max))
                    own.did(dve.tensor_scalar(negm[:], mx[:, 0], -1.0, None, ALU.mult))
                    dve.tensor_tensor(mx[:, 1], sink, mx[:, 0], ALU.subtract).then_inc(max_ready, 1)
                    heads_of = lambda t: t.rearrange("p (h d) -> p h d", d=HD)
                    if c:
                        dve.wait_ge(off_done, (NT - 1) * g + c)
                        own.did(dve.tensor_tensor(heads_of(y1[:]), heads_of(ps_e[:]), bcast(ea[:, c, heads], HD), ALU.mult))
                    if c == 0:
                        dve.wait_ge(state_done, (NT - 1) * g + 1)
                        dve.tensor_copy(state[:], ps_f[:]).then_inc(state_ready, 1)
                    elif c < NT - 1:
                        do(dve.tensor_tensor(heads_of(kept[:]), heads_of(state[:]), bcast(cdecay[:, c, heads], HD), ALU.mult))
                        dve.wait_ge(state_done, (NT - 1) * g + c + 1)
                        dve.tensor_tensor(state[:], kept[:], ps_f[:], ALU.add).then_inc(state_ready, 1)
                    dve.wait_ge(diag_done, n + 1)
                    dve.wait_ge(xd_ready, n + 1)
                    dve.tensor_tensor(xd[:], ps_d[:], xd[:], ALU.add).then_inc(y2_ready, 1)
                    dve.wait_ge(y2_ready, n + 1)
                    dve.wait_ge(z_used, n + 1)
                    if c:
                        do(dve.tensor_tensor(xd[:], xd[:], y1[:], ALU.add))
                    dve.tensor_tensor(y1[:], xd[:], silu[:], ALU.mult).then_inc(gated, 1)
                    if c == NT - 1 and not last:
                        for k in range(4, KT):
                            split_z(g + 1, k)
                    dve.wait_ge(sink_done, n + 1)
                    do(dve.tensor_tensor(rden[:], sums[:], sink_e[:], ALU.add))
                    do(dve.reciprocal(rden[:], rden[:]))
                    dve.wait_ge(sq_done, n + 1)
                    dve.tensor_scalar(stat[:, 1:2], stat[:, 0:1], 1.0 / GW, EPS, ALU.mult, ALU.add).then_inc(v_ready, 1)
                    dve.wait_ge(r0_ready, n + 1)
                    newton(dve, own, stat[:, 3:4], stat[:, 1:2], stat[:, 4:5], stat[:, 5:6])
                    if not opening:
                        dve.wait_ge(y_turned, n)
                    if c == 0:
                        dve.wait_ge(norm_in, 16 * (g + 1))
                    dve.scalar_tensor_tensor(yn[:], y1[:], stat[:, 5:6], norm_row[:], ALU.mult,
                                             ALU.mult).then_inc(yn_ready, 1)
                assert own.n == OWN

            OWN = 10 * NT + 2 * (NT - 1) + (NT - 2)
            for k in range(KT):
                split_z(0, k)
            split_gate(0, 0)
            group(0, True, False)
            with dve.Fori(1, NG - 1) as g:
                group(g, False, False)
            group(NG - 1, False, True)
            attention_out(NG * NT - 1, False)

        @block.tensor
        def _(pe):
            def gate(g, c, ks, opening):
                j, w = c % 2, (c // 2) % 2
                if ks[0] == 0:
                    pe.wait_ge(g_lo_done, 4 * g + c // 2 + 1)
                    if not opening:
                        pe.wait_ge(gate_out, NT * g + c)
                for k in ks:
                    last = matmul3(pe, ps_g[:], g_hi[:, w, k], g_lo[:, w, k], u_hi[:, k, j * HALF:(j + 1) * HALF],
                                   u_lo[:, k, j * HALF:(j + 1) * HALF], k == 0, k == KT - 1)
                if ks[-1] == KT - 1:
                    last.then_inc(gate_done, 1)

            def z(g, c, ks, opening):
                if ks[0] == 0 and not opening:
                    pe.wait_ge(z_used, NT * g + c)
                for k in ks:
                    if c == 0:
                        pe.wait_ge(z_lo_done, KT * g + k + 1)
                    last = matmul3(pe, ps_z[:], u_hi[:, k, c * P:(c + 1) * P], u_lo[:, k, c * P:(c + 1) * P],
                                   z_hi[:, k], z_lo[:, k], k == 0, k == KT - 1)
                if ks[-1] == KT - 1:
                    last.then_inc(z_done, 1)

            def next_z(g, c, last, ks):
                if c < NT - 1:
                    z(g, c + 1, ks, False)
                elif not last:
                    z(g + 1, 0, ks, False)

            def values(g, c):
                pe.wait_ge(p_ready, NT * g + c + 1)
                j, blocks = c % 2, 1 if c == 0 else 2
                for r in range(REP):
                    for b in range(blocks):
                        block_of = c if b == j else c - 1
                        last = pe.matmul(ps_a[:, r * HD:(r + 1) * HD], p_t[:, r, b], v_in[:, block_of % 4],
                                         start=(b == 0), stop=(b == blocks - 1))
                last.then_inc(pv_done, 1)

            def turn_outputs(g, c, opening):
                n = NT * g + c
                pe.wait_ge(yn_ready, n + 1)
                if not opening:
                    pe.wait_ge(y_out, n)
                for a in range(4):
                    last = pe.transpose(ps_e[:, a * P:(a + 1) * P], yn[:, a * P:(a + 1) * P], ident[:])
                last.then_inc(y_turned, 1)
                pe.wait_ge(o_ready, n + 1)
                if c < NT - 1:
                    pe.wait_ge(state_ready, (NT - 1) * g + c + 1)
                else:
                    pe.wait_ge(o_out, n)
                for a in range(2):
                    last = pe.transpose(ps_f[:, a * P:(a + 1) * P], o_tok[:, a * P:(a + 1) * P], ident[:])
                last.then_inc(o_turned, 1)

            def group(g, first, last_group):
                for c in range(NT):
                    j, n = c % 2, NT * g + c
                    opening = first and c == 0
                    before = (g if c else g - 1, (c - 1) % NT)
                    if not opening:
                        values(*before)
                    gate(g, c, range(0, 4), opening)
                    pe.wait_ge(step_in[j], 16 * LOADS * (4 * g + c // 2 + 1))
                    pe.wait_ge(rotated, n + 1)
                    if not opening:
                        pe.wait_ge(o_ready, n)
                    for a in range(3):
                        two = qr[:, 2 * a:2 * a + 2].rearrange("p a d -> p (a d)")
                        last = pe.transpose(ps_a[:, a * P:(a + 1) * P], two, ident[:])
                    last.then_inc(qk_turned, 1)
                    if not opening:
                        pe.wait_ge(y2_ready, n)
                    pe.matmul(ps_d[:, 0:P], bc_f[:, j, 0], bc_f[:, j, 1], start=True, stop=True).then_inc(cb_done, 1)
                    gate(g, c, range(4, 6), opening)
                    pe.wait_ge(q_ready, n + 1)
                    if not opening:
                        pe.wait_ge(p_ready, n)
                    keys = P if c == 0 else 2 * P
                    for r in range(REP):
                        lo = (r % 2) * HD
                        last = pe.matmul(ps_s[:, r % 2, r // 2, 0:keys], q_t[lo:lo + HD, r // 2],
                                         k_t[lo:lo + HD].rearrange("p b n -> p (b n)")[:, 0:keys], start=True, stop=True)
                    last.then_inc(scored, 1)
                    if not opening:
                        turn_outputs(*before, first and c == 1)
                    gate(g, c, range(6, KT), opening)
                    if c:
                        pe.wait_ge(state_ready, (NT - 1) * g + c)
                        pe.wait_ge(y_out, n)
                        pe.matmul(ps_e[:], bc_f[:, j, 1], state[:], start=True, stop=True).then_inc(off_done, 1)
                    if c < NT - 1:
                        pe.wait_ge(xdec_ready, (NT - 1) * g + c + 1)
                        if not opening:
                            pe.wait_ge(o_out, n)
                        pe.matmul(ps_f[:], b_tok[:, j], xdec[:], start=True, stop=True).then_inc(state_done, 1)
                    pe.wait_ge(mix_ready, n + 1)
                    pe.wait_ge(xdt_ready, n + 1)
                    for h in range(HPG):
                        last = pe.matmul(ps_d[:, h * HD:(h + 1) * HD], seg[:, h], xdt[:, h * HD:(h + 1) * HD], start=True, stop=True)
                    last.then_inc(diag_done, 1)
                    next_z(g, c, last_group, range(0, 3))
                    pe.wait_ge(exp_done, n + 1)
                    for r in range(REP):
                        for b in range(keys // P):
                            last = pe.transpose(ps_s[:, r // 2, r % 2, b * P:(b + 1) * P], sc[:, r, b * P:(b + 1) * P], ident[:])
                    last.then_inc(p_turned, 1)
                    next_z(g, c, last_group, range(3, KT))

            z(0, 0, range(KT), True)
            group(0, True, False)
            with pe.Fori(1, NG - 1) as g:
                group(g, False, False)
            group(NG - 1, False, True)
            values(NG - 1, NT - 1)
            turn_outputs(NG - 1, NT - 1, False)


def merge(nc, A, gate_s, o_s, y_s, merged):
    RING = 3
    with Stage(nc, "mg") as s:
        w_raw = s.sb("w_raw", [P, 2, KT, P])
        w_hi = s.sb("w_hi", [P, 2, KT, P], F32R)
        w_lo = s.sb("w_lo", [P, 2, KT, P], F32R)
        src = s.sb("src", [P, RING, SEQ])
        o_hi = s.sb("o_hi", [P, KT, SEQ], F32R)
        o_lo = s.sb("o_lo", [P, KT, SEQ], F32R)
        y_hi = s.sb("y_hi", [P, KT, SEQ], F32R)
        y_lo = s.sb("y_lo", [P, KT, SEQ], F32R)
        sig = s.sb("sig", [P, 2, SEQ])
        ps = s.ps("ps", [P, 2, SEQ])
        w_in, s_in, sig_in = s.sems("w_in", 2), s.sems("s_in", RING), s.sems("sig_in", 2)
        w_hi_done, w_lo_done, s_hi_done, s_lo_done, sig_done, scaled, out_done, block_used = (
            s.sem(n) for n in "w_hi_done w_lo_done s_hi_done s_lo_done sig_done scaled out_done block_used".split())
        block = s.block()
        PAIRS = KT // 2
        EARLY_USES = [len(range(a, KT, RING)) for a in range(RING)]
        LATE_USES = [EARLY_USES[a] + (PAIRS if a < 2 else 0) for a in range(RING)]

        def ssd_blocks(i):
            return ((0, 0), (1, 0), (0, 1), (1, 1)) if i is START else ((0, 0), (0, 1), (1, 0), (1, 1))

        START = "first pair"

        def number(i):
            return 0 if i is START else i

        @block.sync
        def _(sp):
            def load_sig(T_next, place, gate_tile):
                sp.wait_ge(out_done, T_next - 1)
                sp.dma_start(sig[:, place], gate_s[gate_tile]).then_inc(sig_in[place], 16)

            def load_ssd(i, q, p):
                j, b = ssd_blocks(i)[p]
                sp.wait_ge(w_lo_done, q - 1)
                sp.dma_start(w_raw[:, p % 2], A["w_ssd_out"][4 * number(i) + (2 * j + b)]).then_inc(w_in[p % 2], 16)

            def attn_pair(i):
                for j in range(2):
                    f = 2 * i + j
                    sp.wait_ge(w_lo_done, f + 1)
                    sp.dma_start(w_raw[:, j], A["w_attn_out"][f + 2]).then_inc(w_in[j], 16)
                    load_sig(f + 2, j, f + (2 + KT))

            for j in range(2):
                sp.dma_start(w_raw[:, j], A["w_attn_out"][j]).then_inc(w_in[j], 16)
            for j in range(2):
                sp.dma_start(sig[:, j], gate_s[KT + j]).then_inc(sig_in[j], 16)
            with sp.Fori(0, PAIRS - 1) as i:
                attn_pair(i)
            for j in range(2):
                load_ssd(START, KT + j, j)
                load_sig(KT + j, j, j)
            for p in range(2, 4):
                load_ssd(START, KT + p, p)
            for p in range(2):
                load_ssd(1, KT + 4 + p, p)
                load_sig(KT + 2 + p, p, 2 + p)

            def ssd_pair(i):
                for p in range(4):
                    nxt = (i, p + 2) if p < 2 else (i + 1, p - 2)
                    load_ssd(nxt[0], KT + 4 * i + p + 2, nxt[1])
                    if p % 2:
                        j = p // 2
                        load_sig(KT + 2 * i + j + 2, j, 2 * i + j + 2)

            with sp.Fori(1, PAIRS - 1) as i:
                ssd_pair(i)
            for p in range(2, 4):
                load_ssd(PAIRS - 1, KT + 4 * (PAIRS - 1) + p, p)

        @block.gpsimd
        def _(pool):
            for n in range(KT):
                if n >= RING:
                    pool.wait_ge(s_lo_done, n - RING + 1)
                pool.dma_start(src[:, n % RING], o_s[n]).then_inc(s_in[n % RING], 16)
            with pool.Fori(0, PAIRS) as i:
                for a in range(2):
                    pool.wait_ge(s_lo_done, 2 * i + (KT + a - 1))
                    pool.dma_start(src[:, a], y_s[2 * i + a]).then_inc(s_in[a], 16)
            for m in range(KT):
                n = 2 * KT + m
                pool.wait_ge(s_lo_done, n - 1 if m < RING else n - RING + 1)
                pool.dma_start(src[:, m % RING], y_s[KT + m]).then_inc(s_in[m % RING], 16)

        @block.scalar
        def _(act):
            def split_w(use, slot):
                act.wait_ge(w_in[slot], 16 * (use + 1))
                act.activation(w_hi[:, slot], w_raw[:, slot], ACT.Copy).then_inc(w_hi_done, 1)

            def split_s(dst, k, slot, use):
                act.wait_ge(s_in[slot], 16 * (use + 1))
                act.activation(dst[:, bass.ds(k, 1)].rearrange("p a n -> p (a n)"), src[:, slot], ACT.Copy).then_inc(s_hi_done, 1)

            def sigmoid(pair_no, j):
                act.wait_ge(sig_in[j], 16 * (pair_no + 1))
                act.activation(sig[:, j], sig[:, j], ACT.Sigmoid).then_inc(sig_done, 1)

            def attn_pair(i):
                for j in range(2):
                    sigmoid(i, j)
                    split_s(y_hi, 2 * i + j, j, EARLY_USES[j] + i)
                    act.wait_ge(block_used, 2 * i + j + 1)
                    split_w(i + 1, j)

            def ssd_pair(i, last):
                for p in range(4):
                    if p in (0, 2):
                        sigmoid(PAIRS + number(i), p // 2)
                    if i is START and p < 2:
                        for m in range(4 * p, 4 * p + 4):
                            split_s(o_hi, m, m % RING, LATE_USES[m % RING] + m // RING)
                    if not (last and p >= 2):
                        act.wait_ge(block_used, KT + 4 * number(i) + p + 1)
                        split_w(PAIRS + 2 * number(i) + (p + 2) // 2, p % 2)

            split_w(0, 0)
            for n in range(KT):
                split_s(o_hi, n, n % RING, n // RING)
                if n == 0:
                    split_w(0, 1)
            with act.Fori(0, PAIRS) as i:
                attn_pair(i)
            ssd_pair(START, False)
            with act.Fori(1, PAIRS - 1) as i:
                ssd_pair(i, False)
            ssd_pair(PAIRS - 1, True)

        @block.vector
        def _(dve):
            def split_w(q, slot):
                dve.wait_ge(w_hi_done, q + 1)
                dve.tensor_tensor(w_lo[:, slot], w_raw[:, slot], w_hi[:, slot].bitcast(F32), ALU.subtract).then_inc(w_lo_done, 1)

            def split_s(n, hi, lo, k, slot):
                at = lambda t: t[:, bass.ds(k, 1)].rearrange("p a n -> p (a n)")
                dve.wait_ge(s_hi_done, n + 1)
                dve.tensor_tensor(at(lo), src[:, slot], at(hi).bitcast(F32), ALU.subtract).then_inc(s_lo_done, 1)

            def tile_of(f):
                return merged[:, bass.ds(f, 1)].rearrange("p a n -> p (a n)")

            def attn_pair(i):
                for j in range(2):
                    f = 2 * i + j
                    split_s(KT + f, y_hi, y_lo, f, j)
                    dve.wait_ge(sig_done, f + 1)
                    dve.wait_ge(block_used, f + 1)
                    dve.tensor_tensor(tile_of(f), sig[:, j], ps[:, j], ALU.mult).then_inc(out_done, 1)
                    split_w(f + 2, j)

            def ssd_pair(i, last):
                for p in range(4):
                    q = KT + 4 * number(i) + p
                    if i is START and p < 2:
                        for m in range(4 * p, 4 * p + 4):
                            split_s(2 * KT + m, o_hi, o_lo, m, m % RING)
                    j, b = ssd_blocks(i)[p]
                    if b:
                        f = 2 * number(i) + j
                        dve.wait_ge(sig_done, KT + f + 1)
                        dve.wait_ge(block_used, q + 1)
                        dve.tensor_tensor(sig[:, j], sig[:, j], ps[:, j], ALU.mult).then_inc(scaled, 1)
                        dve.wait_ge(scaled, f + 1)
                        dve.tensor_tensor(tile_of(f), tile_of(f), sig[:, j], ALU.add).then_inc(out_done, 1)
                    if not (last and p >= 2):
                        split_w(q + 2, p % 2)

            split_w(0, 0)
            for n in range(KT):
                split_s(n, o_hi, o_lo, n, n % RING)
                if n == 0:
                    split_w(1, 1)
            with dve.Fori(0, PAIRS) as i:
                attn_pair(i)
            ssd_pair(START, False)
            with dve.Fori(1, PAIRS - 1) as i:
                ssd_pair(i, False)
            ssd_pair(PAIRS - 1, True)

        @block.tensor
        def _(pe):
            def part(j, slot, k, hi, lo, h, first, last):
                return matmul3(pe, ps[:, j, h * HALF:(h + 1) * HALF], w_hi[:, slot, k], w_lo[:, slot, k],
                               hi[:, k, h * HALF:(h + 1) * HALF], lo[:, k, h * HALF:(h + 1) * HALF], first, last)

            for k in range(KT):
                for j in range(2):
                    if k == 0:
                        pe.wait_ge(w_lo_done, j + 1)
                    if j == 0:
                        pe.wait_ge(s_lo_done, k + 1)
                    for h in range(2):
                        last = part(j, j, k, o_hi, o_lo, h, k == 0, k == KT - 1)
                    if k == KT - 1:
                        last.then_inc(block_used, 1)
            with pe.Fori(1, PAIRS) as i:
                for j in range(2):
                    f = 2 * i + j
                    pe.wait_ge(w_lo_done, f + 1)
                    pe.wait_ge(out_done, f - 1)
                    for h in range(2):
                        for k in range(KT):
                            last = part(j, j, k, o_hi, o_lo, h, k == 0, k == KT - 1)
                    last.then_inc(block_used, 1)

            def ssd_pair(i):
                for p, (j, b) in enumerate(ssd_blocks(i)):
                    q = KT + 4 * number(i) + p
                    hi, lo = (o_hi, o_lo) if b else (y_hi, y_lo)
                    if not b:
                        pe.wait_ge(out_done, KT + 2 * number(i) + j - 1)
                    pe.wait_ge(w_lo_done, q + 1)
                    if i is START and p == 0:
                        pe.wait_ge(s_lo_done, 2 * KT)
                    for k in range(KT):
                        if i is START and p == 2:
                            pe.wait_ge(s_lo_done, 2 * KT + k + 1)
                        for h in range(2):
                            last = part(j, p % 2, k, hi, lo, h, b == 0 and k == 0, b == 1 and k == KT - 1)
                    last.then_inc(block_used, 1)

            ssd_pair(START)
            with pe.Fori(1, PAIRS) as i:
                ssd_pair(i)


def mix_rows(nc, A, merged, x2_s, h_hi, h_lo, ident):
    with Stage(nc, "mr") as s:
        w_raw = s.sb("w_raw", [P, 3, D])
        w_hi = s.sb("w_hi", [P, KT, D], F32R)
        w_lo = s.sb("w_lo", [P, KT, D], F32R)
        post = s.sb("post", [P, D])
        pre = s.sb("pre", [P, D])
        x_t = s.sb("x_t", [P, 2, D])
        y_t = s.sb("y_t", [P, 3, D])
        stat = s.sb("stat", [P, 2, NT, 6])
        ps = s.ps("ps", [P, 3, D])
        ps_t = s.ps("ps_t", [P, KT, P])
        rows_in, w_in, x_in, stored = s.sem("rows_in"), s.sems("w_in", 3), s.sems("x_in", 2), s.sems("stored", 2)
        s_hi_done, s_lo_done, w_hi_done, w_lo_done, product_done, sq_done, v_ready, r0_ready, y_ready, x2_ready, h_ready, turned, h_hi_done, h_lo_done, act_own, dve_own = (
            s.sem(n) for n in ("s_hi_done s_lo_done w_hi_done w_lo_done product_done sq_done v_ready r0_ready y_ready "
                               "x2_ready h_ready turned h_hi_done h_lo_done act_own dve_own").split())
        block = s.block()
        x_tiles = A["x"].rearrange("(t p) d -> t p d", p=P)

        @block.sync
        def _(sp):
            for k in range(KT):
                if k >= 3:
                    sp.wait_ge(w_lo_done, k - 2)
                sp.dma_start(w_raw[:, k % 3], A["w_mix"][:, k]).then_inc(w_in[k % 3], 16)
            sp.dma_start(post[:], A["mix_post_row"].partition_broadcast(P)).then_inc(rows_in, 16)
            sp.dma_start(pre[:], A["ffn_pre_row"].partition_broadcast(P)).then_inc(rows_in, 16)
            for t in range(NT):
                if t >= 2:
                    sp.wait_ge(stored[t % 2], 16 * (t // 2))
                    sp.wait_ge(h_ready, t - 1)
                sp.dma_start(x_t[:, t % 2], x_tiles[t]).then_inc(x_in[t % 2], 16)

        @block.gpsimd
        def _(pool):
            for t in range(NT):
                pool.wait_ge(x2_ready, t + 1)
                pool.dma_start(x2_s[t], x_t[:, t % 2]).then_inc(stored[t % 2], 16)
            for j in range(2):
                pool.wait_ge(stored[j], 16 * NT // 2)

        @block.scalar
        def _(act):
            def rstd(t, n, src_ap, junk):
                act.activation(junk, src_ap, ACT.Square, accum_out=stat[:, n, t, 0:1]).then_inc(sq_done, 1)
                act.wait_ge(v_ready, 2 * t + n + 1)
                act.activation(stat[:, n, t, 2:3], stat[:, n, t, 1:2], ACT.Ln).then_inc(act_own, 1)
                act.wait_ge(act_own, 2 * t + n + 1)
                act.activation(stat[:, n, t, 3:4], stat[:, n, t, 2:3], ACT.Exp, scale=-0.5).then_inc(r0_ready, 1)

            act.preload_act_table_set("natural_log_exp_and_others")
            for k in range(KT):
                act.activation(h_hi[:, k], merged[:, k], ACT.Copy).then_inc(s_hi_done, 1)
                act.wait_ge(w_in[k % 3], 16 * (k // 3 + 1))
                act.activation(w_hi[:, k], w_raw[:, k % 3], ACT.Copy).then_inc(w_hi_done, 1)
            def split_h(t):
                act.wait_ge(turned, t + 1)
                act.activation(h_hi[:, :, t * P:(t + 1) * P], ps_t[:], ACT.Copy).then_inc(h_hi_done, 1)

            for t in range(NT):
                act.wait_ge(product_done, t + 1)
                if t >= 3:
                    act.wait_ge(turned, t - 2)
                rstd(t, 0, ps[:, t % 3], y_t[:, t % 3])
                act.wait_ge(x2_ready, t + 1)
                rstd(t, 1, x_t[:, t % 2], y_t[:, t % 3])
                if t >= 2:
                    split_h(t - 2)
            for t in (NT - 2, NT - 1):
                split_h(t)

        @block.vector
        def _(dve):
            own = Chain(dve, dve_own)

            def rstd(t, n):
                dve.wait_ge(sq_done, 2 * t + n + 1)
                dve.tensor_scalar(stat[:, n, t, 1:2], stat[:, n, t, 0:1], 1.0 / D, EPS, ALU.mult, ALU.add).then_inc(v_ready, 1)
                dve.wait_ge(r0_ready, 2 * t + n + 1)
                newton(dve, own, stat[:, n, t, 3:4], stat[:, n, t, 1:2], stat[:, n, t, 4:5], stat[:, n, t, 5:6])

            for k in range(KT):
                dve.wait_ge(s_hi_done, k + 1)
                dve.tensor_tensor(h_lo[:, k], merged[:, k], h_hi[:, k].bitcast(F32), ALU.subtract).then_inc(s_lo_done, 1)
                dve.wait_ge(w_hi_done, k + 1)
                dve.tensor_tensor(w_lo[:, k], w_raw[:, k % 3], w_hi[:, k].bitcast(F32), ALU.subtract).then_inc(w_lo_done, 1)
            dve.wait_ge(rows_in, 32)
            def split_h(t):
                dve.wait_ge(h_hi_done, t + 1)
                dve.tensor_tensor(h_lo[:, :, t * P:(t + 1) * P], ps_t[:], h_hi[:, :, t * P:(t + 1) * P].bitcast(F32),
                                  ALU.subtract).then_inc(h_lo_done, 1)

            for t in range(NT):
                j, y = t % 2, y_t[:, t % 3]
                rstd(t, 0)
                dve.scalar_tensor_tensor(y, ps[:, t % 3], stat[:, 0, t, 5:6], post[:], ALU.mult, ALU.mult).then_inc(y_ready, 1)
                dve.wait_ge(y_ready, t + 1)
                dve.wait_ge(x_in[j], 16 * (t // 2 + 1))
                dve.tensor_tensor(x_t[:, j], x_t[:, j], y, ALU.add).then_inc(x2_ready, 1)
                rstd(t, 1)
                dve.scalar_tensor_tensor(y, x_t[:, j], stat[:, 1, t, 5:6], pre[:], ALU.mult, ALU.mult).then_inc(h_ready, 1)
                if t >= 2:
                    split_h(t - 2)
            for t in (NT - 2, NT - 1):
                split_h(t)

        @block.tensor
        def _(pe):
            def turn(t):
                pe.wait_ge(h_ready, t + 1)
                if t:
                    pe.wait_ge(h_lo_done, t)
                for k in range(KT):
                    last = pe.transpose(ps_t[:, k], y_t[:, t % 3, k * P:(k + 1) * P], ident[:])
                last.then_inc(turned, 1)

            def product(t, k):
                for h in range(2):
                    last = matmul3(pe, ps[:, t % 3, h * HALF:(h + 1) * HALF], h_hi[:, k, t * P:(t + 1) * P],
                                   h_lo[:, k, t * P:(t + 1) * P], w_hi[:, k, h * HALF:(h + 1) * HALF],
                                   w_lo[:, k, h * HALF:(h + 1) * HALF], k == 0, k == KT - 1)
                if k == KT - 1:
                    last.then_inc(product_done, 1)

            for k in range(KT):
                pe.wait_ge(s_lo_done, k + 1)
                pe.wait_ge(w_lo_done, k + 1)
                for t in range(2):
                    product(t, k)
            for t in range(2, NT):
                if t >= 3:
                    pe.wait_ge(y_ready, t - 2)
                for k in range(KT):
                    product(t, k)
                turn(t - 2)
            turn(NT - 2)
            turn(NT - 1)


def ffn_up(nc, A, ff, h_hi, h_lo):
    TAPS = 3
    with Stage(nc, "fu") as s:
        cw = s.sb("cw", [P, FT, 2, TAPS + 1])
        w_raw = s.sb("w_raw", [P, 2, KT, P])
        w_hi = s.sb("w_hi", [P, 2, KT, P], F32R)
        w_lo = s.sb("w_lo", [P, 2, KT, P], F32R)
        xc = s.sb("xc", [P, 2, SEQ])
        ps = s.ps("ps", [P, 2, SEQ])
        cw_in, w_in = s.sem("cw_in"), s.sems("w_in", 2)
        hi_done, lo_done, product_done, tap_done, dve_own, conv_done, gelu_done, ff_done = (
            s.sem(n) for n in "hi_done lo_done product_done tap_done dve_own conv_done gelu_done ff_done".split())
        block = s.block()

        @block.sync
        def _(sp):
            sp.dma_start(cw[:], A["ffn_conv"]).then_inc(cw_in, 16)
            for j in range(2):
                sp.dma_start(w_raw[:, j], A["w_up"][j]).then_inc(w_in[j], 16)
            with sp.Fori(0, FT - 1) as i:
                for j in range(2):
                    sp.wait_ge(lo_done, 2 * i + j + 1)
                    sp.dma_start(w_raw[:, j], A["w_up"][2 * i + (j + 2)]).then_inc(w_in[j], 16)

        @block.scalar
        def _(act):
            def split(i, j):
                act.wait_ge(w_in[j], 16 * (i + 1))
                act.activation(w_hi[:, j], w_raw[:, j], ACT.Copy).then_inc(hi_done, 1)

            def pair(i, first, last):
                for j in range(2):
                    act.wait_ge(product_done, 2 * i + j + 1)
                    if j == 0 and not first:
                        act.wait_ge(ff_done, i)
                    act.activation(xc[:, j], ps[:, j], ACT.Identity, scale=cw[:, bass.ds(i, 1), j, TAPS - 1],
                                   bias=cw[:, bass.ds(i, 1), j, TAPS]).then_inc(tap_done, 1)
                    if not last:
                        split(i + 1, j)
                    if j == 0:
                        act.wait_ge(conv_done, 2 * i + 1)
                        act.activation(xc[:, 0], xc[:, 0], ACT.Gelu_apprx_tanh).then_inc(gelu_done, 1)

            for j in range(2):
                split(0, j)
            act.wait_ge(cw_in, 16)
            pair(0, True, False)
            with act.Fori(1, FT - 1) as i:
                pair(i, False, False)
            pair(FT - 1, False, True)

        @block.vector
        def _(dve):
            def split(i, j):
                dve.wait_ge(hi_done, 2 * i + j + 1)
                dve.tensor_tensor(w_lo[:, j], w_raw[:, j], w_hi[:, j].bitcast(F32), ALU.subtract).then_inc(lo_done, 1)

            def pair(i, last):
                for j in range(2):
                    f = 2 * i + j
                    dve.wait_ge(tap_done, f + 1)
                    dve.scalar_tensor_tensor(xc[:, j, 1:SEQ], ps[:, j, 0:SEQ - 1], cw[:, bass.ds(i, 1), j, 1],
                                             xc[:, j, 1:SEQ], ALU.mult, ALU.add).then_inc(dve_own, 1)
                    dve.wait_ge(dve_own, f + 1)
                    dve.scalar_tensor_tensor(xc[:, j, 2:SEQ], ps[:, j, 0:SEQ - 2], cw[:, bass.ds(i, 1), j, 0],
                                             xc[:, j, 2:SEQ], ALU.mult, ALU.add).then_inc(conv_done, 1)
                    if not last:
                        split(i + 1, j)
                dve.wait_ge(gelu_done, i + 1)
                dve.wait_ge(conv_done, 2 * i + 2)
                dve.tensor_tensor(ff[:, bass.ds(i, 1)].rearrange("p a n -> p (a n)"), xc[:, 0], xc[:, 1],
                                  ALU.mult).then_inc(ff_done, 1)

            for j in range(2):
                split(0, j)
            dve.wait_ge(cw_in, 16)
            with dve.Fori(0, FT - 1) as i:
                pair(i, False)
            pair(FT - 1, True)

        @block.tensor
        def _(pe):
            def pair(i, first):
                for j in range(2):
                    f = 2 * i + j
                    pe.wait_ge(lo_done, f + 1)
                    if not first:
                        pe.wait_ge(conv_done, f - 1)
                    for h in range(2):
                        for k in range(KT):
                            last = matmul3(pe, ps[:, j, h * HALF:(h + 1) * HALF], w_hi[:, j, k], w_lo[:, j, k],
                                           h_hi[:, k, h * HALF:(h + 1) * HALF], h_lo[:, k, h * HALF:(h + 1) * HALF],
                                           k == 0, k == KT - 1)
                    last.then_inc(product_done, 1)

            pair(0, True)
            with pe.Fori(1, FT) as i:
                pair(i, False)


def ffn_down(nc, A, ff, x2_s, out, ident):
    BLK = ((0, 6), (6, 6), (12, 5), (17, 5))
    NBK = len(BLK)
    WK = max(n for _, n in BLK)
    PB = 2 * NBK
    PAIRS = KT // 2
    TH = NT // 2
    with Stage(nc, "fd") as s:
        w_raw = s.sb("w_raw", [P, 2, WK, P])
        w_hi = s.sb("w_hi", [P, 2, WK, P], F32R)
        w_lo = s.sb("w_lo", [P, 2, WK, P], F32R)
        s_hi = s.sb("s_hi", [P, FT, HALF], F32R)
        s_lo = s.sb("s_lo", [P, FT, HALF], F32R)
        d_f = s.sb("d_f", [P, 2, HALF])
        post = s.sb("post", [P, D])
        ssq = s.sb("ssq", [P, 2, TH, KT])
        v, r0, tmp, r = (s.sb(n, [P, 2, TH]) for n in ("v", "r0", "tmp", "r"))
        ps = s.ps("ps", [P, 2, HALF])
        ps_t = s.ps("ps_t", [P, 2, TH, P])
        junk = s.ps("junk", [P, HALF])
        row_in, w_in, x2_in, late_in = s.sem("row_in"), s.sems("w_in", 2), s.sem("x2_in"), s.sem("late_in")
        stored, late_stored = s.sem("stored"), s.sem("late_stored")
        w_hi_done, w_lo_done, block_used, s_hi_done, s_lo_done, f_out, turned, t_out = (
            s.sem(n) for n in "w_hi_done w_lo_done block_used s_hi_done s_lo_done f_out turned t_out".split())
        sq_done, v_ready, ln_done, r0_ready, out_ready, dve_own = (
            s.sem(n) for n in "sq_done v_ready ln_done r0_ready out_ready dve_own".split())
        block = s.block()
        out_tiles = out.rearrange("(t p) d -> t p d", p=P)

        def ahead(j, b):
            p = j * NBK + b + 2
            return p // NBK - j, p % NBK

        def ff_of(h, k):
            return ff[:, k, h * HALF:(h + 1) * HALF]

        def product(h, t):
            return ff[:, h * KT:(h + 1) * KT, t * P:(t + 1) * P].rearrange("p (a b) c -> p a b c", a=2)

        def residual(h, t):
            if h:
                return product(0, t)
            k = 2 * KT + 2 * t if t < 3 else KT
            return ff[:, k:k + 2, 0:HALF].rearrange("p a (b c) -> p a b c", b=4)

        def row_tile(ap):
            return ap.rearrange("p (a b c) -> p a b c", a=2, b=4)

        @block.sync
        def _(sp):
            def load_w(f, b, slot):
                k0, n = BLK[b]
                sp.dma_start(w_raw[:, slot, 0:n], A["w_down"][f, :, k0:k0 + n]).then_inc(w_in[slot], 16)

            def pair(h, i, last):
                for j in range(2):
                    for b in range(NBK):
                        p = j * NBK + b
                        more, nb = ahead(j, b)
                        if last and j + more == 2:
                            if h == 0:
                                sp.wait_ge(w_lo_done, PB * (h * PAIRS + i) + p + 1)
                                load_w(0, nb, p % 2)
                        else:
                            sp.wait_ge(w_lo_done, PB * (h * PAIRS + i) + p + 1)
                            load_w(2 * i + (j + more), nb, p % 2)

            for b in range(2):
                load_w(0, b, b)
            sp.dma_start(post[:], A["ffn_post_row"].partition_broadcast(P)).then_inc(row_in, 16)
            for h in range(2):
                with sp.Fori(0, PAIRS - 1) as i:
                    pair(h, i, False)
                pair(h, PAIRS - 1, True)
            for t in range(TH):
                sp.wait_ge(out_ready, TH + t + 1)
                sp.dma_start(row_tile(out_tiles[TH + t]), product(1, t)).then_inc(late_stored, 16)
            sp.wait_ge(late_stored, 16 * TH)

        @block.gpsimd
        def _(pool):
            pool.wait_ge(s_lo_done, FT)
            for t in range(TH):
                pool.dma_start(residual(0, t), row_tile(x2_s[t])).then_inc(x2_in, 16)
            for t in range(TH):
                pool.wait_ge(out_ready, t + 1)
                pool.dma_start(row_tile(out_tiles[t]), product(0, t)).then_inc(stored, 16)
            pool.wait_ge(stored, 16 * TH)
            for t in range(TH):
                pool.dma_start(residual(1, t), row_tile(x2_s[TH + t])).then_inc(late_in, 16)

        @block.scalar
        def _(act):
            def split_w(use, slot, b):
                n = BLK[b][1]
                act.wait_ge(w_in[slot], 16 * (use + 1))
                act.activation(w_hi[:, slot, 0:n], w_raw[:, slot, 0:n], ACT.Copy).then_inc(w_hi_done, 1)

            def split_s(h, k):
                act.activation(s_hi[:, k], ff_of(h, k), ACT.Copy).then_inc(s_hi_done, 1)

            def squares(h, f, j):
                act.wait_ge(t_out, h * KT + f + 1)
                for t in range(TH):
                    ins = act.activation(junk[:, t * P:(t + 1) * P], ps_t[:, j, t], ACT.Square,
                                         accum_out=ssq[:, h, t, bass.ds(f, 1)])
                ins.then_inc(sq_done, 1)

            def pair(h, i, first, last):
                for j in range(2):
                    f = h * KT + 2 * i + j
                    for b in range(NBK):
                        p = j * NBK + b
                        if not (h == 1 and last and p >= PB - 2):
                            act.wait_ge(block_used, PB * (h * PAIRS + i) + p + 1)
                            split_w(NBK * (h * PAIRS + i) + (p + 2) // 2, p % 2, ahead(j, b)[1])
                        if h == 0 and last and j == 1:
                            for k in range(BLK[b][0], BLK[b][0] + BLK[b][1]):
                                split_s(1, k)
                        if b == 1 and not (first and j == 0):
                            squares(h, 2 * i + j - 1, 1 - j)
                        if b == 1 and h == 1 and first and j == 0:
                            squares(0, KT - 1, 1)
                            root(0)
                    act.wait_ge(block_used, PB * (h * PAIRS + i) + (j + 1) * NBK)
                    if not (h == 0 and first and j == 0):
                        act.wait_ge(turned, f)
                    act.activation(d_f[:, j], ps[:, j], ACT.Copy).then_inc(f_out, 1)

            def root(h):
                act.wait_ge(v_ready, h + 1)
                act.activation(tmp[:, h], v[:, h], ACT.Ln).then_inc(ln_done, 1)
                act.wait_ge(ln_done, h + 1)
                act.activation(r0[:, h], tmp[:, h], ACT.Exp, scale=-0.5).then_inc(r0_ready, 1)

            act.preload_act_table_set("natural_log_exp_and_others")
            for k in range(FT):
                if k in (3, 6):
                    split_w(0, k // 3 - 1, k // 3 - 1)
                split_s(0, k)
            pair(0, 0, True, False)
            with act.Fori(1, PAIRS - 1) as i:
                pair(0, i, False, False)
            pair(0, PAIRS - 1, False, True)
            pair(1, 0, True, False)
            with act.Fori(1, PAIRS - 1) as i:
                pair(1, i, False, False)
            pair(1, PAIRS - 1, False, True)
            squares(1, KT - 1, 1)
            root(1)

        @block.vector
        def _(dve):
            own = Chain(dve, dve_own)

            def do(ins):
                own.did(ins)
                own.wait()

            def split_w(q, slot, b):
                n = BLK[b][1]
                dve.wait_ge(w_hi_done, q + 1)
                dve.tensor_tensor(w_lo[:, slot, 0:n], w_raw[:, slot, 0:n], w_hi[:, slot, 0:n].bitcast(F32),
                                  ALU.subtract).then_inc(w_lo_done, 1)

            def split_s(h, k):
                dve.wait_ge(s_hi_done, h * FT + k + 1)
                dve.tensor_tensor(s_lo[:, k], ff_of(h, k), s_hi[:, k].bitcast(F32),
                                  ALU.subtract).then_inc(s_lo_done, 1)

            def to_tokens(h, f, j):
                dve.wait_ge(turned, h * KT + f + 1)
                if h:
                    dve.wait_ge(out_ready, TH)
                place = ff[:, bass.ds(h * KT + f, 1), 0:HALF].rearrange("p a (t c) -> p (a t) c", c=P)
                dve.tensor_tensor(place, ps_t[:, j], post[:, bass.ds(f * P, P)].unsqueeze(1).to_broadcast([P, TH, P]),
                                  ALU.mult).then_inc(t_out, 1)

            def pair(h, i, first, last):
                for j in range(2):
                    for b in range(NBK):
                        p = j * NBK + b
                        if not (h == 1 and last and p >= PB - 2):
                            split_w(PB * (h * PAIRS + i) + p + 2, p % 2, ahead(j, b)[1])
                        if h == 0 and last and j == 1:
                            for k in range(BLK[b][0], BLK[b][0] + BLK[b][1]):
                                split_s(1, k)
                        if b == 1 and not (first and j == 0):
                            to_tokens(h, 2 * i + j - 1, 1 - j)
                        if b == 1 and h == 1 and first and j == 0:
                            to_tokens(0, KT - 1, 1)
                            rstd(0)
                        if b >= 2 and h == 1 and first and j == 0:
                            dve.wait_ge(x2_in, 16 * TH)
                            for t in range(2 * b - 4, 2 * b - 2):
                                output(0, t)

            def rstd(h):
                dve.wait_ge(sq_done, KT * (h + 1))
                do(dve.tensor_reduce(v[:, h], ssq[:, h], AX, ALU.add))
                dve.tensor_scalar(v[:, h], v[:, h], 1.0 / D, EPS, ALU.mult, ALU.add).then_inc(v_ready, 1)
                dve.wait_ge(r0_ready, h + 1)
                do(dve.tensor_tensor(tmp[:, h], r0[:, h], r0[:, h], ALU.mult))
                do(dve.tensor_tensor(tmp[:, h], tmp[:, h], v[:, h], ALU.mult))
                do(dve.tensor_scalar(tmp[:, h], tmp[:, h], -0.5, 1.5, ALU.mult, ALU.add))
                do(dve.tensor_tensor(r[:, h], r0[:, h], tmp[:, h], ALU.mult))

            def output(h, t):
                dve.scalar_tensor_tensor(product(h, t), product(h, t), r[:, h, t:t + 1], residual(h, t), ALU.mult,
                                         ALU.add).then_inc(out_ready, 1)

            for k in range(FT):
                if k in (3, 6):
                    split_w(k // 3 - 1, k // 3 - 1, k // 3 - 1)
                split_s(0, k)
            dve.wait_ge(row_in, 16)
            pair(0, 0, True, False)
            with dve.Fori(1, PAIRS - 1) as i:
                pair(0, i, False, False)
            pair(0, PAIRS - 1, False, True)
            pair(1, 0, True, False)
            with dve.Fori(1, PAIRS - 1) as i:
                pair(1, i, False, False)
            pair(1, PAIRS - 1, False, True)
            to_tokens(1, KT - 1, 1)
            rstd(1)
            dve.wait_ge(late_in, 16 * TH)
            for t in range(TH):
                dve.wait_ge(t_out, 2 * KT)
                output(1, t)

        @block.tensor
        def _(pe):
            def turn(f, j):
                pe.wait_ge(f_out, f + 1)
                for t in range(TH):
                    last = pe.transpose(ps_t[:, j, t], d_f[:, j, t * P:(t + 1) * P], ident[:])
                last.then_inc(turned, 1)

            def pair(h, i, first):
                for j in range(2):
                    f = h * KT + 2 * i + j
                    if not (first and h == 0):
                        pe.wait_ge(f_out, f - 1)
                        pe.wait_ge(t_out, f - 1)
                        pe.wait_ge(sq_done, f - 1)
                    for b, (k0, n) in enumerate(BLK):
                        p = j * NBK + b
                        pe.wait_ge(w_lo_done, PB * (h * PAIRS + i) + p + 1)
                        for k in range(k0, k0 + n):
                            if first and j == 0:
                                pe.wait_ge(s_lo_done, h * FT + k + 1)
                            last = matmul3(pe, ps[:, j], w_hi[:, p % 2, k - k0], w_lo[:, p % 2, k - k0], s_hi[:, k],
                                           s_lo[:, k], k == 0, k == FT - 1)
                        last.then_inc(block_used, 1)
                        if b == 0 and not (h == 0 and first and j == 0):
                            turn(f - 1, 1 - j)

            for h in range(2):
                pair(h, 0, True)
                with pe.Fori(1, PAIRS) as i:
                    pair(h, i, False)
            turn(2 * KT - 1, 1)


def lay_out(x, positions, norm_mix_pre_w, w_in, ssd_conv_w, ssd_conv_b, ssd_dt_bias, ssd_a_log, ssd_d,
            ssd_norm_w, ssd_w_out, attn_sinks, attn_w_out, w_mix_out, norm_mix_post_w,
            norm_ffn_pre_w, ffn_w_up, ffn_conv_w, ffn_conv_b, ffn_w_down, norm_ffn_post_w):
    import numpy as np

    def tiles(w, width):
        k, n = w.shape
        return np.ascontiguousarray(w.reshape(k // P, P, n // width, width).transpose(2, 1, 0, 3))

    def columns(*rows):
        return np.ascontiguousarray(np.stack([r.reshape(-1, P).T for r in rows], axis=2))

    w = w_in[0]
    xbc_0, rows_0, gate_0 = INNER, INNER + CONV_DIM, INNER + CONV_DIM + ROWS
    w_ssd = ssd_w_out[0]
    w_up = ffn_w_up[0].reshape(D, 2, FT, P).transpose(0, 2, 1, 3).reshape(D, 2 * FF)
    conv = [r.reshape(2, FT, P) for r in (*ffn_conv_w[0], ffn_conv_b[0])]
    head_order = [(h % 2) * 2 + h // 2 for h in range(REP)]
    freq = (10000.0 ** (-np.arange(HD // 2, dtype=np.float32) * 2.0 / HD)).astype(np.float32)
    return {
        "x": x[0],
        "pos": np.ascontiguousarray(positions[0].reshape(NT, P).T),
        "mix_pre_row": norm_mix_pre_w[0],
        "w_rows": tiles(w[:, rows_0:gate_0], RW),
        "w_xbc": tiles(w[:, xbc_0:rows_0], P),
        "w_z": tiles(w[:, 0:INNER], GW),
        "w_gate": tiles(w[:, gate_0:], P),
        "ssd_conv": columns(*ssd_conv_w[0], ssd_conv_b[0]),
        "dt_bias_row": ssd_dt_bias[0],
        "a_log_row": ssd_a_log[0],
        "d_row": ssd_d[0],
        "freq_row": freq,
        "ssd_norm_row": ssd_norm_w[0],
        "w_ssd_out": np.ascontiguousarray(w_ssd.reshape(2, KT, P, KT, P).transpose(3, 0, 2, 1, 4)).reshape(2 * KT, P, KT, P),
        "sink_row": np.ascontiguousarray(attn_sinks[0].reshape(NG, REP)[:, head_order]).reshape(-1),
        "w_attn_out": tiles(attn_w_out[0], P),
        "w_mix": np.ascontiguousarray(w_mix_out[0].reshape(KT, P, D).transpose(1, 0, 2)),
        "mix_post_row": norm_mix_post_w[0],
        "ffn_pre_row": norm_ffn_pre_w[0],
        "w_up": tiles(w_up, P),
        "ffn_conv": np.ascontiguousarray(np.stack(conv, axis=3).transpose(2, 1, 0, 3)),
        "w_down": tiles(ffn_w_down[0], P),
        "ffn_post_row": norm_ffn_post_w[0],
    }


def kernel(**inputs):
    import numpy as np
    import concourse.bacc as bacc
    from concourse.bass_utils import run_bass_kernel_spmd

    arrays = lay_out(**{k: np.asarray(v) for k, v in inputs.items()})
    arrays = {f"in_{k}": np.ascontiguousarray(v) for k, v in arrays.items()}
    nc = bacc.Bacc("TRN2", target_bir_lowering=False, num_devices=1)
    aps = {k[3:]: nc.dram_tensor(k, v.shape, mybir.dt.from_np(v.dtype), kind="ExternalInput").ap()
           for k, v in arrays.items()}
    out = nc.dram_tensor("out", (SEQ, D), F32, kind="ExternalOutput").ap()
    hybrid_block_kernel(nc, aps, out)
    got = run_bass_kernel_spmd(nc, [arrays], core_ids=[0])
    return got.results[0]["out"].reshape(1, SEQ, D)
```
